# Optimizing a Trainium2 kernel written in Bass

```python
import jax, jax.numpy as jnp
from jax import lax
import numpy as np

D_MODEL = 1024
BATCH = 1
SEQ = 512
DEPTH = 1

MLA_HEADS = 4
QK_NOPE = 128
QK_ROPE = 64
V_HEAD = 128
Q_LORA = 256
KV_LORA = 256
QK_HEAD = QK_NOPE + QK_ROPE
MLA_WIDTH = MLA_HEADS * V_HEAD
HG_HEADS = 4
HG_DK = 128
HG_DV = 128
HG_FDIM = HG_HEADS * HG_DK
HG_WIDTH = HG_HEADS * HG_DV
CHUNK = 64
D_MIX = MLA_WIDTH + HG_WIDTH
D_FF = -(-8 * D_MODEL // (3 * 256)) * 256
PLE_DIM = 256
ROPE_THETA = 10000.0
EPS = 1e-6
Q_BLOCK = 128
IN_SIZES = (Q_LORA, KV_LORA, QK_ROPE, HG_FDIM, HG_FDIM, HG_FDIM, HG_WIDTH, HG_WIDTH)
D_IN = sum(IN_SIZES)
IN_SPLITS = tuple(int(v) for v in np.cumsum(IN_SIZES)[:-1])


def rms_norm(x, g):
    xf = x.astype(jnp.float32)
    y = xf * lax.rsqrt(jnp.mean(xf * xf, axis=-1, keepdims=True) + EPS)
    return (y * g.astype(jnp.float32)).astype(x.dtype)

def rope(x, cos, sin):
    x1, x2 = jnp.split(x.astype(jnp.float32), 2, axis=-1)
    return jnp.concatenate([x1 * cos - x2 * sin, x1 * sin + x2 * cos], axis=-1).astype(x.dtype)

def blocked_attention(q, k, v):
    B, S, H, D = q.shape
    nb = S // Q_BLOCK
    qb = q.reshape(B, nb, Q_BLOCK, H, D).transpose(1, 0, 2, 3, 4)
    scale = QK_HEAD ** -0.5

    def one_block(q_blk):
        s = jnp.einsum('bqhd,bkhd->bhqk', q_blk, k, preferred_element_type=jnp.float32) * scale
        w = jax.nn.softmax(s, axis=-1).astype(v.dtype)
        return jnp.einsum('bhqk,bkhd->bqhd', w, v)

    o = lax.map(one_block, qb)
    return o.transpose(1, 0, 2, 3, 4).reshape(B, S, H * v.shape[-1])

def mla(c_q, c_kv, k_r, cos, sin, g_qa, g_kva, w_qb, w_kvb, g_qn, g_kn):
    B, S, _ = c_q.shape
    q = (rms_norm(c_q, g_qa) @ w_qb).reshape(B, S, MLA_HEADS, QK_HEAD)
    kv = (rms_norm(c_kv, g_kva) @ w_kvb).reshape(B, S, MLA_HEADS, QK_NOPE + V_HEAD)
    k_nope, v = kv[..., :QK_NOPE], kv[..., QK_NOPE:]
    k = jnp.concatenate([k_nope, jnp.broadcast_to(k_r[:, :, None, :], (B, S, MLA_HEADS, QK_ROPE))], axis=-1)
    q = rms_norm(q, g_qn)
    k = rms_norm(k, g_kn)
    c, s = cos[:, :, None, :], sin[:, :, None, :]
    q = jnp.concatenate([q[..., :QK_NOPE], rope(q[..., QK_NOPE:], c, s)], axis=-1)
    k = jnp.concatenate([k[..., :QK_NOPE], rope(k[..., QK_NOPE:], c, s)], axis=-1)
    return blocked_attention(q, k, v)

def gla_chunkwise(q, k, v, logf):
    B, H, S, DK = q.shape
    DV = v.shape[-1]
    N = S // CHUNK
    q = q.reshape(B, H, N, CHUNK, DK)
    k = k.reshape(B, H, N, CHUNK, DK)
    v = v.reshape(B, H, N, CHUNK, DV)
    b = jnp.cumsum(logf.reshape(B, H, N, CHUNK, DK), axis=3)
    b_last = b[:, :, :, -1:, :]
    b_mid = b[:, :, :, CHUNK // 2 - 1:CHUNK // 2, :]
    q_intra = q * jnp.exp(b - b_mid)
    k_intra = k * jnp.exp(b_mid - b)
    mask = jnp.tril(jnp.ones((CHUNK, CHUNK), jnp.float32))
    A = jnp.einsum('bhntd,bhnsd->bhnts', q_intra, k_intra) * mask
    o_intra = jnp.einsum('bhnts,bhnsv->bhntv', A, v)
    kv = jnp.einsum('bhnsd,bhnsv->bhndv', k * jnp.exp(b_last - b), v)
    decay = jnp.exp(b_last[:, :, :, 0, :])

    def step(state, inp):
        dec, kv_n = inp
        return dec[..., None] * state + kv_n, state

    _, s_before = lax.scan(step, jnp.zeros((B, H, DK, DV), jnp.float32),
                           (jnp.moveaxis(decay, 2, 0), jnp.moveaxis(kv, 2, 0)))
    s_before = jnp.moveaxis(s_before, 0, 2)
    o_inter = jnp.einsum('bhntd,bhndv->bhntv', q * jnp.exp(b), s_before)
    return (o_intra + o_inter).reshape(B, H, S, DV)

def hgrn2(hq, hf_fwd, hf_bwd, hi, hg, lb, g_out):
    B, S, _ = hq.shape

    def heads(t):
        return t.reshape(B, S, HG_HEADS, -1).transpose(0, 2, 1, 3)

    q = heads(jax.nn.silu(hq.astype(jnp.float32)))
    v = heads(hi.astype(jnp.float32))

    def gates(f_pre, lower):
        f = lower + (1.0 - lower) * jax.nn.sigmoid(f_pre.astype(jnp.float32))
        return heads(1.0 - f), heads(jnp.log(f))

    k_f, lf_f = gates(hf_fwd, lb[0])
    k_b, lf_b = gates(hf_bwd, lb[1])
    o_f = gla_chunkwise(q, k_f, v, lf_f)
    o_b = gla_chunkwise(q[:, :, ::-1], k_b[:, :, ::-1], v[:, :, ::-1], lf_b[:, :, ::-1])[:, :, ::-1]
    o = (o_f + o_b).transpose(0, 2, 1, 3)
    o = rms_norm(o, g_out).reshape(B, S, HG_WIDTH)
    return (o * jax.nn.silu(hg.astype(jnp.float32))).astype(hq.dtype)

def first_inputs(seed: int = 0) -> dict:
    key = jax.random.key(seed)
    ks = jax.random.split(key, 32)
    f32 = jnp.float32

    def w(k, shape, fan_in):
        return jax.random.normal(k, shape, f32) * (fan_in ** -0.5)

    def gain(k, shape):
        return 1.0 + 0.05 * jax.random.normal(k, shape, f32)

    x = jax.random.normal(ks[0], (BATCH, SEQ, D_MODEL), f32)
    p = jax.random.normal(ks[1], (DEPTH, BATCH, SEQ, PLE_DIM), f32)
    offsets = jax.random.randint(ks[2], (BATCH, 1), 0, 1024, jnp.int32)
    positions = offsets + jnp.arange(SEQ, dtype=jnp.int32)[None, :]
    return {
        "x": x,
        "p": p,
        "positions": positions,
        "g_mix": gain(ks[3], (DEPTH, D_MODEL)),
        "w_in": w(ks[4], (DEPTH, D_MODEL, D_IN), D_MODEL),
        "g_qa": gain(ks[5], (DEPTH, Q_LORA)),
        "g_kva": gain(ks[6], (DEPTH, KV_LORA)),
        "w_qb": w(ks[7], (DEPTH, Q_LORA, MLA_HEADS * QK_HEAD), Q_LORA),
        "w_kvb": w(ks[8], (DEPTH, KV_LORA, MLA_HEADS * (QK_NOPE + V_HEAD)), KV_LORA),
        "g_qn": gain(ks[9], (DEPTH, QK_HEAD)),
        "g_kn": gain(ks[10], (DEPTH, QK_HEAD)),
        "lb_param": 0.1 * jax.random.normal(ks[11], (DEPTH + 1, 2, HG_FDIM), f32),
        "g_hgo": gain(ks[12], (DEPTH, HG_HEADS, HG_DV)),
        "w_o": w(ks[13], (DEPTH, D_MIX, D_MODEL), D_MIX),
        "g_ffn": gain(ks[14], (DEPTH, D_MODEL)),
        "w_gate": w(ks[15], (DEPTH, D_MODEL, D_FF), D_MODEL),
        "w_up": w(ks[16], (DEPTH, D_MODEL, D_FF), D_MODEL),
        "w_down": w(ks[17], (DEPTH, D_FF, D_MODEL), D_FF),
        "g_ple": gain(ks[18], (DEPTH, D_MODEL)),
        "w_ple_gate": w(ks[19], (DEPTH, D_MODEL, D_MODEL), D_MODEL),
        "w_ple_proj": w(ks[20], (DEPTH, PLE_DIM, D_MODEL), PLE_DIM),
    }

def first_block(x, p, positions, g_mix, w_in, g_qa, g_kva, w_qb, w_kvb, g_qn, g_kn,
              lb_param, g_hgo, w_o, g_ffn, w_gate, w_up, w_down, g_ple, w_ple_gate, w_ple_proj):
    inv_freq = ROPE_THETA ** (-jnp.arange(0, QK_ROPE, 2, dtype=jnp.float32) / QK_ROPE)
    ang = positions.astype(jnp.float32)[..., None] * inv_freq
    cos, sin = jnp.cos(ang), jnp.sin(ang)
    lower_bounds = jnp.cumsum(jax.nn.softmax(lb_param.astype(jnp.float32), axis=0), axis=0)

    for l in range(DEPTH):
        h = rms_norm(x, g_mix[l])
        z = h @ w_in[l]
        c_q, c_kv, k_r, hq, hf_f, hf_b, hi, hg = jnp.split(z, IN_SPLITS, axis=-1)
        a = mla(c_q, c_kv, k_r, cos, sin, g_qa[l], g_kva[l], w_qb[l], w_kvb[l], g_qn[l], g_kn[l])
        r = hgrn2(hq, hf_f, hf_b, hi, hg, lower_bounds[l], g_hgo[l])
        x = x + jnp.concatenate([a, r], axis=-1) @ w_o[l]
        h = rms_norm(x, g_ffn[l])
        x = x + (jax.nn.silu(h @ w_gate[l]) * (h @ w_up[l])) @ w_down[l]
        gate = jax.nn.sigmoid(rms_norm(x, g_ple[l]) @ w_ple_gate[l])
        x = x + gate * (p[l].astype(x.dtype) @ w_ple_proj[l])
    return x


CHUNK_2 = 128
RET_HEADS = 4
RET_DK = 128
RET_DV = 256
RET_QK_W = RET_HEADS * RET_DK
RET_V_W = RET_HEADS * RET_DV
SGU_GROUPS = 4
SGU_W = 1024
SGU_GW = SGU_W // SGU_GROUPS
D_FF_2 = 2816
CONV_W = 3
ROPE_BASE = 10000.0
IN_SPLITS_2 = (RET_QK_W, RET_QK_W, RET_V_W, RET_V_W, SGU_W, SGU_W, D_MODEL, D_MODEL)
IN_W = sum(IN_SPLITS_2)


def _rmsnorm(x, g):
    xf = x.astype(jnp.float32)
    y = xf * lax.rsqrt(jnp.mean(xf * xf, axis=-1, keepdims=True) + EPS)
    return (y * g.astype(jnp.float32)).astype(x.dtype)

def _layernorm(x, g=None, b=None):
    xf = x.astype(jnp.float32)
    mu = jnp.mean(xf, axis=-1, keepdims=True)
    var = jnp.mean(jnp.square(xf - mu), axis=-1, keepdims=True)
    y = (xf - mu) * lax.rsqrt(var + EPS)
    if g is not None:
        y = y * g.astype(jnp.float32) + b.astype(jnp.float32)
    return y.astype(x.dtype)

def _rotary(t):
    S, d = t.shape[1], t.shape[-1]
    half = d // 2
    inv_freq = 1.0 / (ROPE_BASE ** (jnp.arange(half, dtype=jnp.float32) / half))
    ang = jnp.arange(S, dtype=jnp.float32)[:, None] * inv_freq[None, :]
    cos = jnp.cos(ang)[None, :, None, :].astype(t.dtype)
    sin = jnp.sin(ang)[None, :, None, :].astype(t.dtype)
    t1, t2 = t[..., :half], t[..., half:]
    return jnp.concatenate([t1 * cos - t2 * sin, t1 * sin + t2 * cos], axis=-1)

def _to_chunks(t):
    B, S, H, d = t.shape
    return t.reshape(B, S // CHUNK_2, CHUNK_2, H, d).transpose(0, 3, 1, 2, 4)

def _from_chunks(t):
    B, H, N, C, d = t.shape
    return t.transpose(0, 2, 3, 1, 4).reshape(B, N * C, H, d)

def _retention_one_direction(q, k, v, log_gamma, strict):
    dt = q.dtype
    idx = jnp.arange(CHUNK_2, dtype=jnp.float32)
    diff = idx[:, None] - idx[None, :]
    mask = (diff > 0) if strict else (diff >= 0)
    lg = log_gamma[:, None, None]
    dmat = jnp.where(mask[None], jnp.exp(jnp.where(mask, diff, 0.0)[None] * lg), 0.0)
    s = jnp.einsum('bhncd,bhnmd->bhncm', q, k) * dmat[None, :, None].astype(dt)
    intra = jnp.einsum('bhncm,bhnme->bhnce', s, v)
    zeta = jnp.exp((CHUNK_2 - 1.0 - idx)[None, :] * log_gamma[:, None]).astype(dt)
    xi = jnp.exp((idx + 1.0)[None, :] * log_gamma[:, None]).astype(dt)
    decay_c = jnp.exp(CHUNK_2 * log_gamma).astype(dt)[None, :, None, None]
    kv = jnp.einsum('bhnmd,bhnme->nbhde', k, v * zeta[None, :, None, :, None])

    def step(state, kv_n):
        return decay_c * state + kv_n, state

    _, r_prev = lax.scan(step, jnp.zeros_like(kv[0]), kv)
    cross = jnp.einsum('bhncd,nbhde->bhnce', q * xi[None, :, None, :, None], r_prev)
    return intra + cross

def _retention_branch(q, k, v, g, ret_decay_logit, w_ret_o):
    B, S, _ = q.shape
    q = _rotary(q.reshape(B, S, RET_HEADS, RET_DK))
    k = _rotary(k.reshape(B, S, RET_HEADS, RET_DK)) * (RET_DK ** -0.5)
    v = v.reshape(B, S, RET_HEADS, RET_DV)
    log_gamma = jax.nn.log_sigmoid(ret_decay_logit.astype(jnp.float32))
    fwd = _retention_one_direction(_to_chunks(q), _to_chunks(k), _to_chunks(v), log_gamma[0], False)
    qb, kb, vb = (jnp.flip(t, axis=1) for t in (q, k, v))
    bwd = _retention_one_direction(_to_chunks(qb), _to_chunks(kb), _to_chunks(vb), log_gamma[1], True)
    o = _from_chunks(fwd) + jnp.flip(_from_chunks(bwd), axis=1)
    o = _layernorm(o).reshape(B, S, RET_V_W)
    return (o * jax.nn.silu(g)) @ w_ret_o

def _sgu_branch(u, sv, sgu_ln_g, sgu_ln_b, w_spatial, b_spatial, w_sgu_o):
    B, S, _ = u.shape
    u = jax.nn.gelu(u)
    sv = _layernorm(jax.nn.gelu(sv), sgu_ln_g, sgu_ln_b)
    svc = sv.reshape(B, S // CHUNK_2, CHUNK_2, SGU_GROUPS, SGU_GW)
    mixed = jnp.einsum('gpq,bnqgc->bnpgc', w_spatial, svc) + b_spatial.T[None, None, :, :, None]
    y = u * mixed.reshape(B, S, SGU_W)
    return y @ w_sgu_o

def _conv_gated_mlp(h, w_up, conv_w, conv_b, w_down):
    hid = h @ w_up
    c = hid.shape[-1]
    hid = lax.conv_general_dilated(
        hid, conv_w.reshape(CONV_W, 1, c), window_strides=(1,),
        padding=((CONV_W // 2, CONV_W // 2),),
        dimension_numbers=('NWC', 'WIO', 'NWC'), feature_group_count=c) + conv_b
    a, b = jnp.split(hid, 2, axis=-1)
    return (jax.nn.gelu(a) * b) @ w_down

def second_inputs(seed: int = 0) -> dict:
    key = jax.random.key(seed)
    ks = jax.random.split(key, 20)
    f32 = jnp.float32
    nrm = lambda k, shape, s: jax.random.normal(k, shape, f32) * s
    gamma0 = 1.0 - 2.0 ** (-5.0 - np.arange(RET_HEADS, dtype=np.float32))
    logit0 = jnp.asarray(np.log(gamma0) - np.log1p(-gamma0), f32)
    return {
        "x": nrm(ks[0], (BATCH, SEQ, D_MODEL), 1.0),
        "g_pre_mix": 1.0 + nrm(ks[1], (D_MODEL,), 0.05),
        "w_in": nrm(ks[2], (D_MODEL, IN_W), D_MODEL ** -0.5),
        "ret_decay_logit": logit0[None, :] + nrm(ks[3], (2, RET_HEADS), 0.1),
        "sgu_ln_g": 1.0 + nrm(ks[4], (SGU_W,), 0.05),
        "sgu_ln_b": nrm(ks[5], (SGU_W,), 0.02),
        "w_spatial": nrm(ks[6], (SGU_GROUPS, CHUNK_2, CHUNK_2), CHUNK_2 ** -0.5),
        "b_spatial": nrm(ks[7], (SGU_GROUPS, CHUNK_2), 0.02),
        "w_ret_o": nrm(ks[8], (RET_V_W, D_MODEL), RET_V_W ** -0.5),
        "w_sgu_o": nrm(ks[9], (SGU_W, D_MODEL), SGU_W ** -0.5),
        "w_out": nrm(ks[10], (D_MODEL, D_MODEL), D_MODEL ** -0.5),
        "g_post_mix": 1.0 + nrm(ks[11], (D_MODEL,), 0.05),
        "g_pre_ffn": 1.0 + nrm(ks[12], (D_MODEL,), 0.05),
        "w_up": nrm(ks[13], (D_MODEL, 2 * D_FF_2), D_MODEL ** -0.5),
        "conv_w": nrm(ks[14], (CONV_W, 2 * D_FF_2), CONV_W ** -0.5),
        "conv_b": nrm(ks[15], (2 * D_FF_2,), 0.02),
        "w_down": nrm(ks[16], (D_FF_2, D_MODEL), D_FF_2 ** -0.5),
        "g_post_ffn": 1.0 + nrm(ks[17], (D_MODEL,), 0.05),
    }

def second_block(x, g_pre_mix, w_in, ret_decay_logit, sgu_ln_g, sgu_ln_b, w_spatial, b_spatial,
              w_ret_o, w_sgu_o, w_out, g_post_mix, g_pre_ffn, w_up, conv_w, conv_b, w_down,
              g_post_ffn):
    for _ in range(DEPTH):
        h = _rmsnorm(x, g_pre_mix)
        proj = h @ w_in
        q, k, v, g, u, sv, a_ret, a_sgu = jnp.split(proj, list(np.cumsum(IN_SPLITS_2)[:-1]), axis=-1)
        y_ret = _retention_branch(q, k, v, g, ret_decay_logit, w_ret_o)
        y_sgu = _sgu_branch(u, sv, sgu_ln_g, sgu_ln_b, w_spatial, b_spatial, w_sgu_o)
        merged = jax.nn.sigmoid(a_ret) * y_ret + jax.nn.sigmoid(a_sgu) * y_sgu
        x = x + _rmsnorm(merged @ w_out, g_post_mix)
        h2 = _rmsnorm(x, g_pre_ffn)
        x = x + _rmsnorm(_conv_gated_mlp(h2, w_up, conv_w, conv_b, w_down), g_post_ffn)
    return x


def setup_inputs(seed=0):
    out = dict(first_inputs(seed))
    for name, value in second_inputs(seed + 1).items():
        if name != "x":
            out[name + "_2"] = value
    return out


def reference(
    x, p, positions, g_mix, w_in, g_qa, g_kva, w_qb, w_kvb, g_qn, g_kn, lb_param, g_hgo, w_o,
    g_ffn, w_gate, w_up, w_down, g_ple, w_ple_gate, w_ple_proj, g_pre_mix_2, w_in_2,
    ret_decay_logit_2, sgu_ln_g_2, sgu_ln_b_2, w_spatial_2, b_spatial_2, w_ret_o_2, w_sgu_o_2,
    w_out_2, g_post_mix_2, g_pre_ffn_2, w_up_2, conv_w_2, conv_b_2, w_down_2, g_post_ffn_2,
):
    x = first_block(
        x, p, positions, g_mix, w_in, g_qa, g_kva, w_qb, w_kvb, g_qn, g_kn, lb_param, g_hgo,
        w_o, g_ffn, w_gate, w_up, w_down, g_ple, w_ple_gate, w_ple_proj,
    )
    return second_block(
        x, g_pre_mix_2, w_in_2, ret_decay_logit_2, sgu_ln_g_2, sgu_ln_b_2, w_spatial_2,
        b_spatial_2, w_ret_o_2, w_sgu_o_2, w_out_2, g_post_mix_2, g_pre_ffn_2, w_up_2, conv_w_2,
        conv_b_2, w_down_2, g_post_ffn_2,
    )


_drawn_inputs = setup_inputs


def setup_inputs(seed=0):
    import zlib

    import numpy as np

    out = dict(_drawn_inputs(seed))
    spreads = {}
    factors = {'g_qa': 8.0,
     'g_kva': 7.536,
     'g_qn': 8.0,
     'g_kn': 8.0,
     'lb_param': 64.0,
     'g_ple': 200.0,
     'sgu_ln_b_2': 141.113,
     'b_spatial_2': 138.977,
     'conv_b_2': 48.056,
     'g_hgo': 8.0,
     'g_ffn': 6.804,
     'g_pre_mix_2': 12.14,
     'sgu_ln_g_2': 53.878,
     'g_post_mix_2': 35.559,
     'g_pre_ffn_2': 18.945,
     'g_post_ffn_2': 39.094,
     'w_ple_gate': 3.7,
     'ret_decay_logit_2': 8.0}
    for name, (base, spread) in spreads.items():
        noise = np.random.default_rng([zlib.crc32(name.encode()), seed]).standard_normal(out[name].shape)
        drawn = base * np.exp(spread * noise) if base else spread * noise
        out[name] = __import__('jax').numpy.asarray(drawn.astype(out[name].dtype))
    for name, factor in factors.items():
        out[name] = (out[name] * factor).astype(out[name].dtype)
    return out
```

```python
import numpy as np

import concourse.bass as bass
from concourse import mybir

F32, F32R, I32 = mybir.dt.float32, mybir.dt.float32r, mybir.dt.int32
ALU, ACT, AX = mybir.AluOpType, mybir.ActivationFunctionType, mybir.AxisListType

COMPUTE = (mybir.EngineType.PE, mybir.EngineType.Activation, mybir.EngineType.DVE)
SP_ONLY = (mybir.EngineType.SP,)

P = 128
S = 512
D = 1024
KT = D // P
TT = S // P
EPS = 1e-6
HEADS = 4
NOPE, ROPE, VH = 128, 64, 128
QK = NOPE + ROPE
LORA = 256
HG_CHUNK = 64
NCH = S // HG_CHUNK
F1 = 2816
FT = F1 // P
SLAB = 2048
CW = SLAB // KT
RDK, RDV = 128, 256
SGU_W, GRP = 1024, 4
F2T = 2 * F1 // P

ROWS = {}
_at = 0
for _n, _k in (("g_mix", 8), ("g_qa", 2), ("g_kva", 2), ("g_qn", 1), ("g_kn", 1), ("g_hgo", 4), ("lb_param", 16),
               ("g_ffn", 8), ("g_ple", 8), ("g_pre_mix_2", 8), ("g_post_mix_2", 8), ("g_pre_ffn_2", 8),
               ("g_post_ffn_2", 8), ("conv_b_2", F2T)):
    ROWS[_n] = _at
    _at += _k
assert _at <= P
ROWS["conv_w0"], ROWS["conv_w1"], ROWS["g_qn_rope"], ROWS["g_kn_rope"] = P, P + F2T, P + 2 * F2T, P + 2 * F2T + 1
ROWS["conv_w2"], ROWS["sgu_ln_g_2"], ROWS["sgu_ln_b_2"] = 2 * P, 2 * P + F2T, 2 * P + F2T + 8


def const_tables():
    i = np.arange(P)
    ident = np.eye(P)
    ones = np.ones((P, P))
    inv = (10000.0 ** (-np.arange(0, ROPE, 2) / ROPE))
    cols = np.zeros((P, 12))
    cols[:, 0] = EPS
    cols[:, 1] = np.pi / 2
    cols[:, 2] = inv[i % 32]
    cols[:, 3] = np.where(i % 64 < 32, -1.0, 1.0)
    cols[:, 4] = 1.0
    cols[:, 5] = RDK ** -0.5
    cols[:, 6] = 127 - i
    cols[:, 7] = i
    cols[:, 8] = i < 64
    cols[:, 9] = i >= 64
    small = np.concatenate([ident, ones, cols], 1)
    perm = np.zeros((P, P))
    perm[i ^ 32, i] = 1.0
    s, t = i[:, None], i[None, :]
    same = s // HG_CHUNK == t // HG_CHUNK
    maskf = same & (s <= t)
    maskb = same & (s >= t)
    reset = np.ones((P, S))
    reset[:, ::HG_CHUNK] = 0.0
    mix1 = np.concatenate([perm, maskf, maskb, reset], 1)
    m, n = i[:, None], i[None, :]
    after = np.maximum(n - m, 0)
    before = np.maximum(m - n, 0)
    xif = np.broadcast_to(n + 1, (P, P))
    xib = np.broadcast_to(P - n, (P, P))
    half = RDK // 2
    freq = (1.0 / (10000.0 ** (np.arange(half) / half))).astype(np.float32)
    ang = (np.arange(S, dtype=np.float32)[None, :] * freq[i % half][:, None]).astype(np.float32).astype(np.float64)
    cos, sin = np.cos(ang), np.sin(ang) * np.where(i < half, -1.0, 1.0)[:, None]
    mix2 = np.concatenate([after, before, xif, xib, cos, sin], 1)
    return {k: np.ascontiguousarray(v, dtype=np.float32)
            for k, v in (("const_small", small), ("const_mix1", mix1), ("const_mix2", mix2))}


class Mark:

    def __init__(self, sem, base, i=None, step=0):
        self.sem, self.base, self.i, self.step = sem, base, i, step

    def value(self):
        return self.base if self.i is None else self.i * self.step + self.base

    def before(self):
        return Mark(self.sem, self.base - self.step, self.i, self.step)

    def last(self, rounds):
        return Mark(self.sem, self.base + (rounds - 1) * self.step)


class Queue:

    def __init__(self, nc, engine, name):
        self.nc, self.e, self.sem, self.count, self.i, self.step = nc, engine, nc.alloc_semaphore(name), 0, None, 0
        self.seen = {}

    def wait(self, *marks):
        for m in marks:
            if m is None:
                continue
            key = (m.sem.name, m.i is None)
            if self.seen.get(key, -1) >= m.base:
                continue
            self.seen[key] = m.base
            self.e.wait_ge(m.sem, m.value())

    def done(self, ins):
        ins.then_inc(self.sem, 1)
        self.count += 1
        return Mark(self.sem, self.count, self.i, self.step)

    def do(self, fn, *args, after=(), **kw):
        self.wait(*after)
        return self.done(fn(*args, **kw))

    def now(self):
        return Mark(self.sem, self.count, self.i, self.step)


def program(nc, x, p, positions, g_mix, w_in, g_qa, g_kva, w_qb, w_kvb, g_qn, g_kn, lb_param, g_hgo, w_o,
            g_ffn, w_gate, w_up, w_down, g_ple, w_ple_gate, w_ple_proj, g_pre_mix_2, w_in_2,
            ret_decay_logit_2, sgu_ln_g_2, sgu_ln_b_2, w_spatial_2, b_spatial_2, w_ret_o_2, w_sgu_o_2,
            w_out_2, g_post_mix_2, g_pre_ffn_2, w_up_2, conv_w_2, conv_b_2, w_down_2, g_post_ffn_2,
            const_small, const_mix1, const_mix2, out):
    pe, act, dve = Queue(nc, nc.tensor, "pe_done"), Queue(nc, nc.scalar, "act_done"), Queue(nc, nc.vector, "dve_done")
    pool = Queue(nc, nc.gpsimd, "pool_done")
    T, A, V, G, SP = nc.tensor, nc.scalar, nc.vector, nc.gpsimd, nc.sync
    queues = (pe, act, dve, pool)
    w_in, w_qb, w_kvb, w_o, w_gate, w_up, w_down, w_ple_gate, w_ple_proj = (
        w[0] for w in (w_in, w_qb, w_kvb, w_o, w_gate, w_up, w_down, w_ple_gate, w_ple_proj))

    limit = []
    top = [(nc.sbuf_base + 63) // 64 * 64]

    def sb(name, shape, dt=F32, at=None):
        size = int(np.prod(shape[1:])) * 4
        if at is None:
            at = top[0]
            top[0] += (size + 31) // 32 * 32
            assert not limit or top[0] <= limit[0]
        return nc.alloc_sbuf_tensor_at(name, shape, dtype=dt, offset=at)

    xT = sb("residual", [P, KT, S])
    raw = [sb(f"slab_raw{j}", [P, SLAB]) for j in range(2)]
    w_hi = [sb(f"slab_hi{j}", [P, SLAB], F32R) for j in range(2)]
    w_lo = [sb(f"slab_lo{j}", [P, SLAB], F32R) for j in range(2)]
    h_hi = sb("h_hi", [P, KT, S], F32R)
    h_lo = sb("h_lo", [P, KT, S], F32R)
    cs = sb("const_small_sb", [P, 2 * P + 12])
    ident, ones, ccol = cs[:, 0:P], cs[:, P:2 * P], cs[:, 2 * P:]
    eps_col, halfpi_col, freq_col, sign_col = (ccol[:, k:k + 1] for k in range(4))
    cols = sb("param_cols", [P, 3 * P])
    dcol = sb("decay_cols", [P, 8 * 10])
    rcol = sb("rstd_cols", [P, 32])
    NT = 8
    tmp = [sb(f"tmp{j}", [P, S]) for j in range(NT)]
    tmp_end = top[0]
    arena = top[0] + 2048
    limit.append(arena)
    BLK = S * 4
    assert arena + 44 * BLK <= nc.sbuf_usable_end, (arena, nc.sbuf_usable_end)

    def slot(name, first, n, dt=F32, shape=None):
        assert first + n <= 44
        return sb(name, shape or [P, n, S], dt, at=arena + first * BLK)

    def col(name, k=0):
        c = ROWS[name] + k
        return cols[:, c:c + 1]

    bank = [nc.alloc_psum_tensor(f"bank{b}", [P, S], F32) for b in range(8)]
    free = [()] * 8
    turn = [0]

    def take(banks=(4, 5, 6, 7)):
        b = banks[turn[0] % len(banks)]
        turn[0] += 1
        claim(b)
        return b

    def claim(b):
        pe.wait(*free[b])
        if b < 4 and uses[b]:
            pe.wait(Mark(s_evac[b], uses[b]))

    landed = [nc.alloc_semaphore(f"slab_landed{j}") for j in range(2)]
    s_hi = nc.alloc_semaphore("slab_hi_done")
    s_lo = nc.alloc_semaphore("slab_lo_done")
    s_tile = nc.alloc_semaphore("slab_products")
    s_evac = [nc.alloc_semaphore(f"bank_read{b}") for b in range(4)]
    landings, landing = [0, 0], {}
    stream = {"loaded": 0, "split": 0, "used": 0}
    uses = [0] * 4
    loop = {"i": None, "n": 1}

    def at_round(value, per_round):
        return value if loop["i"] is None else loop["i"] * per_round + value

    def load_slab(columns, *srcs, i=None, per_round=2):
        g = stream["loaded"]
        stream["loaded"] += 1
        rounds = 0 if i is None else i
        if g >= 2:
            SP.wait_ge(s_lo, rounds * per_round + g - 1)
        k = srcs[0].shape[1]
        dst = raw[g % 2][:, 0:k * columns].rearrange("p (k c) -> p k c", k=k)
        at = 0
        for src in srcs:
            n = int(np.prod(src.shape[2:]))
            SP.dma_start(dst[:, :, at:at + n] if len(srcs) > 1 else dst, src).then_inc(landed[g % 2], 16)
            landings[g % 2] += 16
            at += n
        landing[g] = landings[g % 2]

    def load_loop(rounds, *sources):
        first = stream["loaded"]
        with nc.Fori(0, rounds, engines=SP_ONLY) as i:
            for src in sources:
                load_slab(SLAB // src(i).shape[1], src(i), i=i, per_round=len(sources))
        assert len(sources) == 2
        for g in range(first, first + 2 * rounds):
            landing[g] = landing[first + (g - first) % 2] + 16 * ((g - first) // 2)
        for j in range(2):
            landings[j] += 16 * (rounds - 1)
        stream["loaded"] = first + 2 * rounds

    def split_slab(slabs_per_round=2):
        g = stream["split"]
        stream["split"] += 1
        A.wait_ge(landed[g % 2], at_round(landing[g], 8 * slabs_per_round))
        if g >= 2:
            A.wait_ge(s_tile, at_round(2 * (g - 1), 2 * slabs_per_round))
        A.activation(w_hi[g % 2][:, :], raw[g % 2][:, :], ACT.Copy).then_inc(s_hi, 1)
        V.wait_ge(s_hi, at_round(g + 1, slabs_per_round))
        V.tensor_tensor(w_lo[g % 2][:, :], raw[g % 2][:, :], w_hi[g % 2][:, :].bitcast(F32),
                        ALU.subtract).then_inc(s_lo, 1)

    def slab_parts(slabs_per_round=2):
        g = stream["used"]
        stream["used"] += 1
        T.wait_ge(s_lo, at_round(g + 1, slabs_per_round))
        return g, w_hi[g % 2], w_lo[g % 2]

    def three(psum, a_hi, a_lo, b_hi, b_lo, start, stop, skip=False):
        T.matmul(psum, a_hi, b_hi, start=start, stop=False, skip_group_check=skip)
        T.matmul(psum, a_hi, b_lo, start=False, stop=False, skip_group_check=skip)
        return T.matmul(psum, a_lo, b_hi, start=False, stop=stop, skip_group_check=skip)

    def use_bank(b):
        if loop["i"] is None:
            pe.wait(*free[b])
        if uses[b]:
            T.wait_ge(s_evac[b], at_round(uses[b], 1))
        uses[b] += 1

    class Product:

        def __init__(self, b, ready):
            self.b, self.ready, self.ps = b, ready, bank[b]

        def wait(self, *qs):
            for q in qs:
                q.e.wait_ge(s_tile, self.ready)

    def products_fm(src_hi=None, src_lo=None, cols_of=None, per=2):
        g, hi, lo = slab_parts(per)
        src_hi, src_lo = src_hi or h_hi, src_lo or h_lo
        hv, lv = (w[:, :].rearrange("p (k c) -> p k c", k=KT) for w in (hi, lo))
        tiles = []
        for t in range(2):
            b = 2 * (g % 2) + t
            use_bank(b)
            for k in range(KT):
                last = three(bank[b][:, :], hv[:, k, t * P:(t + 1) * P], lv[:, k, t * P:(t + 1) * P],
                             src_hi[:, k, :], src_lo[:, k, :], k == 0, k == KT - 1)
            last.then_inc(s_tile, 1)
            tiles.append(Product(b, at_round(2 * g + t + 1, 2 * per)))
        return tiles

    def products_tm(per=2):
        g, hi, lo = slab_parts(per)
        hv, lv = (w[:, :].rearrange("p (k c) -> p k c", k=KT) for w in (hi, lo))
        tiles = []
        for t in range(2):
            b = 2 * (g % 2) + t
            use_bank(b)
            for u in range(2):
                tok = slice((2 * t + u) * P, (2 * t + u + 1) * P)
                for k in range(KT):
                    last = three(bank[b][:, u * CW:(u + 1) * CW], h_hi[:, k, tok], h_lo[:, k, tok],
                                 hv[:, k, :], lv[:, k, :], k == 0, k == KT - 1)
            last.then_inc(s_tile, 1)
            tiles.append(Product(b, at_round(2 * g + t + 1, 2 * per)))
        return tiles

    def read_last(prod, fn, *args, **kw):
        fn(*args, **kw).then_inc(s_evac[prod.b], 1)
        return Mark(s_evac[prod.b], uses[prod.b], loop["i"], 0 if loop["i"] is None else 1)

    class Loop:

        def __init__(self, n, slabs=2, bank_uses=1, **counts):
            self.n, self.slabs, self.bank_uses, self.counts = n, slabs, bank_uses, counts

        def __enter__(self):
            for b in range(4):
                pe.wait(*free[b])
            self.f = nc.Fori(0, self.n, engines=COMPUTE)
            i = self.f.__enter__()
            loop["i"] = i
            self.start = dict(stream)
            self.uses = list(uses)
            self.base = [q.count for q in queues]
            for q, k in zip(queues, ("pe", "act", "dve", "pool")):
                q.i, q.step = i, self.counts.get(k, 0)
                q.outer, q.seen = q.seen, {}
            return i

        def __exit__(self, *e):
            if e[0] is None:
                for k in ("split", "used"):
                    n = stream[k] - self.start[k]
                    assert n == self.slabs, (k, n)
                    stream[k] = self.start[k] + n * self.n
                for b in range(4):
                    assert uses[b] - self.uses[b] == self.bank_uses, (b, uses[b] - self.uses[b])
                    uses[b] = self.uses[b] + self.n * self.bank_uses
                said = {}
                for q, k, b0 in zip(queues, ("pe", "act", "dve", "pool"), self.base):
                    said[k] = q.count - b0
                wrong = {k: v for k, v in said.items() if v != self.counts.get(k, 0)}
                assert not wrong, said
                for q, b0 in zip(queues, self.base):
                    q.count = b0 + (q.count - b0) * self.n
                    q.i, q.step, q.seen = None, 0, q.outer
                loop["i"] = None
            return self.f.__exit__(*e)

    def dma(dst, src, sem, e=G):
        return e.dma_start(dst, src).then_inc(sem, 16)

    def weight_cols(w, c0, n=CW):
        return w[:, c0:c0 + n].rearrange("(k p) c -> p k c", p=P)

    def weight_cols_at(w, i, step, c0):
        return w[:, bass.ds(i * step + c0, CW)].rearrange("(k p) c -> p k c", p=P)

    def sum_rows(dst, sq, ready, first, last, clear, which=None):
        pe.wait(*ready)
        for t in range(TT):
            ins = T.matmul(dst[:, t:t + 1], sq[:, t * P:(t + 1) * P], which or ones[:, 0:1], start=clear and t == 0,
                           stop=last, skip_group_check=True)
        return pe.done(ins)

    def rstd_cols(dst, sums, n, ready):
        m = act.do(A.activation, dst, sums, ACT.Sqrt, bias=eps_col, scale=1.0 / n, after=ready)
        return dve.do(V.reciprocal, dst, dst, after=(m,)), m

    def spread(b, rcols, dtile, ready, busy=()):
        d = dtile[:, :].rearrange("p (t c) -> p t c", t=TT)
        m = dve.do(V.tensor_tensor, d, ident.unsqueeze(1).broadcast_to([P, TT, P]),
                   rcols.unsqueeze(2).broadcast_to([P, TT, P]), ALU.mult, after=(*ready, *busy))
        return pe.do(T.matmul, bank[b][:, :], ones, dtile[:, :], start=True, stop=True, after=(m,))

    def norm_to_parts(src, ready, gname, count, dst_hi, dst_lo, n, busy=()):
        b = take()
        read = {}
        for k in range(count):
            t = tmp[k % 2]
            m = act.do(A.activation, t[:, :], src[:, k, :], ACT.Square, after=(*ready, read.get(k - 2), *busy))
            read[k] = sum_rows(bank[b][:, 0:TT], t[:, :], (m,), k == 0, k == count - 1, k == 0)
        r, m = rstd_cols(rcol[:, 0:TT], bank[b][:, 0:TT], n, (read[count - 1],))
        free[b] = (m,)
        b = take()
        r = spread(b, rcol[:, 0:TT], tmp[2], (r,), busy)
        made, sub = [], {}
        for k in range(count):
            t = tmp[3 + k % 2]
            hm = dve.do(V.scalar_tensor_tensor, t[:, :], src[:, k, :], col(gname, k), bank[b][:, :],
                        ALU.mult, ALU.mult, after=(r, sub.get(k - 2), *busy))
            am = act.do(A.activation, dst_hi[:, k, :], t[:, :], ACT.Copy, after=(hm, *busy))
            sub[k] = dve.do(V.tensor_tensor, dst_lo[:, k, :], t[:, :], dst_hi[:, k, :].bitcast(F32),
                            ALU.subtract, after=(am,))
            made.append(sub[k])
        free[b] = (hm,)
        return made[-1]

    def split_tile(t_ap, ready, hi_ap, lo_ap, busy=()):
        am = act.do(A.activation, hi_ap, t_ap, ACT.Copy, after=(*ready, *busy))
        return dve.do(V.tensor_tensor, lo_ap, t_ap, hi_ap.bitcast(F32), ALU.subtract, after=(am,))

    d_const, d_rows, d_x = (nc.alloc_semaphore(n) for n in ("consts_landed", "rows_landed", "x_landed"))
    c1 = slot("const_mix1_sb", 43, 1, shape=[P, 3 * P + P])
    perm, maskf, maskb = c1[:, 0:P], c1[:, P:2 * P], c1[:, 2 * P:3 * P]
    x_tm = slot("x_tm", 0, 8, shape=[P, TT, D])
    rows = slot("param_rows", 8, 1, shape=[P, 3, P])
    rows_zero = dve.do(V.memset, rows[:, :, :], 0.0)
    dma(cs[:, :], const_small, d_const, SP)
    for t in range(TT):
        dma(x_tm[:, t, :], x[0, t * P:(t + 1) * P, :], d_x, SP)
    load_slab(CW, weight_cols(w_in, 0))
    G.wait_ge(dve.sem, rows_zero.base)
    n_rows = 0
    for name, ap in (("g_mix", g_mix), ("g_qa", g_qa), ("g_kva", g_kva), ("g_qn", g_qn[:, 0:NOPE]),
                     ("g_kn", g_kn[:, 0:NOPE]), ("g_ffn", g_ffn), ("g_ple", g_ple)):
        src = ap.rearrange("a (k c) -> (a k) c", c=P)
        r = ROWS[name]
        dma(rows[r:r + src.shape[0], 0, :], src, d_rows)
        n_rows += 16
    for name, src in (("g_hgo", g_hgo.rearrange("a h d -> (a h) d")),
                      ("lb_param", lb_param.rearrange("a d (h c) -> (a d h) c", c=P)),
                      *((n, ap.rearrange("(k c) -> k c", c=P)) for n, ap in (
                          ("g_pre_mix_2", g_pre_mix_2), ("g_post_mix_2", g_post_mix_2), ("g_pre_ffn_2", g_pre_ffn_2),
                          ("g_post_ffn_2", g_post_ffn_2), ("conv_b_2", conv_b_2)))):
        r = ROWS[name]
        dma(rows[r:r + src.shape[0], 0, :], src, d_rows)
        n_rows += 16
    for k in range(3):
        src = conv_w_2[k, :].rearrange("(k c) -> k c", c=P)
        r, blk = ROWS[f"conv_w{k}"] % P, ROWS[f"conv_w{k}"] // P
        dma(rows[r:r + F2T, blk, :], src, d_rows)
        n_rows += 16
    for name, ap in (("sgu_ln_g_2", sgu_ln_g_2), ("sgu_ln_b_2", sgu_ln_b_2)):
        r = ROWS[name] - 2 * P
        dma(rows[r:r + 8, 2, :], ap.rearrange("(k c) -> k c", c=P), d_rows)
        n_rows += 16
    for name, ap in (("g_qn_rope", g_qn), ("g_kn_rope", g_kn)):
        r = ROWS[name] - P
        for half in range(2):
            dma(rows[r:r + 1, 1, half * ROPE:(half + 1) * ROPE], ap[:, NOPE:QK], d_rows)
            n_rows += 16
    def cols_of(w, c0=0, step=2 * CW):
        return lambda i: weight_cols_at(w, i, step, c0)

    def rows_of(w, s0, per_round):
        return lambda i: w[bass.ds(i * (per_round * 2 * P) + s0 * 2 * P, 2 * P), :].rearrange("(k p) c -> p k c", p=P)

    load_slab(CW, weight_cols(w_in, LORA))
    load_slab(2 * ROPE, *[weight_cols(w_in, 2 * LORA, ROPE)] * 2)
    z0 = 2 * LORA + ROPE
    load_loop(5, cols_of(w_in, z0), cols_of(w_in, z0 + CW))
    qb_cols = w_qb.rearrange("(k p) (h c) -> p k h c", p=P, c=QK)
    load_slab(HEADS * QK, *[qb_cols[:, :, hd, 0:NOPE] for hd in range(HEADS)],
              *[qb_cols[:, :, hd, NOPE:QK] for hd in range(HEADS)])
    load_slab(HEADS * 2 * P, w_kvb.rearrange("(k p) c -> p k c", p=P))
    load_loop(2, cols_of(w_o), cols_of(w_o, CW))
    load_loop(FT // 2, cols_of(w_gate, 0, CW), cols_of(w_up, 0, CW))
    load_slab(D, w_down[0:2 * P, :].rearrange("(k p) c -> p k c", p=P))
    load_loop(FT // 4, rows_of(w_down, 1, 2), rows_of(w_down, 2, 2))
    load_slab(D, w_ple_proj.rearrange("(k p) c -> p k c", p=P))
    load_loop(2, cols_of(w_ple_gate), cols_of(w_ple_gate, CW))
    load_loop(6, cols_of(w_in_2), cols_of(w_in_2, CW))
    load_loop(2, cols_of(w_in_2, 4 * D), cols_of(w_in_2, 4 * D + CW))
    load_loop(4, cols_of(w_ret_o_2, 0, CW), cols_of(w_in_2, 5 * D, CW))
    load_loop(2, cols_of(w_in_2, 3 * D), cols_of(w_in_2, 3 * D + CW))
    load_loop(4, cols_of(w_sgu_o_2, 0, CW), cols_of(w_in_2, 6 * D, CW))
    load_loop(2, cols_of(w_out_2), cols_of(w_out_2, CW))
    load_loop(FT // 2, cols_of(w_up_2, 0, CW), cols_of(w_up_2, F1, CW))
    load_slab(D, w_down_2[0:2 * P, :].rearrange("(k p) c -> p k c", p=P))
    load_loop(FT // 4, rows_of(w_down_2, 1, 2), rows_of(w_down_2, 2, 2))
    T.wait_ge(d_const, 16)
    A.wait_ge(d_const, 16)
    V.wait_ge(d_const, 16)
    T.wait_ge(d_x, 16 * TT)

    x_ready = []
    for k in range(KT):
        b = take((4, 5, 6, 7))
        for t in range(TT):
            m = T.transpose(bank[b][:, t * P:(t + 1) * P], x_tm[:, t, k * P:(k + 1) * P], ident)
        m = pe.done(m)
        if k % 2:
            e = dve.do(V.tensor_copy, xT[:, k, :], bank[b][:, :], after=(m,))
        else:
            e = act.do(A.activation, xT[:, k, :], bank[b][:, :], ACT.Copy, after=(m,))
        free[b] = (e,)
        x_ready.append(e)
    T.wait_ge(d_rows, n_rows)
    b = take()
    for blk in range(3):
        m = T.transpose(bank[b][:, blk * P:(blk + 1) * P], rows[:, blk, :], ident)
    cols_ready = dve.do(V.tensor_copy, cols[:, :], bank[b][:, 0:3 * P], after=(pe.done(m),))
    free[b] = (cols_ready,)
    split_slab()

    ready = norm_to_parts(xT, (x_ready[-1], x_ready[-2], cols_ready), "g_mix", KT, h_hi, h_lo, D)
    d_c1 = nc.alloc_semaphore("mix1_consts_landed")
    G.wait_ge(pe.sem, pe.count)
    dma(c1[:, 0:3 * P], const_mix1[:, 0:3 * P], d_c1)

    zt = slot("z", 0, 20)
    v_hg = zt[:, 12:16, :]
    c_raw = slot("c_raw", 20, 4)
    cq_hi, cq_lo, ckv_hi, ckv_lo = (slot(n, 32 + 2 * k, 2, F32R)
                                    for k, n in enumerate(("cq_hi", "cq_lo", "ckv_hi", "ckv_lo")))
    c_hi = [cq_hi[:, 0, :], cq_hi[:, 1, :], ckv_hi[:, 0, :], ckv_hi[:, 1, :]]
    c_lo = [cq_lo[:, 0, :], cq_lo[:, 1, :], ckv_lo[:, 0, :], ckv_lo[:, 1, :]]
    kr_raw = slot("kr_raw", 24, 1)
    pe.wait(ready)

    def copy_out(prod, q, dst, after=()):
        prod.wait(q)
        q.wait(*after)
        if q is act:
            return read_last(prod, A.activation, dst, prod.ps[:, :], ACT.Copy)
        return read_last(prod, V.tensor_copy, dst, prod.ps[:, :])

    c_ready = []
    for j in range(2):
        split_slab()
        tiles = products_fm()
        for t in range(2):
            c_ready.append(copy_out(tiles[t], (act, dve)[t], c_raw[:, 2 * j + t, :]))
    split_slab()
    g, hi, lo = slab_parts()
    hv, lv = (w[:, 0:KT * 2 * ROPE].rearrange("p (k c) -> p k c", k=KT) for w in (hi, lo))
    b = 2 * (g % 2)
    use_bank(b)
    use_bank(b + 1)
    for k in range(KT):
        last = three(bank[b][:, :], hv[:, k, :], lv[:, k, :], h_hi[:, k, :], h_lo[:, k, :], k == 0, k == KT - 1)
    last.then_inc(s_tile, 2)
    A.wait_ge(s_tile, 2 * g + 2)
    ins = A.activation(kr_raw[:, 0, :], bank[b][:, :], ACT.Copy)
    ins.then_inc(s_evac[b], 1)
    A.sem_inc(s_evac[b + 1], 1)

    with Loop(3) as i:
        for s2 in range(2):
            split_slab()
            tiles = products_fm()
            for t in range(2):
                q = (act, dve)[t]
                tiles[t].wait(q)
                dst = zt[:, bass.ds(i * 4 + 2 * s2 + t, 1), :].rearrange("p a s -> p (a s)")
                if t == 0:
                    m = read_last(tiles[t], A.activation, dst, tiles[t].ps[:, :], ACT.Copy)
                else:
                    m = read_last(tiles[t], V.tensor_copy, dst, tiles[t].ps[:, :])
    for s2 in range(2):
        split_slab()
        tiles = products_tm()
        for t in range(2):
            q = (act, dve)[t]
            tiles[t].wait(q)
            dst = v_hg[:, 2 * t:2 * t + 2, s2 * CW:(s2 + 1) * CW]
            src = tiles[t].ps[:, :].rearrange("p (u c) -> p u c", u=2)
            if t == 0:
                m = read_last(tiles[t], A.activation, dst, src, ACT.Copy)
            else:
                m = read_last(tiles[t], V.tensor_copy, dst, src)
    for s2 in range(2):
        split_slab()
        tiles = products_fm()
        for t in range(2):
            copy_out(tiles[t], (act, dve)[t], zt[:, 16 + 2 * s2 + t, :])
    z_ready = [Mark(s_evac[b], uses[b]) for b in range(4)]
    q_nope, q_rope = slot("q_nope", 25, 4), slot("q_rope", 29, 2)
    k_nope, k_rope = slot("k_nope", 20, 4), slot("k_rope", 40, 2)
    v_mla = slot("v_mla", 32, 4)
    cos1, sin1 = slot("rope_cos", 42, 1)[:, 0, :], slot("rope_sin", 31, 1)[:, 0, :]

    c_all = (c_ready[0], c_ready[1], c_ready[2], c_ready[3])
    b = take()
    read = {}
    for k in range(4):
        m = act.do(A.activation, tmp[k % 2][:, :], c_raw[:, k, :], ACT.Square, after=(*c_all, read.get(k - 2)))
        read[k] = sum_rows(bank[b][:, TT * (k // 2):TT * (k // 2 + 1)], tmp[k % 2][:, :], (m,), k % 2 == 0, k % 2 == 1,
                           k == 0)
    r, m = rstd_cols(rcol[:, 0:2 * TT], bank[b][:, 0:2 * TT], LORA, (read[3],))
    free[b] = (m,)
    c_parts = []
    for j, gname in enumerate(("g_qa", "g_kva")):
        b = take()
        rr = spread(b, rcol[:, TT * j:TT * (j + 1)], tmp[2 + j], (r,))
        for k in range(2):
            kk = 2 * j + k
            hm = dve.do(V.scalar_tensor_tensor, tmp[4 + kk][:, :], c_raw[:, kk, :], col(gname, k), bank[b][:, :],
                        ALU.mult, ALU.mult, after=(rr,))
            c_parts.append(split_tile(tmp[4 + kk][:, :], (hm,), c_hi[kk], c_lo[kk]))
        free[b] = (hm,)

    pos_i = sb("pos_i", [P, S], I32, at=arena + 31 * BLK)
    d_pos = nc.alloc_semaphore("positions_landed")
    dma(pos_i[:, :], positions[0].partition_broadcast(P), d_pos)
    V.wait_ge(d_pos, 16)
    C1, C2 = 6.28125, float(np.float32(2 * np.pi - 6.28125) // 2.0 ** -23 * 2.0 ** -23)
    C3 = float(2 * np.pi - C1 - C2)
    MAGIC = 1.5 * 2.0 ** 23
    PI = 3.1415925
    m = dve.do(V.tensor_copy, tmp[0][:, :], pos_i[:, :], after=(read[3],))
    m = dve.do(V.tensor_scalar, tmp[0][:, :], tmp[0][:, :], freq_col, None, ALU.mult, after=(m,))
    m = dve.do(V.tensor_scalar, tmp[1][:, :], tmp[0][:, :], float(1 / (2 * np.pi)), MAGIC, ALU.mult, ALU.add, after=(m,))
    m = dve.do(V.tensor_scalar, tmp[1][:, :], tmp[1][:, :], MAGIC, None, ALU.subtract, after=(m,))
    for c in (C1, C2, C3):
        m = dve.do(V.scalar_tensor_tensor, tmp[0][:, :], tmp[1][:, :], -c, tmp[0][:, :], ALU.mult, ALU.add, after=(m,))
    m = dve.do(V.tensor_scalar, tmp[0][:, :], tmp[0][:, :], -PI, PI, ALU.max, ALU.min, after=(m,))
    m1 = act.do(A.activation, tmp[1][:, :], tmp[0][:, :], ACT.Abs, after=(m,))
    m1 = act.do(A.activation, cos1, tmp[1][:, :], ACT.Sin, bias=halfpi_col, scale=-1.0, after=(m1,))
    m2 = act.do(A.activation, tmp[1][:, :], tmp[0][:, :], ACT.Sin, after=(m1,))
    tables = dve.do(V.tensor_scalar, sin1, tmp[1][:, :], sign_col, None, ALU.mult, after=(m1, m2))
    V.wait_ge(d_c1, 16)
    T.wait_ge(d_c1, 16)

    def rotate(t, ready, gcol, tb, g_done=False):
        if gcol is not None:
            ready = (dve.do(V.tensor_scalar, t, t, gcol, None, ALU.mult, after=ready),)
        b = take((4, 5, 6))
        m = pe.do(T.matmul, bank[b][:, :], perm, t, start=True, stop=True, after=ready)
        sw = dve.do(V.tensor_tensor, tmp[tb][:, :], bank[b][:, :], sin1, ALU.mult, after=(m, tables))
        free[b] = (sw,)
        m = dve.do(V.tensor_tensor, t, t, cos1, ALU.mult, after=(m, sw))
        return dve.do(V.tensor_tensor, t, t, tmp[tb][:, :], ALU.add, after=(m, sw))

    claim(7)
    sums = bank[7]
    sq_read = {}
    nsq = [0]

    def squares(src, ready, jobs):
        n = nsq[0]
        nsq[0] += 1
        t = tmp[n % 2]
        m = act.do(A.activation, t[:, :], src, ACT.Square, after=(*ready, sq_read.get(n - 2)))
        for hd, rws, first, last in jobs:
            sq_read[n] = sum_rows(sums[:, TT * hd:TT * (hd + 1)], t[:, :], (m,), first, last, n == 0 and hd == jobs[0][0],
                                  rws)
        return m, sq_read[n]

    lower_half, upper_half, all_rows = ccol[:, 8:9], ccol[:, 9:10], None
    kr_done = [squares(kr_raw[:, 0, :], z_ready + [m2], [(HEADS + hd, lower_half, True, False) for hd in range(HEADS)])]
    KR = rotate(kr_raw[:, 0, :], (kr_done[0][0], cols_ready, *z_ready), col("g_kn_rope"), 4)

    split_slab()
    g, hi, lo = slab_parts()
    hv, lv = (w[:, 0:2 * HEADS * QK].rearrange("p (k c) -> p k c", k=2) for w in (hi, lo))
    pe.wait(c_parts[1])
    q_ready = []
    for t in range(6):
        b = take((4, 5, 6))
        for k in range(2):
            m = three(bank[b][:, :], hv[:, k, t * P:(t + 1) * P], lv[:, k, t * P:(t + 1) * P],
                      c_hi[k], c_lo[k], k == 0, k == 1)
        if t in (2, 5):
            m.then_inc(s_tile, 1)
            m = Mark(s_tile, 2 * g + 1 + (t == 5))
        else:
            m = pe.done(m)
        dst = q_nope[:, t, :] if t < HEADS else q_rope[:, t - HEADS, :]
        e = dve.do(V.tensor_copy, dst, bank[b][:, :], after=(m,))
        jobs = ([(t, all_rows, True, False)] if t < HEADS else
                [(2 * (t - HEADS), lower_half, False, True), (2 * (t - HEADS) + 1, upper_half, False, True)])
        squares(dst, (e,), jobs)
        free[b] = (e,)
        q_ready.append(e)

    split_slab()
    g, hi, lo = slab_parts()
    hv, lv = (w[:, :].rearrange("p (k h c) -> p k h c", k=2, h=HEADS) for w in (hi, lo))
    pe.wait(c_parts[3])
    k_ready, v_ready = [], []
    for t in range(HEADS):
        b = take((4, 5, 6))
        for k in range(2):
            m = three(bank[b][:, :], hv[:, k, t, 0:P], lv[:, k, t, 0:P], c_hi[2 + k], c_lo[2 + k],
                      k == 0, k == 1)
        m = pe.done(m)
        e = dve.do(V.tensor_copy, k_nope[:, t, :], bank[b][:, :], after=(m,))
        _, last_sq = squares(k_nope[:, t, :], (e,), [(HEADS + t, all_rows, False, True)])
        free[b] = (e,)
        k_ready.append(e)
    r_all, m = rstd_cols(rcol[:, :], sums[:, 0:32], QK, (last_sq,))
    free[7] = (m,)
    for t in range(TT):
        b = take((4, 5, 6))
        tok = slice(t * P, (t + 1) * P)
        for k in range(2):
            m = three(bank[b][:, :].rearrange("p (h c) -> p h c", h=HEADS), ckv_hi[:, k, tok], ckv_lo[:, k, tok],
                      hv[:, k, :, P:2 * P], lv[:, k, :, P:2 * P], k == 0, k == 1)
        if t in (1, 3):
            m.then_inc(s_tile, 1)
            m = Mark(s_tile, 2 * g + 1 + (t == 3))
        else:
            m = pe.done(m)
        e = act.do(A.activation, v_mla[:, t, :], bank[b][:, :], ACT.Copy, after=(m, Mark(s_tile, 2 * g)))
        free[b] = (e,)
        v_ready.append(e)

    dt_free = {}
    head_ready = {}
    for n in range(2 * HEADS):
        hd, is_k = n % HEADS, n >= HEADS
        half = slice(ROPE * (hd % 2), ROPE * (hd % 2 + 1))
        b = take((4, 5, 6))
        dt = tmp[2 + n % 2]
        rr = spread(b, rcol[:, TT * n:TT * (n + 1)], dt, (r_all, dt_free.get(n - 2), *c_parts))
        dt_free[n] = rr
        t = (k_nope if is_k else q_nope)[:, hd, :]
        m1 = dve.do(V.scalar_tensor_tensor, t, t, col("g_kn" if is_k else "g_qn"), bank[b][:, :], ALU.mult, ALU.mult,
                    after=(rr, (k_ready if is_k else q_ready)[hd]))
        if is_k:
            m2 = dve.do(V.tensor_tensor, k_rope[half, hd // 2, :], kr_raw[half, 0, :], bank[b][half, :], ALU.mult,
                        after=(rr, KR))
        else:
            t = q_rope[half, hd // 2, :]
            m2 = dve.do(V.scalar_tensor_tensor, t, t, col("g_qn_rope")[half, :], bank[b][half, :], ALU.mult, ALU.mult,
                        after=(rr, q_ready[HEADS + hd // 2]))
        free[b] = (m1, m2)
        head_ready[n] = (m1, m2)
        if not is_k and hd % 2:
            m = rotate(q_rope[:, hd // 2, :], (m2,), None, 4 + hd // 2)
            head_ready[n] = (m1, m)
            head_ready[n - 1] = (head_ready[n - 1][0], m)

    p_t = slot("weights_t", 36, 4)
    scale = QK ** -0.5
    mcol = sb("softmax_cols", [P, 2, 4])
    pv_done, exp_read, copied = None, {}, {}
    units = [(hd, j) for hd in range(HEADS) for j in range(TT)]
    score, attn_ready = {}, []

    def scores(u):
        hd, j = units[u]
        b = take((4, 5, 6))
        qt = slice(j * P, (j + 1) * P)
        half = slice(ROPE * (hd % 2), ROPE * (hd % 2 + 1))
        pe.wait(*head_ready[hd], *head_ready[HEADS + hd])
        T.matmul(bank[b][:, :], q_nope[:, hd, qt], k_nope[:, hd, :], start=True, stop=False)
        m = pe.done(T.matmul(bank[b][:, :], q_rope[half, hd // 2, qt], k_rope[half, hd // 2, :], start=False, stop=True))
        c = mcol[:, u % 2, :]
        m = dve.do(V.reduce_max, c[:, 0:1], bank[b][:, :], AX.X, after=(m,))
        m = dve.do(V.tensor_scalar, c[:, 1:2], c[:, 0:1], -scale, None, ALU.mult, after=(m,))
        w = tmp[u % 2]
        m = act.do(A.activation, w[:, :], bank[b][:, :], ACT.Exp, bias=c[:, 1:2], scale=scale, accum_out=c[:, 2:3],
                   after=(m, exp_read.get(u - 2)))
        free[b] = (m,)
        m = dve.do(V.reciprocal, c[:, 3:4], c[:, 2:3], after=(m,))
        score[u] = dve.do(V.tensor_scalar, w[:, :], w[:, :], c[:, 3:4], None, ALU.mult, after=(m,))

    def transposed(u):
        hd, j = units[u]
        b = take((0, 1))
        pe.wait(score[u])
        for kb in range(TT):
            m = T.transpose(bank[b][:, kb * P:(kb + 1) * P], tmp[u % 2][:, kb * P:(kb + 1) * P], ident)
        m = exp_read[u] = pe.done(m)
        copied[u] = act.do(A.activation, p_t[:, :, j * P:(j + 1) * P],
                           bank[b][:, :].rearrange("p (k q) -> p k q", k=TT), ACT.Copy,
                           after=(m, pv_done, *((v_ready[-1],) if u == 0 else ())))
        free[b] = (copied[u],)

    def values(hd):
        b = take((2, 3))
        pe.wait(copied[TT * hd + TT - 1])
        for kb in range(TT):
            m = T.matmul(bank[b][:, :], v_mla[:, kb, hd * VH:(hd + 1) * VH], p_t[:, kb, :], start=kb == 0,
                         stop=kb == TT - 1)
        m = pe.done(m)
        am = act.do(A.activation, h_hi[:, hd, :], bank[b][:, :], ACT.Copy, after=(m,))
        e = dve.do(V.tensor_tensor, h_lo[:, hd, :], bank[b][:, :], h_hi[:, hd, :].bitcast(F32), ALU.subtract, after=(am,))
        free[b] = (e,)
        attn_ready.append(e)
        return m

    for u in range(len(units) + 1):
        if u < len(units):
            scores(u)
        if u >= 1:
            transposed(u - 1)
            if u % TT == 0:
                pv_done = values(u // TT - 1)

    lbc = sb("lower_bounds", [P, 4, 8])
    L0, L1 = (cols[:, ROWS["lb_param"] + 8 * k:ROWS["lb_param"] + 8 * (k + 1)] for k in range(2))
    lower, one_minus, e0, e1 = (lbc[:, k, :] for k in range(4))
    m = dve.do(V.tensor_tensor, lower, L0, L1, ALU.max, after=(cols_ready,))
    a0 = dve.do(V.tensor_tensor, e0, L0, lower, ALU.subtract, after=(m,))
    a1 = dve.do(V.tensor_tensor, e1, L1, lower, ALU.subtract, after=(m,))
    m0 = act.do(A.activation, e0, e0, ACT.Exp, after=(a0,))
    m1 = act.do(A.activation, e1, e1, ACT.Exp, after=(a1,))
    m = dve.do(V.tensor_tensor, e1, e0, e1, ALU.add, after=(m0, m1))
    m = dve.do(V.reciprocal, e1, e1, after=(m,))
    m = dve.do(V.tensor_tensor, lower, e0, e1, ALU.mult, after=(m,))
    low_ready = dve.do(V.tensor_scalar, one_minus, lower, -1.0, 1.0, ALU.mult, ALU.add, after=(m,))
    for k in range(HEADS):
        hq_ready = act.do(A.activation, zt[:, k, :], zt[:, k, :], ACT.Silu, after=z_ready)
        hg_ready = act.do(A.activation, zt[:, 16 + k, :], zt[:, 16 + k, :], ACT.Silu)
    log_f = slot("log_f", 20, 8)
    f_ready = []
    for k in range(8):
        f = zt[:, 4 + k, :]
        m = act.do(A.activation, f, f, ACT.Sigmoid)
        f_ready.append(dve.do(V.tensor_scalar, f, f, one_minus[:, k:k + 1], lower[:, k:k + 1], ALU.mult, ALU.add,
                              after=(m, low_ready)))
    lf_ready = []
    all_attn = pe.now()
    for k in range(8):
        lf_ready.append(act.do(A.activation, log_f[:, k, :], zt[:, 4 + k, :], ACT.Ln, after=(f_ready[k], all_attn)))
    reset = slot("reset", 42, 1)[:, 0, :]
    d_reset = nc.alloc_semaphore("reset_landed")
    G.wait_ge(pe.sem, all_attn.base)
    G.wait_ge(dve.sem, dve.count)
    dma(reset, const_mix1[:, 3 * P:3 * P + S], d_reset)
    V.wait_ge(d_reset, 16)

    gl = [[slot(f"gla_{n}{k}", 28 + 4 * k + j, 1)[:, 0, :] for j, n in enumerate(("qi", "ki", "qb", "kd"))] for k in range(2)]
    a_t = [slot(f"gla_a{k}", 36 + k, 1)[:, 0, :] for k in range(2)]
    kd_t = [slot(f"gla_kdt{k}", 38 + k, 1)[:, 0, :].rearrange("p (j d) -> p j d", j=TT) for k in range(2)]
    states = [slot("gla_s0", 40, 2, shape=[P, NCH, P]),
              sb("gla_s1", [P, NCH, P], at=tmp_end - 2 * BLK)]
    bt = [tmp[4], tmp[5]]
    decs = sb("gla_decay", [P, 2, NCH])
    used_by, a_read, kd_read, st_read, dec_read = {}, {}, {}, {}, {}
    o_bank, o_sq, o_ready = {}, {}, {}
    stage = {}

    def chunks(t):
        return t.rearrange("p (c t) -> p c t", t=HG_CHUNK)

    def prepare(n):
        hd, back = n // 2, n % 2
        k = 4 * back + hd
        f, lf, q = zt[:, 4 + k, :], log_f[:, k, :], zt[:, hd, :]
        par = n % 2
        qi, ki, qb, kd = gl[par]
        bb, t0, t1 = bt[par][:, :], tmp[2 * par][:, :], tmp[2 * par + 1][:, :]
        mid, last = (HG_CHUNK // 2, 0) if back else (HG_CHUNK // 2 - 1, HG_CHUNK - 1)
        busy = used_by.get(n - 2, ())
        if back:
            m = dve.do(V.tensor_tensor_scan, bb[:, ::-1], reset, lf[:, ::-1], 0.0, ALU.mult, ALU.add,
                       after=(lf_ready[k], *busy))
        else:
            m = dve.do(V.tensor_tensor_scan, bb, reset, lf, 0.0, ALU.mult, ALU.add, after=(lf_ready[k], *busy))
        at = lambda x: chunks(bb)[:, :, x:x + 1].broadcast_to([P, NCH, HG_CHUNK])
        m_mid = dve.do(V.tensor_tensor, chunks(t0), chunks(bb), at(mid), ALU.subtract, after=(m,))
        m_last = dve.do(V.tensor_tensor, chunks(t1), at(last), chunks(bb), ALU.subtract, after=(m,))
        m_k = dve.do(V.tensor_scalar, lf, f, -1.0, 1.0, ALU.mult, ALU.add, after=(m,))
        e1 = act.do(A.activation, qi, t0, ACT.Exp, after=(m_mid, *busy))
        e2 = act.do(A.activation, ki, t0, ACT.Exp, scale=-1.0)
        e3 = act.do(A.activation, kd, t1, ACT.Exp, after=(m_last,))
        e4 = act.do(A.activation, qb, bb, ACT.Exp)
        dec = decs[:, par, :]
        e5 = act.do(A.activation, dec, chunks(bb)[:, :, last:last + 1].rearrange("p c t -> p (c t)"), ACT.Exp,
                    after=dec_read.get(n - 2, ()))
        m1 = dve.do(V.tensor_tensor, qi, qi, q, ALU.mult, after=(e1, hq_ready))
        m2 = dve.do(V.tensor_tensor, ki, ki, lf, ALU.mult, after=(e2, m_k))
        m3 = dve.do(V.tensor_tensor, kd, kd, lf, ALU.mult, after=(e3,))
        m4 = dve.do(V.tensor_tensor, qb, qb, q, ALU.mult, after=(e4,))
        stage[n] = (m2, m3, m4, e5)

    def intra(n):
        hd, back = n // 2, n % 2
        par = n % 2
        qi, ki, qb, kd = gl[par]
        m2, m3, m4, e5 = stage[n]
        b = take((4, 5))
        pe.wait(m2)
        for j in range(TT):
            sl = slice(j * P, (j + 1) * P)
            m = T.matmul(bank[b][:, sl], ki[:, sl], qi[:, sl], start=j == 0, stop=True, skip_group_check=True)
        m = pe.done(m)
        mask = maskb if back else maskf
        e = dve.do(V.tensor_tensor, a_t[par].rearrange("p (j t) -> p j t", j=TT),
                   bank[b][:, :].rearrange("p (j t) -> p j t", j=TT), mask.unsqueeze(1).broadcast_to([P, TT, P]),
                   ALU.mult, after=(m, a_read.get(n - 2)))
        free[b] = (e,)
        b = take((4, 5))
        pe.wait(m3)
        for j in range(TT):
            m = T.transpose(bank[b][:, j * P:(j + 1) * P], kd[:, j * P:(j + 1) * P], ident)
        m = pe.done(m)
        e2 = act.do(A.activation, kd_t[par], bank[b][:, :].rearrange("p (j d) -> p j d", j=TT), ACT.Copy,
                    after=(m, kd_read.get(n - 2)))
        free[b] = (e2,)
        stage[n] = (e, e2, m4, e5, m)

    def state(n):
        hd, back = n // 2, n % 2
        par = n % 2
        e, e2, m4, e5, mt = stage[n]
        cols_v = slice(hd * P, (hd + 1) * P)
        bs = (6, 7)
        for half in range(2):
            claim(bs[half])
        pe.wait(e2)
        order = list(range(NCH - 1, 0, -1)) if back else list(range(NCH - 1))
        for half in range(2):
            rws = slice(HG_CHUNK * half, HG_CHUNK * (half + 1))
            first = True
            for c in (c for c in range(NCH) if c % 2 == half and c in order):
                j = c // 2
                m = T.matmul(bank[bs[half]][:, j * P:(j + 1) * P], kd_t[par][rws, j, :], v_hg[rws, j, cols_v],
                             start=first, stop=True, skip_group_check=True)
                first = False
        m = kd_read[n] = pe.done(m)
        st = states[par]
        prev = None
        for c in order:
            to = c - 1 if back else c + 1
            kv = bank[bs[c % 2]][:, (c // 2) * P:(c // 2 + 1) * P]
            if prev is None:
                s_m = dve.do(V.tensor_copy, st[:, to, :], kv, after=(m, st_read.get(n - 2)))
            else:
                s_m = dve.do(V.scalar_tensor_tensor, st[:, to, :], st[:, c, :], decs[:, par, c:c + 1], kv,
                             ALU.mult, ALU.add, after=(prev, e5))
            prev = s_m
        free[6] = free[7] = (prev,)
        dec_read[n] = (prev,)
        stage[n] = (e, m4, prev, mt)

    def outputs(n):
        hd, back = n // 2, n % 2
        par = n % 2
        e, m4, s_m, mt = stage[n]
        if not back:
            o_bank[hd] = take((0, 1))
        b = o_bank[hd]
        pe.wait(e, m4, s_m)
        cols_v = slice(hd * P, (hd + 1) * P)
        for j in range(TT):
            sl = slice(j * P, (j + 1) * P)
            m = T.matmul(bank[b][:, sl], v_hg[:, j, cols_v], a_t[par][:, sl], start=not back and j == 0, stop=False,
                         skip_group_check=True)
        qb = gl[par][2]
        for c in range(NCH):
            if c == (NCH - 1 if back else 0):
                continue
            sl = slice(c * HG_CHUNK, (c + 1) * HG_CHUNK)
            m = T.matmul(bank[b][:, sl], states[par][:, c, :], qb[:, sl], start=False, stop=True, skip_group_check=True)
        m = pe.done(m)
        a_read[n] = st_read[n] = m
        used_by[n] = (m,)
        if back:
            o = zt[:, 4 + hd, :]
            o_ready[hd] = dve.do(V.tensor_copy, o, bank[b][:, :], after=(m,))
            free[b] = (o_ready[hd],)

    for n in range(2 * HEADS + 1):
        if n < 2 * HEADS:
            prepare(n)
            intra(n)
            state(n)
        if n:
            outputs(n - 1)

    b = take((4, 5))
    read = {}
    for hd in range(HEADS):
        t = tmp[hd % 2]
        m = act.do(A.activation, t[:, :], zt[:, 4 + hd, :], ACT.Square, after=(o_ready[hd], read.get(hd - 2), stage[7][0]))
        read[hd] = sum_rows(bank[b][:, TT * hd:TT * (hd + 1)], t[:, :], (m,), True, True, hd == 0)
    r, m = rstd_cols(rcol[:, 0:4 * TT], bank[b][:, 0:4 * TT], P, (read[3],))
    free[b] = (m,)
    mix_ready = list(attn_ready)
    for hd in range(HEADS):
        b = take((4, 5))
        rr = spread(b, rcol[:, TT * hd:TT * (hd + 1)], tmp[2 + hd % 2], (r, *((dt_free[hd - 2],) if hd >= 2 else ())))
        dt_free[hd] = rr
        o = zt[:, 4 + hd, :]
        m = dve.do(V.scalar_tensor_tensor, o, o, col("g_hgo", hd), bank[b][:, :], ALU.mult, ALU.mult, after=(rr, read[hd]))
        free[b] = (m,)
        m = dve.do(V.tensor_tensor, o, o, zt[:, 16 + hd, :], ALU.mult, after=(m, hg_ready))
        mix_ready.append(split_tile(o, (m,), h_hi[:, HEADS + hd, :], h_lo[:, HEADS + hd, :]))

    def tile_at(t, i, step, off):
        return t[:, bass.ds(i * step + off, 1), :].rearrange("p a s -> p (a s)")

    def evac_marks():
        return [Mark(s_evac[b], uses[b]) for b in range(4)]

    pe.wait(*mix_ready)
    with Loop(2) as i:
        for s2 in range(2):
            split_slab()
            tiles = products_fm()
            for t in range(2):
                tiles[t].wait(dve)
                xt = tile_at(xT, i, 4, 2 * s2 + t)
                read_last(tiles[t], V.tensor_tensor, xt, xt, tiles[t].ps[:, :], ALU.add)

    ready = norm_to_parts(xT, evac_marks(), "g_ffn", KT, h_hi, h_lo, D)
    hid_hi, hid_lo = slot("hid_hi", 0, FT, F32R), slot("hid_lo", FT, FT, F32R)
    pe.wait(ready)
    with Loop(FT // 2, act=2, dve=2) as i:
        for s2 in range(2):
            split_slab()
            tiles = products_fm()
            for t in range(2):
                a_t2, h_t = tmp[t][:, :], tmp[2 + t][:, :]
                if s2 == 0:
                    tiles[t].wait(act)
                    other = 2 * (1 - tiles[t].b // 2) + t
                    A.wait_ge(s_evac[other], at_round(uses[other], 1))
                    read_last(tiles[t], A.activation, a_t2, tiles[t].ps[:, :], ACT.Silu)
                    continue
                other = 2 * (1 - tiles[t].b // 2) + t
                V.wait_ge(s_evac[other], at_round(uses[other], 1))
                tiles[t].wait(dve)
                m = read_last(tiles[t], V.tensor_tensor, h_t, a_t2, tiles[t].ps[:, :], ALU.mult)
                am = act.do(A.activation, tile_at(hid_hi, i, 2, t), h_t, ACT.Copy, after=(m,))
                dve.do(V.tensor_tensor, tile_at(hid_lo, i, 2, t), h_t, tile_at(hid_hi, i, 2, t).bitcast(F32),
                       ALU.subtract, after=(am,))

    def down(hid_hi, hid_lo, more):
        for b in range(4):
            use_bank(b)
            claim(4 + b)

        def products(first_tile, start, stop, per=2):
            g, hi, lo = slab_parts(per)
            hv, lv = (w[:, :].rearrange("p (k c) -> p k c", k=2) for w in (hi, lo))
            for n in range(KT):
                for k in range(2):
                    last = three(bank[n][:, :], hv[:, k, n * P:(n + 1) * P], lv[:, k, n * P:(n + 1) * P],
                                 first_tile(hid_hi, k), first_tile(hid_lo, k), start and k == 0, stop and k == 1, True)
                if n % 4 == 3:
                    last.then_inc(s_tile, 1)
            return g

        split_slab()
        products(lambda t, k: t[:, k, :], True, False)
        rounds = FT // 4 - 1
        with Loop(rounds, bank_uses=0) as i:
            for s2 in range(2):
                split_slab()
                products(lambda t, k: tile_at(t, i, 4, 2 + 2 * s2 + k), False, False)
        for s2 in range(2):
            if more or s2 == 0:
                split_slab()
            g = products(lambda t, k: t[:, FT - 4 + 2 * s2 + k, :], False, s2 == 1)
        return [Mark(s_tile, 2 * g + 1 + n // 4) for n in range(KT)]

    pe.wait(act.now(), dve.now())
    done = down(hid_hi, hid_lo, True)
    x_ready = []
    for n in range(KT):
        if n < 4:
            V.wait_ge(done[n].sem, done[n].base)
            V.tensor_tensor(xT[:, n, :], xT[:, n, :], bank[n][:, :], ALU.add).then_inc(s_evac[n], 1)
            x_ready.append(Mark(s_evac[n], uses[n]))
        else:
            m = dve.do(V.tensor_tensor, xT[:, n, :], xT[:, n, :], bank[n][:, :], ALU.add, after=(done[n],))
            free[n] = (m,)
            x_ready.append(m)

    p_tm = slot("p_tm", 0, 2, shape=[P, TT, 2 * P])
    p_hi, p_lo = slot("p_hi", 2, 2, F32R), slot("p_lo", 4, 2, F32R)
    proj = slot("ple_proj", 8, KT)
    d_p = nc.alloc_semaphore("p_landed")
    G.wait_ge(s_tile, done[-1].base)
    dma(p_tm[:, :, :], p[0, 0].rearrange("(t q) c -> q t c", q=P), d_p)
    T.wait_ge(d_p, 16)
    p_parts = []
    for k in range(2):
        b = take()
        for t in range(TT):
            m = T.transpose(bank[b][:, t * P:(t + 1) * P], p_tm[:, t, k * P:(k + 1) * P], ident)
        m = pe.done(m)
        am = act.do(A.activation, p_hi[:, k, :], bank[b][:, :], ACT.Copy, after=(m,))
        e = dve.do(V.tensor_tensor, p_lo[:, k, :], bank[b][:, :], p_hi[:, k, :].bitcast(F32), ALU.subtract, after=(am,))
        free[b] = (e,)
        p_parts.append(e)
    split_slab()
    g, hi, lo = slab_parts()
    hv, lv = (w[:, :].rearrange("p (k c) -> p k c", k=2) for w in (hi, lo))
    pe.wait(*p_parts)
    proj_ready = []
    for n in range(KT):
        b = take((4, 5, 6, 7))
        for k in range(2):
            m = three(bank[b][:, :], hv[:, k, n * P:(n + 1) * P], lv[:, k, n * P:(n + 1) * P], p_hi[:, k, :],
                      p_lo[:, k, :], k == 0, k == 1)
        if n % 4 == 3:
            m.then_inc(s_tile, 1)
            m = Mark(s_tile, 2 * g + 1 + n // 4)
        else:
            m = pe.done(m)
        e = act.do(A.activation, proj[:, n, :], bank[b][:, :], ACT.Copy, after=(m,))
        free[b] = (e,)
        proj_ready.append(e)
    ready = norm_to_parts(xT, x_ready, "g_ple", KT, h_hi, h_lo, D)
    pe.wait(ready)
    dve.wait(proj_ready[-1])
    with Loop(2, dve=8) as i:
        for s2 in range(2):
            split_slab()
            tiles = products_fm()
            for t in range(2):
                gt = tmp[2 * s2 + t][:, :]
                tiles[t].wait(act)
                act.wait(dve.now().before())
                m = read_last(tiles[t], A.activation, gt, tiles[t].ps[:, :], ACT.Sigmoid)
                m = dve.do(V.tensor_tensor, gt, gt, tile_at(proj, i, 4, 2 * s2 + t), ALU.mult, after=(m,))
                xt = tile_at(xT, i, 4, 2 * s2 + t)
                m = dve.do(V.tensor_tensor, xt, xt, gt, ALU.add, after=(m,))
    x_ready = [dve.now()]
    qk, v_ret, gate = slot("ret_qk", 0, 8), slot("ret_v", 8, 8, shape=[P, TT, SGU_W]), slot("ret_gate", 16, 8)
    c2 = slot("const_mix2_sb", 24, 3)
    after_t, before_t, xif_t, xib_t = (c2[:, 0, k * P:(k + 1) * P] for k in range(4))
    cos2, sin2 = c2[:, 1, :], c2[:, 2, :]
    y_hi, y_lo = slot("y_hi", 28, 8, F32R), slot("y_lo", 36, 8, F32R)
    d_c2 = nc.alloc_semaphore("mix2_consts_landed")
    d_logit = nc.alloc_semaphore("decay_logits_landed")
    dma(c2[:, :, :], const_mix2.rearrange("p (k s) -> p k s", k=3), d_c2)
    logit, lg, e8, z8, zz8, q8, dec, zeta, neg8 = (dcol[:, 8 * k:8 * (k + 1)] for k in range(9))
    dma(logit, ret_decay_logit_2.rearrange("d h -> (d h)").partition_broadcast(P), d_logit)
    ready = norm_to_parts(xT, x_ready, "g_pre_mix_2", KT, h_hi, h_lo, D)

    def ago(q, k):
        return Mark(q.sem, q.count + k - q.step, q.i, q.step)

    pe.wait(ready)
    V.wait_ge(d_c2, 16)
    act.wait(dve.now())
    with Loop(2, act=8, dve=8) as i:
        for s2 in range(2):
            split_slab()
            tiles = products_fm()
            for t in range(2):
                n = 2 * s2 + t
                sw, dst, ps = tmp[n], tile_at(qk, i, 4, n), tiles[t].ps
                tiles[t].wait(act)
                act.do(A.activation, sw[0:64, :], ps[64:128, :], ACT.Copy, after=(ago(dve, 2),))
                am = act.do(A.activation, sw[64:128, :], ps[0:64, :], ACT.Copy)
                dve.wait(am)
                m1 = read_last(tiles[t], V.tensor_tensor, dst, ps[:, :], cos2, ALU.mult)
                m2 = dve.do(V.tensor_tensor, sw[:, :], sw[:, :], sin2, ALU.mult)
                dve.do(V.tensor_tensor, dst, dst, sw[:, :], ALU.add, after=(m1, m2))
    qk_ready = dve.now()

    V.wait_ge(d_logit, 16)
    A.wait_ge(d_logit, 16)
    m = act.do(A.activation, e8, logit, ACT.Abs)
    m = act.do(A.activation, e8, e8, ACT.Exp, scale=-1.0, after=(m,))
    m = dve.do(V.tensor_scalar, z8, e8, 2.0, None, ALU.add, after=(m,))
    m = dve.do(V.reciprocal, z8, z8, after=(m,))
    m = dve.do(V.tensor_tensor, z8, z8, e8, ALU.mult, after=(m,))
    m = dve.do(V.tensor_tensor, zz8, z8, z8, ALU.mult, after=(m,))
    m = dve.do(V.tensor_scalar, q8, zz8, 1 / 17, None, ALU.mult, after=(m,))
    for n in range(15, 1, -2):
        m = dve.do(V.scalar_tensor_tensor, q8, q8, 1 / n, zz8, ALU.add, ALU.mult, after=(m,))
    m = dve.do(V.scalar_tensor_tensor, q8, q8, 1.0, z8, ALU.add, ALU.mult, after=(m,))
    m0 = dve.do(V.tensor_scalar, neg8, logit, 0.0, None, ALU.min)
    lg_ready = dve.do(V.scalar_tensor_tensor, lg, q8, -2.0, neg8, ALU.mult, ALU.add, after=(m, m0))

    dmat, xi_f, xi_b = slot("ret_dmat", 27, 1), slot("ret_xi_f", 25, 1), slot("ret_xi_b", 26, 1)
    K_SCALE = RDK ** -0.5
    for hd in range(HEADS):
        hc = slice(hd * P, (hd + 1) * P)
        m = dve.do(V.tensor_scalar, dmat[:, 0, hc], after_t, lg[:, hd:hd + 1], None, ALU.mult, after=(lg_ready,))
        m = dve.do(V.scalar_tensor_tensor, dmat[:, 0, hc], before_t, lg[:, 4 + hd:5 + hd], dmat[:, 0, hc], ALU.mult,
                   ALU.add, after=(m,))
        act.do(A.activation, xi_f[:, 0, hc], xif_t, ACT.Exp, scale=lg[:, hd:hd + 1], after=(lg_ready, qk_ready))
        me = act.do(A.activation, xi_b[:, 0, hc], xib_t, ACT.Exp, scale=lg[:, 4 + hd:5 + hd])
    mz0 = dve.do(V.tensor_scalar, zeta[:, 0:4], lg[:, 0:4], ccol[:, 6:7], None, ALU.mult)
    mz1 = dve.do(V.tensor_scalar, zeta[:, 4:8], lg[:, 4:8], ccol[:, 7:8], None, ALU.mult)
    act.do(A.activation, dmat[:, 0, :], dmat[:, 0, :], ACT.Exp, after=(m,))
    act.do(A.activation, zeta, zeta, ACT.Exp, after=(mz0, mz1))
    me = act.do(A.activation, dec, lg, ACT.Exp, scale=float(P))
    for t in (dmat, xi_f, xi_b):
        tables = dve.do(V.tensor_scalar, t[:, 0, :], t[:, 0, :], K_SCALE, None, ALU.mult, after=(me,))

    w_sp = slot("w_spatial_raw", 24, 1)[:, 0, :].rearrange("p (g q) -> p g q", g=GRP)
    d_sp = nc.alloc_semaphore("spatial_landed")
    G.wait_ge(tables.sem, tables.base)
    dma(w_sp, w_spatial_2.rearrange("g p q -> p g q"), d_sp)

    with Loop(2) as i:
        for s2 in range(2):
            split_slab()
            tiles = products_tm()
            for t in range(2):
                dst = v_ret[:, 2 * t:2 * t + 2, bass.ds(i * (2 * CW) + s2 * CW, CW)]
                src = tiles[t].ps[:, :].rearrange("p (u c) -> p u c", u=2)
                tiles[t].wait((act, dve)[t])
                if t == 0:
                    read_last(tiles[t], A.activation, dst, src, ACT.Copy)
                else:
                    read_last(tiles[t], V.tensor_copy, dst, src)
    v_ready = evac_marks()
    with Loop(2) as i:
        for s2 in range(2):
            split_slab()
            tiles = products_fm()
            for t in range(2):
                tiles[t].wait(act)
                read_last(tiles[t], A.activation, tile_at(gate, i, 4, 2 * s2 + t), tiles[t].ps[:, :], ACT.Silu)
    gate_ready = evac_marks()

    RC = TT
    r_f, r_b = (slot(n, at, 2, shape=[P, TT, RDV]) for n, at in (("ret_state_f", 34), ("ret_state_b", 42)))
    ln_stats, ln_mv, ln_rs = sb("ln_stats", [P, 8, 6]), sb("ln_mean_var", [P, 8, 2]), sb("ln_rstd", [P, 8])
    kf, kb = tmp[0][:, :], tmp[1][:, :]
    kv_read, out_done, pair_t, s_t, st_ready, ln_ready, o_read, y_parts = None, {}, {}, {}, {}, {}, {}, []

    def per_chunk(t):
        return t.rearrange("p (j c) -> p j c", j=RC)

    def table(t, hd):
        return t[:, 0, hd * P:(hd + 1) * P].unsqueeze(1).broadcast_to([P, RC, P])

    def ret_prepare(hd):
        q, k = qk[:, hd, :], qk[:, HEADS + hd, :]
        chunk = [slice(j * P, (j + 1) * P) for j in range(RC)]
        claim(0)
        pe.wait(qk_ready)
        for j in range(RC):
            T.matmul(bank[0][:, chunk[j]], k[:, chunk[j]], q[:, chunk[j]], start=j == 0, stop=True,
                     skip_group_check=True)
        claim(1)
        for j in range(RC):
            m = T.transpose(bank[1][:, chunk[j]], k[:, chunk[j]], ident)
        m = pe.done(m)
        m1 = act.do(A.activation, kf, bank[1][:, :], ACT.Identity, scale=zeta[:, hd:hd + 1], after=(m, kv_read))
        m2 = act.do(A.activation, kb, bank[1][:, :], ACT.Identity, scale=zeta[:, 4 + hd:5 + hd])
        free[1] = (m2,)
        sm = dve.do(V.tensor_tensor, per_chunk(k), per_chunk(bank[0][:, :]), table(dmat, hd), ALU.mult,
                    after=(m, tables))
        free[0] = (sm,)
        xf = tmp[2 + hd % 2][:, :]
        m = dve.do(V.tensor_tensor, per_chunk(xf), per_chunk(q), table(xi_f, hd), ALU.mult, after=(out_done.get(hd - 2),))
        xm = dve.do(V.tensor_tensor, per_chunk(q), per_chunk(q), table(xi_b, hd), ALU.mult, after=(m,))
        s_t[hd] = (sm, xm)
        for b in (2, 3, 4):
            claim(b)
        pe.wait(m1, m2, *v_ready)
        vc = slice(hd * RDV, (hd + 1) * RDV)
        for n, (src, j) in enumerate(((kf, 0), (kf, 1), (kf, 2), (kb, 3), (kb, 2), (kb, 1))):
            m = T.matmul(bank[2 + n // 2][:, (n % 2) * RDV:(n % 2 + 1) * RDV], src[:, chunk[j]], v_ret[:, j, vc],
                         start=n % 2 == 0, stop=True, skip_group_check=True)
        pair_t[hd] = pe.done(m)
        return pair_t[hd]

    def ret_states(hd):
        for d, r in ((0, r_f), (1, r_b)):
            for j in range(RC - 1):
                n = 3 * d + j
                kv = bank[2 + n // 2][:, (n % 2) * RDV:(n % 2 + 1) * RDV]
                if j == 0:
                    m = dve.do(V.tensor_copy, r[:, 0, :], kv, after=(pair_t[hd], out_done.get(hd - 1)))
                else:
                    m = dve.do(V.scalar_tensor_tensor, r[:, j, :], r[:, j - 1, :], dec[:, 4 * d + hd:4 * d + hd + 1],
                               kv, ALU.mult, ALU.add, after=(m,))
        st_ready[hd] = m
        free[2] = free[3] = free[4] = (m,)

    def ret_outputs(hd):
        claim(5)
        claim(6)
        pe.wait(*s_t[hd], st_ready[hd])
        vc = slice(hd * RDV, (hd + 1) * RDV)
        for j in range(RC):
            c = slice(j * P, (j + 1) * P)
            terms = [(qk[:, HEADS + hd, c], v_ret[:, j, vc])]
            if j > 0:
                terms.append((tmp[2 + hd % 2][:, c], r_f[:, j - 1, :]))
            if j < RC - 1:
                terms.append((qk[:, hd, c], r_b[:, RC - 2 - j, :]))
            o = bank[5 + j // 2][:, (j % 2) * RDV:(j % 2 + 1) * RDV]
            for n, (a, b) in enumerate(terms):
                m = T.matmul(o, a, b, start=n == 0, stop=n == len(terms) - 1)
        out_done[hd] = pe.done(m)

    def ret_layernorm(hd):
        base = 4 * (hd % 2)
        for j in range(RC):
            o = bank[5 + j // 2][:, (j % 2) * RDV:(j % 2 + 1) * RDV]
            m = dve.do(V.bn_stats, ln_stats[:, base + j, :], o, after=(out_done[hd],))
            mm = dve.do(V.bn_aggr, ln_mv[:, base + j, :], ln_stats[:, base + j, :], after=(m,))
        rs = ln_rs[:, base:base + 4]
        m = act.do(A.activation, rs, ln_mv[:, base:base + 4, 1:2].rearrange("p j a -> p (j a)"), ACT.Sqrt, bias=eps_col,
                   scale=1.0, after=(mm,))
        m = dve.do(V.reciprocal, rs, rs, after=(m,))
        for j in range(RC):
            o = bank[5 + j // 2][:, (j % 2) * RDV:(j % 2 + 1) * RDV]
            dst = tmp[4 + 2 * (hd % 2) + j // 2][:, (j % 2) * RDV:(j % 2 + 1) * RDV]
            mm = dve.do(V.tensor_scalar, dst, o, ln_mv[:, base + j, 0:1], rs[:, j:j + 1], ALU.subtract, ALU.mult,
                        after=(m, o_read.get(hd - 2)))
        free[5] = free[6] = (mm,)
        ln_ready[hd] = mm

    def ret_gated(hd):
        pe.wait(ln_ready[hd])
        for e in range(2):
            claim(7)
            for j in range(RC):
                src = tmp[4 + 2 * (hd % 2) + j // 2][:, (j % 2) * RDV + e * P:(j % 2) * RDV + (e + 1) * P]
                m = T.transpose(bank[7][:, j * P:(j + 1) * P], src, ident)
            m = o_read[hd] = pe.done(m)
            n = 2 * hd + e
            m = dve.do(V.tensor_tensor, gate[:, n, :], gate[:, n, :], bank[7][:, :], ALU.mult, after=(m, *gate_ready))
            free[7] = (m,)
            y_parts.append(split_tile(gate[:, n, :], (m,), y_hi[:, n, :], y_lo[:, n, :]))

    for step in range(HEADS + 2):
        if step < HEADS:
            kv_read = ret_prepare(step)
        if 1 <= step <= HEADS:
            ret_outputs(step - 1)
        if step < HEADS:
            ret_states(step)
        if 1 <= step <= HEADS:
            ret_layernorm(step - 1)
        if step >= 2:
            ret_gated(step - 2)

    bs_b = slot("b_spatial_rows", 26, 1)
    d_bs = nc.alloc_semaphore("b_spatial_landed")
    G.wait_ge(dve.sem, dve.count)
    dma(bs_b[:, 0, :], b_spatial_2.rearrange("g p -> (g p)").partition_broadcast(P), d_bs)
    with Loop(2) as i:
        for s2 in range(2):
            split_slab()
            tiles = products_tm()
            for t in range(2):
                dst = v_ret[:, 2 * t:2 * t + 2, bass.ds(i * (2 * CW) + s2 * CW, CW)]
                src = tiles[t].ps[:, :].rearrange("p (u c) -> p u c", u=2)
                tiles[t].wait(act)
                read_last(tiles[t], A.activation, dst, src, ACT.Gelu_apprx_tanh)
    sv_ready = evac_marks()
    for t in range(TT):
        for j in range(2):
            m = dve.do(V.bn_stats, ln_stats[:, 2 * t + j, :], v_ret[:, t, j * S:(j + 1) * S], after=sv_ready)
        m = dve.do(V.bn_aggr, ln_mv[:, t, :], ln_stats[:, 2 * t:2 * t + 2, :], after=(m,))
    m = act.do(A.activation, ln_rs[:, 0:TT], ln_mv[:, 0:TT, 1:2].rearrange("p j a -> p (j a)"), ACT.Sqrt, bias=eps_col,
               scale=1.0, after=(m,))
    m = dve.do(V.reciprocal, ln_rs[:, 0:TT], ln_rs[:, 0:TT], after=(m,))
    for t in range(TT):
        xhat_ready = dve.do(V.tensor_scalar, v_ret[:, t, :], v_ret[:, t, :], ln_mv[:, t, 0:1], ln_rs[:, t:t + 1],
                            ALU.subtract, ALU.mult, after=(m,))

    merged = slot("merged", 0, 8)

    def gated_branch(add):
        ops = 2 if add else 1
        act.wait(dve.now())
        with Loop(4, dve=2 * ops) as i:
            split_slab()
            tiles = products_fm(y_hi, y_lo)
            for t in range(2):
                tiles[t].wait(act)
                act.wait(ago(dve, ops * (t + 1)))
                read_last(tiles[t], A.activation, tmp[2 + t][:, :], tiles[t].ps[:, :], ACT.Copy)
            copied = [Mark(s_evac[x.b], uses[x.b], i, 1) for x in tiles]
            split_slab()
            tiles = products_fm()
            for t in range(2):
                tiles[t].wait(act)
                act.wait(ago(dve, ops))
                am = read_last(tiles[t], A.activation, tmp[4 + t][:, :], tiles[t].ps[:, :], ACT.Sigmoid)
                dst = tile_at(merged, i, 2, t)
                if add:
                    m = dve.do(V.tensor_tensor, tmp[4 + t][:, :], tmp[4 + t][:, :], tmp[2 + t][:, :], ALU.mult,
                               after=(copied[t], am))
                    dve.do(V.tensor_tensor, dst, dst, tmp[4 + t][:, :], ALU.add, after=(m,))
                else:
                    dve.do(V.tensor_tensor, dst, tmp[4 + t][:, :], tmp[2 + t][:, :], ALU.mult, after=(copied[t], am))

    pe.wait(*y_parts)
    gated_branch(False)

    w_t, w_rows, mixed = slot("w_spatial_t", 25, 1)[:, 0, :], slot("w_spatial_rowsums", 27, 1)[:, 0, :], slot("mixed", 16, 8)
    T.wait_ge(d_sp, 16)
    V.wait_ge(d_bs, 16)
    b = take()
    for g in range(GRP):
        m = T.transpose(bank[b][:, g * P:(g + 1) * P], w_sp[:, g, :], ident)
    wt_ready = dve.do(V.tensor_copy, w_t, bank[b][:, :], after=(pe.done(m),))
    free[b] = (wt_ready,)
    b = take()
    m = pe.do(T.matmul, bank[b][:, :], ones, w_t, start=True, stop=True, after=(wt_ready,))
    rows_ready = dve.do(V.tensor_copy, w_rows, bank[b][:, :], after=(m,))
    free[b] = (rows_ready,)
    pe.wait(xhat_ready)
    mix_read = {}
    for c in range(KT):
        b = take()
        grp = slice(P * (c // 2), P * (c // 2 + 1))
        for j in range(RC):
            m = T.matmul(bank[b][:, j * P:(j + 1) * P], v_ret[:, j, c * P:(c + 1) * P], w_t[:, grp],
                         start=j == 0, stop=True, skip_group_check=True)
        m = pe.done(m)
        off = tmp[c % 2][:, 0:P]
        m1 = dve.do(V.scalar_tensor_tensor, off, w_rows[:, grp], col("sgu_ln_b_2", c), bs_b[:, 0, grp], ALU.mult, ALU.add,
                    after=(rows_ready, mix_read.get(c - 2)))
        mix_read[c] = dve.do(V.scalar_tensor_tensor, per_chunk(mixed[:, c, :]), per_chunk(bank[b][:, :]),
                             col("sgu_ln_g_2", c), off.unsqueeze(1).broadcast_to([P, RC, P]), ALU.mult, ALU.add,
                             after=(m, m1))
        free[b] = (mix_read[c],)

    act.wait(dve.now())
    with Loop(2, act=4, dve=8) as i:
        for s2 in range(2):
            split_slab()
            tiles = products_fm()
            for t in range(2):
                n = 2 * s2 + t
                w = tmp[n][:, :]
                tiles[t].wait(act)
                act.wait(ago(dve, 2))
                am = read_last(tiles[t], A.activation, w, tiles[t].ps[:, :], ACT.Gelu_apprx_tanh)
                m = dve.do(V.tensor_tensor, w, w, tile_at(mixed, i, 4, n), ALU.mult, after=(am,))
                am = act.do(A.activation, tile_at(y_hi, i, 4, n), w, ACT.Copy, after=(m,))
                dve.do(V.tensor_tensor, tile_at(y_lo, i, 4, n), w, tile_at(y_hi, i, 4, n).bitcast(F32), ALU.subtract,
                       after=(am,))
    pe.wait(dve.now())
    gated_branch(True)

    ready = dve.now()
    for k in range(KT):
        m = split_tile(merged[:, k, :], (ready,), h_hi[:, k, :], h_lo[:, k, :])
    pe.wait(m)
    o2 = slot("mixed_out", 8, 8)
    with Loop(2) as i:
        for s2 in range(2):
            split_slab()
            tiles = products_fm()
            for t in range(2):
                dst = tile_at(o2, i, 4, 2 * s2 + t)
                tiles[t].wait((act, dve)[t])
                if t == 0:
                    read_last(tiles[t], A.activation, dst, tiles[t].ps[:, :], ACT.Copy)
                else:
                    read_last(tiles[t], V.tensor_copy, dst, tiles[t].ps[:, :])

    def add_normed(src, ready, gname):
        b = take()
        read = {}
        for k in range(KT):
            t = tmp[k % 2]
            m = act.do(A.activation, t[:, :], src[:, k, :], ACT.Square, after=(*ready, read.get(k - 2)))
            read[k] = sum_rows(bank[b][:, 0:TT], t[:, :], (m,), k == 0, k == KT - 1, k == 0)
        r, m = rstd_cols(rcol[:, 0:TT], bank[b][:, 0:TT], D, (read[KT - 1],))
        free[b] = (m,)
        b = take()
        r = spread(b, rcol[:, 0:TT], tmp[2], (r,))
        made, added = [], {}
        for k in range(KT):
            t = tmp[3 + k % 2]
            m = dve.do(V.scalar_tensor_tensor, t[:, :], src[:, k, :], col(gname, k), bank[b][:, :], ALU.mult, ALU.mult,
                       after=(r, added.get(k - 2)))
            added[k] = dve.do(V.tensor_tensor, xT[:, k, :], xT[:, k, :], t[:, :], ALU.add, after=(m,))
            made.append(added[k])
        free[b] = (m,)
        return made

    x_ready = add_normed(o2, evac_marks(), "g_post_mix_2")

    ready = norm_to_parts(xT, (x_ready[-1],), "g_pre_ffn_2", KT, h_hi, h_lo, D)
    pe.wait(ready)
    hid_hi, hid_lo = slot("hid2_hi", 0, FT, F32R), slot("hid2_lo", FT, FT, F32R)

    def col_at(name, i, off):
        return cols[:, bass.ds(i * 2 + ROWS[name] + off, 1)]

    act.wait(dve.now())
    with Loop(FT // 2, act=8, dve=8) as i:
        for s2 in range(2):
            split_slab()
            tiles = products_fm()
            for t in range(2):
                f = FT * s2 + t
                acc, ps = tmp[2 * s2 + t][:, :], tiles[t].ps
                tiles[t].wait(act)
                am = act.do(A.activation, acc, ps[:, :], ACT.Identity, scale=col_at("conv_w1", i, f),
                            bias=col_at("conv_b_2", i, f), after=(ago(dve, 2 if s2 else 6),))
                m = dve.do(V.scalar_tensor_tensor, acc[:, 1:S], ps[:, 0:S - 1], col_at("conv_w0", i, f), acc[:, 1:S],
                           ALU.mult, ALU.add, after=(am,))
                dve.wait(m)
                m = read_last(tiles[t], V.scalar_tensor_tensor, acc[:, 0:S - 1], ps[:, 1:S], col_at("conv_w2", i, f),
                              acc[:, 0:S - 1], ALU.mult, ALU.add)
                if s2 == 0:
                    g_m = act.do(A.activation, acc, acc, ACT.Gelu_apprx_tanh, after=(m,))
                    continue
                h_t = tmp[4 + t][:, :]
                m = dve.do(V.tensor_tensor, h_t, tmp[t][:, :], acc, ALU.mult, after=(m, g_m))
                am = act.do(A.activation, tile_at(hid_hi, i, 2, t), h_t, ACT.Copy, after=(m,))
                dve.do(V.tensor_tensor, tile_at(hid_lo, i, 2, t), h_t, tile_at(hid_hi, i, 2, t).bitcast(F32),
                       ALU.subtract, after=(am,))

    pe.wait(act.now(), dve.now())
    done = down(hid_hi, hid_lo, False)
    o3 = slot("mlp_out", 0, KT)
    o3_ready = []
    for n in range(KT):
        if n < 4:
            act.wait(done[n], done[-1])
            A.activation(o3[:, n, :], bank[n][:, :], ACT.Copy).then_inc(s_evac[n], 1)
            o3_ready.append(Mark(s_evac[n], uses[n]))
        else:
            m = dve.do(V.tensor_copy, o3[:, n, :], bank[n][:, :], after=(done[-1],))
            free[n] = (m,)
            o3_ready.append(m)
    x_ready = add_normed(o3, o3_ready, "g_post_ffn_2")

    out_tm = slot("out_tm", 8, 8)
    stored = nc.alloc_semaphore("out_stored")
    pe.wait(*x_ready)
    for n in range(2 * TT):
        t, half = n // 2, n % 2
        b = take()
        for k in range(4):
            m = T.transpose(bank[b][:, k * P:(k + 1) * P], xT[:, 4 * half + k, t * P:(t + 1) * P], ident)
        m = pe.done(m)
        if half:
            m = act.do(A.activation, out_tm[:, n, :], bank[b][:, :], ACT.Copy, after=(m,))
        else:
            m = dve.do(V.tensor_copy, out_tm[:, n, :], bank[b][:, :], after=(m,))
        free[b] = (m,)
        SP.wait_ge(m.sem, m.base)
        SP.dma_start(out[0, t * P:(t + 1) * P, half * 4 * P:(half + 1) * 4 * P], out_tm[:, n, :]).then_inc(stored, 16)
    SP.wait_ge(stored, 16 * 2 * TT)


_INS = ["x", "p", "positions", "g_mix", "w_in", "g_qa", "g_kva", "w_qb", "w_kvb", "g_qn", "g_kn", "lb_param",
        "g_hgo", "w_o", "g_ffn", "w_gate", "w_up", "w_down", "g_ple", "w_ple_gate", "w_ple_proj", "g_pre_mix_2",
        "w_in_2", "ret_decay_logit_2", "sgu_ln_g_2", "sgu_ln_b_2", "w_spatial_2", "b_spatial_2", "w_ret_o_2",
        "w_sgu_o_2", "w_out_2", "g_post_mix_2", "g_pre_ffn_2", "w_up_2", "conv_w_2", "conv_b_2", "w_down_2",
        "g_post_ffn_2"]


def kernel(**inputs):
    import concourse.bacc as bacc
    from concourse.bass_utils import run_bass_kernel_spmd

    nc = bacc.Bacc("TRN2", target_bir_lowering=False, num_devices=1)
    arrays = {n: np.ascontiguousarray(inputs[n]) for n in _INS}
    arrays.update(const_tables())
    args = {n: nc.dram_tensor(f"in_{n}", a.shape, mybir.dt.from_np(a.dtype), kind="ExternalInput").ap()
            for n, a in arrays.items()}
    out = nc.dram_tensor("out", (1, S, D), F32, kind="ExternalOutput").ap()
    program(nc, **args, out=out)
    r = run_bass_kernel_spmd(nc, [{f"in_{n}": a for n, a in arrays.items()}], core_ids=[0])
    return r.results[0]["out"]
```

```python
import numpy as np

import concourse.bass as bass
from concourse import mybir

F32, F32R, I32 = mybir.dt.float32, mybir.dt.float32r, mybir.dt.int32
ALU, ACT, AX = mybir.AluOpType, mybir.ActivationFunctionType, mybir.AxisListType

COMPUTE = (mybir.EngineType.PE, mybir.EngineType.Activation, mybir.EngineType.DVE)
SP_ONLY = (mybir.EngineType.SP,)

P = 128
S = 512
D = 1024
KT = D // P
TT = S // P
EPS = 1e-6
HEADS = 4
NOPE, ROPE, VH = 128, 64, 128
QK = NOPE + ROPE
LORA = 256
HG_CHUNK = 64
NCH = S // HG_CHUNK
F1 = 2816
FT = F1 // P
SLAB = 2048
CW = SLAB // KT
RDK, RDV = 128, 256
SGU_W, GRP = 1024, 4
F2T = 2 * F1 // P

ROWS = {}
_at = 0
for _n, _k in (("g_mix", 8), ("g_qa", 2), ("g_kva", 2), ("g_qn", 1), ("g_kn", 1), ("g_hgo", 4), ("lb_param", 16),
               ("g_ffn", 8), ("g_ple", 8), ("g_pre_mix_2", 8), ("g_post_mix_2", 8), ("g_pre_ffn_2", 8),
               ("g_post_ffn_2", 8), ("conv_b_2", F2T)):
    ROWS[_n] = _at
    _at += _k
assert _at <= P
ROWS["conv_w0"], ROWS["conv_w1"], ROWS["g_qn_rope"], ROWS["g_kn_rope"] = P, P + F2T, P + 2 * F2T, P + 2 * F2T + 1
ROWS["conv_w2"], ROWS["sgu_ln_g_2"], ROWS["sgu_ln_b_2"] = 2 * P, 2 * P + F2T, 2 * P + F2T + 8


def const_tables():
    i = np.arange(P)
    ident = np.eye(P)
    ones = np.ones((P, P))
    inv = (10000.0 ** (-np.arange(0, ROPE, 2) / ROPE))
    cols = np.zeros((P, 12))
    cols[:, 0] = EPS
    cols[:, 1] = np.pi / 2
    cols[:, 2] = inv[i % 32]
    cols[:, 3] = np.where(i % 64 < 32, -1.0, 1.0)
    cols[:, 4] = 1.0
    cols[:, 5] = RDK ** -0.5
    cols[:, 6] = 127 - i
    cols[:, 7] = i
    cols[:, 8] = i < 64
    cols[:, 9] = i >= 64
    small = np.concatenate([ident, ones, cols], 1)
    perm = np.zeros((P, P))
    perm[i ^ 32, i] = 1.0
    s, t = i[:, None], i[None, :]
    same = s // HG_CHUNK == t // HG_CHUNK
    maskf = same & (s <= t)
    maskb = same & (s >= t)
    reset = np.ones((P, S))
    reset[:, ::HG_CHUNK] = 0.0
    mix1 = np.concatenate([perm, maskf, maskb, reset], 1)
    m, n = i[:, None], i[None, :]
    after = np.maximum(n - m, 0)
    before = np.maximum(m - n, 0)
    xif = np.broadcast_to(n + 1, (P, P))
    xib = np.broadcast_to(P - n, (P, P))
    half = RDK // 2
    freq = (1.0 / (10000.0 ** (np.arange(half) / half))).astype(np.float32)
    ang = (np.arange(S, dtype=np.float32)[None, :] * freq[i % half][:, None]).astype(np.float32).astype(np.float64)
    cos, sin = np.cos(ang), np.sin(ang) * np.where(i < half, -1.0, 1.0)[:, None]
    mix2 = np.concatenate([after, before, xif, xib, cos, sin], 1)
    return {k: np.ascontiguousarray(v, dtype=np.float32)
            for k, v in (("const_small", small), ("const_mix1", mix1), ("const_mix2", mix2))}


class Mark:

    def __init__(self, sem, base, i=None, step=0):
        self.sem, self.base, self.i, self.step = sem, base, i, step

    def value(self):
        return self.base if self.i is None else self.i * self.step + self.base

    def before(self):
        return Mark(self.sem, self.base - self.step, self.i, self.step)

    def last(self, rounds):
        return Mark(self.sem, self.base + (rounds - 1) * self.step)


class Queue:

    def __init__(self, nc, engine, name):
        self.nc, self.e, self.sem, self.count, self.i, self.step = nc, engine, nc.alloc_semaphore(name), 0, None, 0
        self.seen = {}

    def wait(self, *marks):
        for m in marks:
            if m is None:
                continue
            key = (m.sem.name, m.i is None)
            if self.seen.get(key, -1) >= m.base:
                continue
            self.seen[key] = m.base
            self.e.wait_ge(m.sem, m.value())

    def done(self, ins):
        ins.then_inc(self.sem, 1)
        self.count += 1
        return Mark(self.sem, self.count, self.i, self.step)

    def do(self, fn, *args, after=(), **kw):
        self.wait(*after)
        return self.done(fn(*args, **kw))

    def now(self):
        return Mark(self.sem, self.count, self.i, self.step)


def program(nc, x, p, positions, g_mix, w_in, g_qa, g_kva, w_qb, w_kvb, g_qn, g_kn, lb_param, g_hgo, w_o,
            g_ffn, w_gate, w_up, w_down, g_ple, w_ple_gate, w_ple_proj, g_pre_mix_2, w_in_2,
            ret_decay_logit_2, sgu_ln_g_2, sgu_ln_b_2, w_spatial_2, b_spatial_2, w_ret_o_2, w_sgu_o_2,
            w_out_2, g_post_mix_2, g_pre_ffn_2, w_up_2, conv_w_2, conv_b_2, w_down_2, g_post_ffn_2,
            const_small, const_mix1, const_mix2, out):
    pe, act, dve = Queue(nc, nc.tensor, "pe_done"), Queue(nc, nc.scalar, "act_done"), Queue(nc, nc.vector, "dve_done")
    pool = Queue(nc, nc.gpsimd, "pool_done")
    T, A, V, G, SP = nc.tensor, nc.scalar, nc.vector, nc.gpsimd, nc.sync
    queues = (pe, act, dve, pool)
    w_in, w_qb, w_kvb, w_o, w_gate, w_up, w_down, w_ple_gate, w_ple_proj = (
        w[0] for w in (w_in, w_qb, w_kvb, w_o, w_gate, w_up, w_down, w_ple_gate, w_ple_proj))

    limit = []
    top = [(nc.sbuf_base + 63) // 64 * 64]

    def sb(name, shape, dt=F32, at=None):
        size = int(np.prod(shape[1:])) * 4
        if at is None:
            at = top[0]
            top[0] += (size + 31) // 32 * 32
            assert not limit or top[0] <= limit[0]
        return nc.alloc_sbuf_tensor_at(name, shape, dtype=dt, offset=at)

    xT = sb("residual", [P, KT, S])
    raw = [sb(f"slab_raw{j}", [P, SLAB]) for j in range(2)]
    w_hi = [sb(f"slab_hi{j}", [P, SLAB], F32R) for j in range(2)]
    w_lo = [sb(f"slab_lo{j}", [P, SLAB], F32R) for j in range(2)]
    h_base = top[0]
    h_hi = sb("h_hi", [P, KT, S], F32R)
    h_lo = sb("h_lo", [P, KT, S], F32R)
    cs = sb("const_small_sb", [P, 2 * P + 12])
    ident, ones, ccol = cs[:, 0:P], cs[:, P:2 * P], cs[:, 2 * P:]
    eps_col, halfpi_col, freq_col, sign_col = (ccol[:, k:k + 1] for k in range(4))
    cols = sb("param_cols", [P, 3 * P])
    dcol = sb("decay_cols", [P, 8 * 10])
    rcol = sb("rstd_cols", [P, 32])
    xcol = sb("x_rstd_cols", [P, TT])
    xrow = sb("x_rstd_rows", [P, S])
    NT = 8
    tmp = [sb(f"tmp{j}", [P, S]) for j in range(NT)]
    tmp_end = top[0]
    arena = top[0] + 2048
    limit.append(arena)
    BLK = S * 4
    assert arena + 44 * BLK <= nc.sbuf_usable_end, (arena, nc.sbuf_usable_end)

    def slot(name, first, n, dt=F32, shape=None):
        assert first + n <= 44
        return sb(name, shape or [P, n, S], dt, at=arena + first * BLK)

    def col(name, k=0):
        c = ROWS[name] + k
        return cols[:, c:c + 1]

    bank = [nc.alloc_psum_tensor(f"bank{b}", [P, S], F32) for b in range(8)]
    free = [()] * 8
    turn = [0]

    def take(banks=(4, 5, 6, 7)):
        b = banks[turn[0] % len(banks)]
        turn[0] += 1
        claim(b)
        return b

    def claim(b):
        pe.wait(*free[b])
        if b < 4 and uses[b]:
            pe.wait(Mark(s_evac[b], uses[b]))

    landed = [nc.alloc_semaphore(f"slab_landed{j}") for j in range(2)]
    s_hi = nc.alloc_semaphore("slab_hi_done")
    s_lo = nc.alloc_semaphore("slab_lo_done")
    s_tile = nc.alloc_semaphore("slab_products")
    s_evac = [nc.alloc_semaphore(f"bank_read{b}") for b in range(4)]
    landings, landing = [0, 0], {}
    stream = {"loaded": 0, "split": 0, "used": 0}
    uses = [0] * 4
    loop = {"i": None, "n": 1}

    def at_round(value, per_round):
        return value if loop["i"] is None else loop["i"] * per_round + value

    def load_slab(columns, *srcs, i=None, per_round=2):
        g = stream["loaded"]
        stream["loaded"] += 1
        rounds = 0 if i is None else i
        if g >= 2:
            SP.wait_ge(s_lo, rounds * per_round + g - 1)
        k = srcs[0].shape[1]
        dst = raw[g % 2][:, 0:k * columns].rearrange("p (k c) -> p k c", k=k)
        at = 0
        for src in srcs:
            n = int(np.prod(src.shape[2:]))
            SP.dma_start(dst[:, :, at:at + n] if len(srcs) > 1 else dst, src).then_inc(landed[g % 2], 16)
            landings[g % 2] += 16
            at += n
        landing[g] = landings[g % 2]

    def load_loop(rounds, *sources):
        first = stream["loaded"]
        with nc.Fori(0, rounds, engines=SP_ONLY) as i:
            for src in sources:
                load_slab(SLAB // src(i).shape[1], src(i), i=i, per_round=len(sources))
        assert len(sources) == 2
        for g in range(first, first + 2 * rounds):
            landing[g] = landing[first + (g - first) % 2] + 16 * ((g - first) // 2)
        for j in range(2):
            landings[j] += 16 * (rounds - 1)
        stream["loaded"] = first + 2 * rounds

    def split_slab(slabs_per_round=2):
        g = stream["split"]
        stream["split"] += 1
        A.wait_ge(landed[g % 2], at_round(landing[g], 8 * slabs_per_round))
        if g >= 2:
            A.wait_ge(s_tile, at_round(2 * (g - 1), 2 * slabs_per_round))
        A.activation(w_hi[g % 2][:, :], raw[g % 2][:, :], ACT.Copy).then_inc(s_hi, 1)
        V.wait_ge(s_hi, at_round(g + 1, slabs_per_round))
        V.tensor_tensor(w_lo[g % 2][:, :], raw[g % 2][:, :], w_hi[g % 2][:, :].bitcast(F32),
                        ALU.subtract).then_inc(s_lo, 1)

    def slab_parts(slabs_per_round=2):
        g = stream["used"]
        stream["used"] += 1
        T.wait_ge(s_lo, at_round(g + 1, slabs_per_round))
        return g, w_hi[g % 2], w_lo[g % 2]

    def three(psum, a_hi, a_lo, b_hi, b_lo, start, stop, skip=False):
        T.matmul(psum, a_hi, b_hi, start=start, stop=False, skip_group_check=skip)
        T.matmul(psum, a_hi, b_lo, start=False, stop=False, skip_group_check=skip)
        return T.matmul(psum, a_lo, b_hi, start=False, stop=stop, skip_group_check=skip)

    def use_bank(b):
        if loop["i"] is None:
            pe.wait(*free[b])
        if uses[b]:
            T.wait_ge(s_evac[b], at_round(uses[b], 1))
        uses[b] += 1

    class Product:

        def __init__(self, b, ready):
            self.b, self.ready, self.ps = b, ready, bank[b]

        def wait(self, *qs):
            for q in qs:
                q.e.wait_ge(s_tile, self.ready)

    def products_fm(src_hi=None, src_lo=None, per=2, ready=None):
        g, hi, lo = slab_parts(per)
        src_hi, src_lo = src_hi or h_hi, src_lo or h_lo
        hv, lv = (w[:, :].rearrange("p (k c) -> p k c", k=KT) for w in (hi, lo))
        banks = [2 * (g % 2) + t for t in range(2)]
        for b in banks:
            use_bank(b)

        def product(k, t):
            ins = three(bank[banks[t]][:, :], hv[:, k, t * P:(t + 1) * P], lv[:, k, t * P:(t + 1) * P],
                        src_hi[:, k, :], src_lo[:, k, :], k == 0, k == KT - 1)
            if k == KT - 1:
                ins.then_inc(s_tile, 1)

        if ready is None:
            for t in range(2):
                for k in range(KT):
                    product(k, t)
        else:
            for k in range(KT):
                pe.wait(ready[k])
                for t in range(2):
                    product(k, t)
        return [Product(banks[t], at_round(2 * g + t + 1, 2 * per)) for t in range(2)]

    def products_tm(per=2):
        g, hi, lo = slab_parts(per)
        hv, lv = (w[:, :].rearrange("p (k c) -> p k c", k=KT) for w in (hi, lo))
        tiles = []
        for t in range(2):
            b = 2 * (g % 2) + t
            use_bank(b)
            for u in range(2):
                tok = slice((2 * t + u) * P, (2 * t + u + 1) * P)
                for k in range(KT):
                    last = three(bank[b][:, u * CW:(u + 1) * CW], h_hi[:, k, tok], h_lo[:, k, tok],
                                 hv[:, k, :], lv[:, k, :], k == 0, k == KT - 1)
            last.then_inc(s_tile, 1)
            tiles.append(Product(b, at_round(2 * g + t + 1, 2 * per)))
        return tiles

    def read_last(prod, fn, *args, **kw):
        fn(*args, **kw).then_inc(s_evac[prod.b], 1)
        return Mark(s_evac[prod.b], uses[prod.b], loop["i"], 0 if loop["i"] is None else 1)

    class Loop:

        def __init__(self, n, slabs=2, bank_uses=1, **counts):
            self.n, self.slabs, self.bank_uses, self.counts = n, slabs, bank_uses, counts

        def __enter__(self):
            for b in range(4):
                pe.wait(*free[b])
            self.f = nc.Fori(0, self.n, engines=COMPUTE)
            i = self.f.__enter__()
            loop["i"] = i
            self.start = dict(stream)
            self.uses = list(uses)
            self.base = [q.count for q in queues]
            for q, k in zip(queues, ("pe", "act", "dve", "pool")):
                q.i, q.step = i, self.counts.get(k, 0)
                q.outer, q.seen = q.seen, {}
            return i

        def __exit__(self, *e):
            if e[0] is None:
                for k in ("split", "used"):
                    n = stream[k] - self.start[k]
                    assert n == self.slabs, (k, n)
                    stream[k] = self.start[k] + n * self.n
                for b in range(4):
                    assert uses[b] - self.uses[b] == self.bank_uses, (b, uses[b] - self.uses[b])
                    uses[b] = self.uses[b] + self.n * self.bank_uses
                said = {}
                for q, k, b0 in zip(queues, ("pe", "act", "dve", "pool"), self.base):
                    said[k] = q.count - b0
                wrong = {k: v for k, v in said.items() if v != self.counts.get(k, 0)}
                assert not wrong, said
                for q, b0 in zip(queues, self.base):
                    q.count = b0 + (q.count - b0) * self.n
                    q.i, q.step, q.seen = None, 0, q.outer
                loop["i"] = None
            return self.f.__exit__(*e)

    def dma(dst, src, sem, e=G):
        return e.dma_start(dst, src).then_inc(sem, 16)

    def weight_cols(w, c0, n=CW):
        return w[:, c0:c0 + n].rearrange("(k p) c -> p k c", p=P)

    def weight_cols_at(w, i, step, c0):
        return w[:, bass.ds(i * step + c0, CW)].rearrange("(k p) c -> p k c", p=P)

    def sum_rows(dst, sq, ready, first, last, clear, which=None):
        pe.wait(*ready)
        for t in range(TT):
            ins = T.matmul(dst[:, t:t + 1], sq[:, t * P:(t + 1) * P], which or ones[:, 0:1], start=clear and t == 0,
                           stop=last, skip_group_check=True)
        return pe.done(ins)

    def rstd_cols(dst, sums, n, ready):
        m = act.do(A.activation, dst, sums, ACT.Sqrt, bias=eps_col, scale=1.0 / n, after=ready)
        return dve.do(V.reciprocal, dst, dst, after=(m,)), m

    def spread(b, rcols, dtile, ready, busy=()):
        d = dtile[:, :].rearrange("p (t c) -> p t c", t=TT)
        m = dve.do(V.tensor_tensor, d, ident.unsqueeze(1).broadcast_to([P, TT, P]),
                   rcols.unsqueeze(2).broadcast_to([P, TT, P]), ALU.mult, after=(*ready, *busy))
        return pe.do(T.matmul, bank[b][:, :], ones, dtile[:, :], start=True, stop=True, after=(m,))

    class Norm:

        def __init__(self, ready, gname, busy=()):
            act.wait(*busy)
            self.parts = []
            for k in range(KT):
                m = act.do(A.activation, h_hi[:, k, :], xT[:, k, :], ACT.Identity, scale=col(gname, k),
                           after=(ready[k],))
                self.parts.append(dve.do(V.scalar_tensor_tensor, h_lo[:, k, :], xT[:, k, :], col(gname, k),
                                         h_hi[:, k, :].bitcast(F32), ALU.mult, ALU.subtract, after=(m,)))
            self.squares = [act.do(A.activation, tmp[k][:, :], xT[:, k, :], ACT.Square) for k in range(KT)]

        def rows(self):
            b = take()
            for k in range(KT):
                m = sum_rows(bank[b][:, 0:TT], tmp[k][:, :], (self.squares[k],), k == 0, k == KT - 1, k == 0)
            r, m = rstd_cols(xcol[:, :], bank[b][:, 0:TT], D, (m,))
            free[b] = (m,)
            b = take()
            m = spread(b, xcol[:, :], tmp[0], (r,))
            m = dve.do(V.tensor_copy, xrow[:, :], bank[b][:, :], after=(m,))
            free[b] = (m,)
            dve.wait(m)
            act.wait(m)

    def first_products(norm):
        tiles = products_fm(ready=norm.parts)
        norm.rows()
        return tiles

    def scaled(prod, dst, q=None):
        prod.wait(dve)
        return read_last(prod, V.tensor_tensor, dst, prod.ps[:, :], xrow[:, :], ALU.mult)

    def scaled_tm(prod, dst, tok, fn):
        prod.wait(act)
        src = prod.ps[:, :].rearrange("p (u c) -> p u c", u=2)
        A.activation(dst[:, 0, :], src[:, 0, :], fn, scale=xcol[:, tok:tok + 1])
        return read_last(prod, A.activation, dst[:, 1, :], src[:, 1, :], fn, scale=xcol[:, tok + 1:tok + 2])

    def rounds(n, body, norm=None, **counts):
        body(0, 0, norm)
        with Loop(n - 1, **counts) as i:
            body(i, 1, None)

    def ago(q, k):
        return None if q.i is None else Mark(q.sem, q.count + k - q.step, q.i, q.step)

    def tile_at(t, i, step, off):
        return t[:, bass.ds(i * step + off, 1), :].rearrange("p a s -> p (a s)")

    def evac_marks():
        return [Mark(s_evac[b], uses[b]) for b in range(4)]

    def split_tile(t_ap, ready, hi_ap, lo_ap, busy=()):
        am = act.do(A.activation, hi_ap, t_ap, ACT.Copy, after=(*ready, *busy))
        return dve.do(V.tensor_tensor, lo_ap, t_ap, hi_ap.bitcast(F32), ALU.subtract, after=(am,))

    d_const, d_rows, d_x = (nc.alloc_semaphore(n) for n in ("consts_landed", "rows_landed", "x_landed"))
    c1 = slot("const_mix1_sb", 43, 1, shape=[P, 3 * P + P])
    perm, maskf, maskb = c1[:, 0:P], c1[:, P:2 * P], c1[:, 2 * P:3 * P]
    x_tm = slot("x_tm", 0, 8, shape=[P, TT, D])
    rows = slot("param_rows", 8, 1, shape=[P, 3, P])
    rows_zero = dve.do(V.memset, rows[:, :, :], 0.0)
    dma(cs[:, :], const_small, d_const, SP)
    for t in range(TT):
        dma(x_tm[:, t, :], x[0, t * P:(t + 1) * P, :], d_x, SP)
    load_slab(CW, weight_cols(w_in, 0))
    G.wait_ge(dve.sem, rows_zero.base)
    n_rows = 0
    for name, ap in (("g_mix", g_mix), ("g_qa", g_qa), ("g_kva", g_kva), ("g_qn", g_qn[:, 0:NOPE]),
                     ("g_kn", g_kn[:, 0:NOPE]), ("g_ffn", g_ffn), ("g_ple", g_ple)):
        src = ap.rearrange("a (k c) -> (a k) c", c=P)
        r = ROWS[name]
        dma(rows[r:r + src.shape[0], 0, :], src, d_rows)
        n_rows += 16
    for name, src in (("g_hgo", g_hgo.rearrange("a h d -> (a h) d")),
                      ("lb_param", lb_param.rearrange("a d (h c) -> (a d h) c", c=P)),
                      *((n, ap.rearrange("(k c) -> k c", c=P)) for n, ap in (
                          ("g_pre_mix_2", g_pre_mix_2), ("g_post_mix_2", g_post_mix_2), ("g_pre_ffn_2", g_pre_ffn_2),
                          ("g_post_ffn_2", g_post_ffn_2), ("conv_b_2", conv_b_2)))):
        r = ROWS[name]
        dma(rows[r:r + src.shape[0], 0, :], src, d_rows)
        n_rows += 16
    for k in range(3):
        src = conv_w_2[k, :].rearrange("(k c) -> k c", c=P)
        r, blk = ROWS[f"conv_w{k}"] % P, ROWS[f"conv_w{k}"] // P
        dma(rows[r:r + F2T, blk, :], src, d_rows)
        n_rows += 16
    for name, ap in (("sgu_ln_g_2", sgu_ln_g_2), ("sgu_ln_b_2", sgu_ln_b_2)):
        r = ROWS[name] - 2 * P
        dma(rows[r:r + 8, 2, :], ap.rearrange("(k c) -> k c", c=P), d_rows)
        n_rows += 16
    for name, ap in (("g_qn_rope", g_qn), ("g_kn_rope", g_kn)):
        r = ROWS[name] - P
        for half in range(2):
            dma(rows[r:r + 1, 1, half * ROPE:(half + 1) * ROPE], ap[:, NOPE:QK], d_rows)
            n_rows += 16
    def cols_of(w, c0=0, step=2 * CW):
        return lambda i: weight_cols_at(w, i, step, c0)

    def rows_of(w, s0, per_round):
        return lambda i: w[bass.ds(i * (per_round * 2 * P) + s0 * 2 * P, 2 * P), :].rearrange("(k p) c -> p k c", p=P)

    load_slab(CW, weight_cols(w_in, LORA))
    load_slab(2 * ROPE, *[weight_cols(w_in, 2 * LORA, ROPE)] * 2)
    z0 = 2 * LORA + ROPE
    load_loop(3, cols_of(w_in, z0), cols_of(w_in, z0 + CW))
    load_slab(CW, weight_cols(w_in, z0 + 6 * CW))
    qb_cols = w_qb.rearrange("(k p) (h c) -> p k h c", p=P, c=QK)
    load_slab(HEADS * QK, *[qb_cols[:, :, hd, 0:NOPE] for hd in range(HEADS)],
              *[qb_cols[:, :, hd, NOPE:QK] for hd in range(HEADS)])
    load_slab(CW, weight_cols(w_in, z0 + 7 * CW))
    load_slab(HEADS * 2 * P, w_kvb.rearrange("(k p) c -> p k c", p=P))
    for n in range(2):
        load_slab(CW, weight_cols(w_in, z0 + (8 + n) * CW))
    load_loop(2, cols_of(w_o), cols_of(w_o, CW))
    load_loop(FT // 2, cols_of(w_gate, 0, CW), cols_of(w_up, 0, CW))
    load_slab(D, w_down[0:2 * P, :].rearrange("(k p) c -> p k c", p=P))
    load_loop(FT // 4, rows_of(w_down, 1, 2), rows_of(w_down, 2, 2))
    load_slab(D, w_ple_proj.rearrange("(k p) c -> p k c", p=P))
    load_loop(2, cols_of(w_ple_gate), cols_of(w_ple_gate, CW))
    load_loop(6, cols_of(w_in_2), cols_of(w_in_2, CW))
    load_loop(2, cols_of(w_in_2, 4 * D), cols_of(w_in_2, 4 * D + CW))
    load_loop(4, cols_of(w_ret_o_2, 0, CW), cols_of(w_in_2, 5 * D, CW))
    load_loop(2, cols_of(w_in_2, 3 * D), cols_of(w_in_2, 3 * D + CW))
    load_loop(4, cols_of(w_sgu_o_2, 0, CW), cols_of(w_in_2, 6 * D, CW))
    load_loop(2, cols_of(w_out_2), cols_of(w_out_2, CW))
    load_loop(FT // 2, cols_of(w_up_2, 0, CW), cols_of(w_up_2, F1, CW))
    load_slab(D, w_down_2[0:2 * P, :].rearrange("(k p) c -> p k c", p=P))
    load_loop(FT // 4, rows_of(w_down_2, 1, 2), rows_of(w_down_2, 2, 2))
    T.wait_ge(d_const, 16)
    A.wait_ge(d_const, 16)
    V.wait_ge(d_const, 16)
    T.wait_ge(d_x, 16 * TT)

    x_ready = []
    for k in range(KT):
        b = take((4, 5, 6, 7))
        for t in range(TT):
            m = T.transpose(bank[b][:, t * P:(t + 1) * P], x_tm[:, t, k * P:(k + 1) * P], ident)
        m = pe.done(m)
        if k % 2:
            e = dve.do(V.tensor_copy, xT[:, k, :], bank[b][:, :], after=(m,))
        else:
            e = act.do(A.activation, xT[:, k, :], bank[b][:, :], ACT.Copy, after=(m,))
        free[b] = (e,)
        x_ready.append(e)
    T.wait_ge(d_rows, n_rows)
    b = take()
    for blk in range(3):
        m = T.transpose(bank[b][:, blk * P:(blk + 1) * P], rows[:, blk, :], ident)
    cols_ready = dve.do(V.tensor_copy, cols[:, :], bank[b][:, 0:3 * P], after=(pe.done(m),))
    free[b] = (cols_ready,)
    split_slab()

    norm = Norm(x_ready, "g_mix", (cols_ready,))
    d_c1 = nc.alloc_semaphore("mix1_consts_landed")
    G.wait_ge(pe.sem, pe.count)
    dma(c1[:, 0:3 * P], const_mix1[:, 0:3 * P], d_c1)

    zt = slot("z", 0, 20)
    v_hg = zt[:, 12:16, :]
    c_raw = slot("c_raw", 20, 4)
    cq_hi, cq_lo, ckv_hi, ckv_lo = (slot(n, 32 + 2 * k, 2, F32R)
                                    for k, n in enumerate(("cq_hi", "cq_lo", "ckv_hi", "ckv_lo")))
    c_hi = [cq_hi[:, 0, :], cq_hi[:, 1, :], ckv_hi[:, 0, :], ckv_hi[:, 1, :]]
    c_lo = [cq_lo[:, 0, :], cq_lo[:, 1, :], ckv_lo[:, 0, :], ckv_lo[:, 1, :]]
    kr_raw = slot("kr_raw", 24, 1)
    c_ready = []
    for j in range(2):
        split_slab()
        tiles = products_fm() if j else first_products(norm)
        for t in range(2):
            c_ready.append(scaled(tiles[t], c_raw[:, 2 * j + t, :]))
    split_slab()
    g, hi, lo = slab_parts()
    hv, lv = (w[:, 0:KT * 2 * ROPE].rearrange("p (k c) -> p k c", k=KT) for w in (hi, lo))
    b = 2 * (g % 2)
    use_bank(b)
    use_bank(b + 1)
    for k in range(KT):
        last = three(bank[b][:, :], hv[:, k, :], lv[:, k, :], h_hi[:, k, :], h_lo[:, k, :], k == 0, k == KT - 1)
    last.then_inc(s_tile, 2)
    V.wait_ge(s_tile, 2 * g + 2)
    V.tensor_tensor(kr_raw[:, 0, :], bank[b][:, :], xrow[:, :], ALU.mult).then_inc(s_evac[b], 1)
    V.sem_inc(s_evac[b + 1], 1)

    b = take()
    read = {}
    for k in range(4):
        m = act.do(A.activation, tmp[k][:, :], c_raw[:, k, :], ACT.Square, after=(c_ready[k], dve.now()))
        read[k] = sum_rows(bank[b][:, TT * (k // 2):TT * (k // 2 + 1)], tmp[k][:, :], (m,), k % 2 == 0, k % 2 == 1,
                           k == 0)
    r, m = rstd_cols(rcol[:, 0:2 * TT], bank[b][:, 0:2 * TT], LORA, (read[3],))
    free[b] = (m,)
    c_parts = []
    for j, gname in enumerate(("g_qa", "g_kva")):
        b = take()
        rr = spread(b, rcol[:, TT * j:TT * (j + 1)], tmp[j], (r,))
        for k in range(2):
            kk = 2 * j + k
            hm = dve.do(V.scalar_tensor_tensor, tmp[4 + kk][:, :], c_raw[:, kk, :], col(gname, k), bank[b][:, :],
                        ALU.mult, ALU.mult, after=(rr,))
            c_parts.append(split_tile(tmp[4 + kk][:, :], (hm,), c_hi[kk], c_lo[kk]))
        free[b] = (hm,)

    lbc = sb("lower_bounds", [P, 4, 8])
    L0, L1 = (cols[:, ROWS["lb_param"] + 8 * k:ROWS["lb_param"] + 8 * (k + 1)] for k in range(2))
    lower, one_minus, e0, e1 = (lbc[:, k, :] for k in range(4))
    m = dve.do(V.tensor_tensor, lower, L0, L1, ALU.max, after=(cols_ready,))
    a0 = dve.do(V.tensor_tensor, e0, L0, lower, ALU.subtract, after=(m,))
    a1 = dve.do(V.tensor_tensor, e1, L1, lower, ALU.subtract, after=(m,))
    m0 = act.do(A.activation, e0, e0, ACT.Exp, after=(a0,))
    m1 = act.do(A.activation, e1, e1, ACT.Exp, after=(a1,))
    m = dve.do(V.tensor_tensor, e1, e0, e1, ALU.add, after=(m0, m1))
    m = dve.do(V.reciprocal, e1, e1, after=(m,))
    m = dve.do(V.tensor_tensor, lower, e0, e1, ALU.mult, after=(m,))
    low_ready = dve.do(V.tensor_scalar, one_minus, lower, -1.0, 1.0, ALU.mult, ALU.add, after=(m,))
    with Loop(3) as i:
        for s2 in range(2):
            split_slab()
            tiles = products_fm()
            for t in range(2):
                scaled(tiles[t], tile_at(zt, i, 4, 2 * s2 + t))
    z_ready = evac_marks()
    tiles = products_tm()
    q_nope, q_rope = slot("q_nope", 25, 4), slot("q_rope", 29, 2)
    k_nope, k_rope = slot("k_nope", 20, 4), slot("k_rope", 40, 2)
    v_mla = slot("v_mla", 32, 4)
    cos1, sin1 = slot("rope_cos", 42, 1)[:, 0, :], slot("rope_sin", 31, 1)[:, 0, :]

    pos_i = sb("pos_i", [P, S], I32, at=arena + 31 * BLK)
    d_pos = nc.alloc_semaphore("positions_landed")
    dma(pos_i[:, :], positions[0].partition_broadcast(P), d_pos)
    V.wait_ge(d_pos, 16)
    C1, C2 = 6.28125, float(np.float32(2 * np.pi - 6.28125) // 2.0 ** -23 * 2.0 ** -23)
    C3 = float(2 * np.pi - C1 - C2)
    MAGIC = 1.5 * 2.0 ** 23
    PI = 3.1415925
    m = dve.do(V.tensor_copy, tmp[0][:, :], pos_i[:, :], after=(c_parts[-1],))
    m = dve.do(V.tensor_scalar, tmp[0][:, :], tmp[0][:, :], freq_col, None, ALU.mult, after=(m,))
    m = dve.do(V.tensor_scalar, tmp[1][:, :], tmp[0][:, :], float(1 / (2 * np.pi)), MAGIC, ALU.mult, ALU.add, after=(m,))
    m = dve.do(V.tensor_scalar, tmp[1][:, :], tmp[1][:, :], MAGIC, None, ALU.subtract, after=(m,))
    for c in (C1, C2, C3):
        m = dve.do(V.scalar_tensor_tensor, tmp[0][:, :], tmp[1][:, :], -c, tmp[0][:, :], ALU.mult, ALU.add, after=(m,))
    m = dve.do(V.tensor_scalar, tmp[0][:, :], tmp[0][:, :], -PI, PI, ALU.max, ALU.min, after=(m,))
    m1 = act.do(A.activation, tmp[1][:, :], tmp[0][:, :], ACT.Abs, after=(m,))
    m1 = act.do(A.activation, cos1, tmp[1][:, :], ACT.Sin, bias=halfpi_col, scale=-1.0, after=(m1,))
    m2 = act.do(A.activation, tmp[1][:, :], tmp[0][:, :], ACT.Sin, after=(m1,))
    tables = dve.do(V.tensor_scalar, sin1, tmp[1][:, :], sign_col, None, ALU.mult, after=(m1, m2))
    V.wait_ge(d_c1, 16)
    T.wait_ge(d_c1, 16)

    def rotate(t, ready, gcol, tb, g_done=False):
        if gcol is not None:
            ready = (dve.do(V.tensor_scalar, t, t, gcol, None, ALU.mult, after=ready),)
        b = take((4, 5, 6))
        m = pe.do(T.matmul, bank[b][:, :], perm, t, start=True, stop=True, after=ready)
        sw = dve.do(V.tensor_tensor, tmp[tb][:, :], bank[b][:, :], sin1, ALU.mult, after=(m, tables))
        free[b] = (sw,)
        m = dve.do(V.tensor_tensor, t, t, cos1, ALU.mult, after=(m, sw))
        return dve.do(V.tensor_tensor, t, t, tmp[tb][:, :], ALU.add, after=(m, sw))

    def hi_out(tiles, s2):
        for t in range(2):
            scaled_tm(tiles[t], v_hg[:, 2 * t:2 * t + 2, s2 * CW:(s2 + 1) * CW], 2 * t, ACT.Identity)

    for k in range(HEADS):
        hq_ready = act.do(A.activation, zt[:, k, :], zt[:, k, :], ACT.Silu, after=z_ready)
    split_slab()
    hi_out(tiles, 0)

    claim(7)
    sums = bank[7]
    sq_read, to_sum = {}, []

    def squares(src, ready, jobs):
        n = len(to_sum)
        m = act.do(A.activation, tmp[n % 4][:, :], src, ACT.Square, after=(*ready, sq_read.get(n - 4)))
        to_sum.append((n, m, jobs))
        return m

    def sum_squares(upto):
        for n, m, jobs in to_sum[len(sq_read):upto]:
            for hd, rws, first, last in jobs:
                sq_read[n] = sum_rows(sums[:, TT * hd:TT * (hd + 1)], tmp[n % 4][:, :], (m,), first, last,
                                      n == 0 and hd == jobs[0][0], rws)

    lower_half, upper_half, all_rows = ccol[:, 8:9], ccol[:, 9:10], None
    kr_sq = squares(kr_raw[:, 0, :], z_ready + [m2], [(HEADS + hd, lower_half, True, False) for hd in range(HEADS)])
    KR = rotate(kr_raw[:, 0, :], (kr_sq, cols_ready, *z_ready), col("g_kn_rope"), 4)
    split_slab()

    g, hi, lo = slab_parts()
    hv, lv = (w[:, 0:2 * HEADS * QK].rearrange("p (k c) -> p k c", k=2) for w in (hi, lo))
    pe.wait(c_parts[1])
    q_ready = []
    for t in range(6):
        b = take((4, 5, 6))
        for k in range(2):
            m = three(bank[b][:, :], hv[:, k, t * P:(t + 1) * P], lv[:, k, t * P:(t + 1) * P],
                      c_hi[k], c_lo[k], k == 0, k == 1)
        if t in (2, 5):
            m.then_inc(s_tile, 1)
            m = Mark(s_tile, 2 * g + 1 + (t == 5))
        else:
            m = pe.done(m)
        dst = q_nope[:, t, :] if t < HEADS else q_rope[:, t - HEADS, :]
        e = dve.do(V.tensor_copy, dst, bank[b][:, :], after=(m,))
        jobs = ([(t, all_rows, True, False)] if t < HEADS else
                [(2 * (t - HEADS), lower_half, False, True), (2 * (t - HEADS) + 1, upper_half, False, True)])
        squares(dst, (e,), jobs)
        sum_squares(t)
        free[b] = (e,)
        q_ready.append(e)

    tiles = products_tm()
    f_ready = []
    for k in range(8):
        f = zt[:, 4 + k, :]
        m = act.do(A.activation, f, f, ACT.Sigmoid)
        f_ready.append(dve.do(V.tensor_scalar, f, f, one_minus[:, k:k + 1], lower[:, k:k + 1], ALU.mult, ALU.add,
                              after=(m, low_ready)))
    split_slab()
    hi_out(tiles, 1)

    split_slab()
    g, hi, lo = slab_parts()
    hv, lv = (w[:, :].rearrange("p (k h c) -> p k h c", k=2, h=HEADS) for w in (hi, lo))
    pe.wait(c_parts[3])
    k_ready, v_ready = [], []
    for t in range(HEADS):
        b = take((4, 5, 6))
        for k in range(2):
            m = three(bank[b][:, :], hv[:, k, t, 0:P], lv[:, k, t, 0:P], c_hi[2 + k], c_lo[2 + k],
                      k == 0, k == 1)
        m = pe.done(m)
        e = dve.do(V.tensor_copy, k_nope[:, t, :], bank[b][:, :], after=(m,))
        squares(k_nope[:, t, :], (e,), [(HEADS + t, all_rows, False, True)])
        sum_squares(len(to_sum) - 1)
        free[b] = (e,)
        k_ready.append(e)
    for t in range(TT):
        b = take((4, 5, 6))
        tok = slice(t * P, (t + 1) * P)
        for k in range(2):
            m = three(bank[b][:, :].rearrange("p (h c) -> p h c", h=HEADS), ckv_hi[:, k, tok], ckv_lo[:, k, tok],
                      hv[:, k, :, P:2 * P], lv[:, k, :, P:2 * P], k == 0, k == 1)
        if t in (1, 3):
            m.then_inc(s_tile, 1)
            m = Mark(s_tile, 2 * g + 1 + (t == 3))
        else:
            m = pe.done(m)
        if t == 0:
            sum_squares(len(to_sum))
            r_all, rm = rstd_cols(rcol[:, :], sums[:, 0:32], QK, (sq_read[len(to_sum) - 1],))
            free[7] = (rm,)
        e = act.do(A.activation, v_mla[:, t, :], bank[b][:, :], ACT.Copy, after=(m, Mark(s_tile, 2 * g)))
        free[b] = (e,)
        v_ready.append(e)

    dt_free, head_ready, row_bank = {}, {}, {}
    order = [n for hd in range(HEADS) for n in (hd, HEADS + hd)]

    def head_rows(at):
        n = order[at]
        b = row_bank[n] = 4 + at % 4
        claim(b)
        dt = tmp[at % 4]
        dt_free[n] = spread(b, rcol[:, TT * n:TT * (n + 1)], dt, (r_all, *((dt_free[order[at - 4]],) if at >= 4 else ())))

    def head_scaled(n):
        hd, is_k = n % HEADS, n >= HEADS
        half = slice(ROPE * (hd % 2), ROPE * (hd % 2 + 1))
        b, rr = row_bank[n], dt_free[n]
        t = (k_nope if is_k else q_nope)[:, hd, :]
        m1 = dve.do(V.scalar_tensor_tensor, t, t, col("g_kn" if is_k else "g_qn"), bank[b][:, :], ALU.mult, ALU.mult,
                    after=(rr, (k_ready if is_k else q_ready)[hd]))
        if is_k:
            m2 = dve.do(V.tensor_tensor, k_rope[half, hd // 2, :], kr_raw[half, 0, :], bank[b][half, :], ALU.mult,
                        after=(rr, KR))
        else:
            t = q_rope[half, hd // 2, :]
            m2 = dve.do(V.scalar_tensor_tensor, t, t, col("g_qn_rope")[half, :], bank[b][half, :], ALU.mult, ALU.mult,
                        after=(rr, q_ready[HEADS + hd // 2]))
        free[b] = (m1, m2)
        head_ready[n] = (m1, m2)

    def pair_rotated(pair):
        m = rotate(q_rope[:, pair, :], (head_ready[2 * pair][1], head_ready[2 * pair + 1][1]), None, 4 + pair)
        for hd in (2 * pair, 2 * pair + 1):
            head_ready[hd] = (head_ready[hd][0], m)

    tiles = products_fm()
    for at in range(4):
        head_rows(at)
    split_slab()
    hg_ready = [scaled(tiles[t], zt[:, 16 + t, :]) for t in range(2)]
    tiles = products_fm()
    h_read = Mark(s_tile, 2 * stream["used"])
    for at in range(4):
        head_scaled(order[at])
    pair_rotated(0)
    for at in range(4, 8):
        head_rows(at)
    split_slab()
    hg_ready += [scaled(tiles[t], zt[:, 18 + t, :]) for t in range(2)]
    z_all = evac_marks()
    for at in range(4, 8):
        head_scaled(order[at])
    pair_rotated(1)
    log_f = [sb(f"log_f{k}", [P, S], at=h_base + (4 + k + 4 * (k // 4)) * BLK)[:, :] for k in range(8)]
    lf_ready = [act.do(A.activation, log_f[k], zt[:, 4 + k, :], ACT.Ln, after=(f_ready[k], h_read)) for k in range(8)]
    reset = slot("reset", 24, 1)[:, 0, :]
    d_reset = nc.alloc_semaphore("reset_landed")
    G.wait_ge(dve.sem, dve.count)
    dma(reset, const_mix1[:, 3 * P:3 * P + S], d_reset)

    p_t = slot("weights_t", 36, 4)
    scale = QK ** -0.5
    mcol = sb("softmax_cols", [P, 2, 4])
    pv_done, exp_read, copied = None, {}, {}
    units = [(hd, j) for hd in range(HEADS) for j in range(TT)]
    score, attn_ready = {}, []

    def scores(u):
        hd, j = units[u]
        b = 4 + u % 2
        claim(b)
        qt = slice(j * P, (j + 1) * P)
        half = slice(ROPE * (hd % 2), ROPE * (hd % 2 + 1))
        pe.wait(*head_ready[hd], *head_ready[HEADS + hd])
        T.matmul(bank[b][:, :], q_nope[:, hd, qt], k_nope[:, hd, :], start=True, stop=False)
        m = pe.done(T.matmul(bank[b][:, :], q_rope[half, hd // 2, qt], k_rope[half, hd // 2, :], start=False, stop=True))
        c = mcol[:, u % 2, :]
        m = dve.do(V.reduce_max, c[:, 0:1], bank[b][:, :], AX.X, after=(m,))
        m = dve.do(V.tensor_scalar, c[:, 1:2], c[:, 0:1], -scale, None, ALU.mult, after=(m,))
        w = tmp[u % 2]
        m = act.do(A.activation, w[:, :], bank[b][:, :], ACT.Exp, bias=c[:, 1:2], scale=scale, accum_out=c[:, 2:3],
                   after=(m, exp_read.get(u - 2)))
        free[b] = (m,)
        m = dve.do(V.reciprocal, c[:, 3:4], c[:, 2:3], after=(m,))
        score[u] = dve.do(V.tensor_scalar, w[:, :], w[:, :], c[:, 3:4], None, ALU.mult, after=(m,))

    def transposed(u):
        hd, j = units[u]
        b = 0
        claim(b)
        pe.wait(score[u])
        for kb in range(TT):
            m = T.transpose(bank[b][:, kb * P:(kb + 1) * P], tmp[u % 2][:, kb * P:(kb + 1) * P], ident)
        m = exp_read[u] = pe.done(m)
        copied[u] = act.do(A.activation, p_t[:, :, j * P:(j + 1) * P],
                           bank[b][:, :].rearrange("p (k q) -> p k q", k=TT), ACT.Copy,
                           after=(m, pv_done, *((v_ready[-1],) if u == 0 else ())))
        free[b] = (copied[u],)

    def values(hd):
        b = 1
        claim(b)
        pe.wait(copied[TT * hd + TT - 1])
        for kb in range(TT):
            m = T.matmul(bank[b][:, :], v_mla[:, kb, hd * VH:(hd + 1) * VH], p_t[:, kb, :], start=kb == 0,
                         stop=kb == TT - 1)
        m = pe.done(m)
        am = act.do(A.activation, h_hi[:, hd, :], bank[b][:, :], ACT.Copy, after=(m,))
        e = dve.do(V.tensor_tensor, h_lo[:, hd, :], bank[b][:, :], h_hi[:, hd, :].bitcast(F32), ALU.subtract, after=(am,))
        free[b] = (e,)
        attn_ready.append(e)
        return m

    qi, ki, qb, kd = (tmp[k][:, :] for k in range(2, 6))
    a_t = slot("gla_scores", 31, 1)[:, 0, :]
    kd_t = slot("gla_keys_t", 42, 1)[:, 0, :].rearrange("p (j d) -> p j d", j=TT)
    st = sb("gla_states", [P, NCH, P], at=tmp_end - 2 * BLK)
    decs = sb("gla_decay", [P, NCH])
    out_read, o_ready = [head_ready[n][1] for n in range(8)] + [dt_free[n] for n in range(8)], {}
    V.wait_ge(d_reset, 16)
    stage = {}

    def chunks(t):
        return t.rearrange("p (c t) -> p c t", t=HG_CHUNK)

    def prepare(n):
        hd, back = n // 2, n % 2
        k = 4 * back + hd
        f, lf, q, bb = zt[:, 4 + k, :], log_f[k], zt[:, hd, :], qb
        mid, last = (HG_CHUNK // 2, 0) if back else (HG_CHUNK // 2 - 1, HG_CHUNK - 1)
        if back:
            m = dve.do(V.tensor_tensor_scan, bb[:, ::-1], reset, lf[:, ::-1], 0.0, ALU.mult, ALU.add,
                       after=(lf_ready[k], *out_read))
        else:
            m = dve.do(V.tensor_tensor_scan, bb, reset, lf, 0.0, ALU.mult, ALU.add, after=(lf_ready[k], *out_read))
        at = lambda x: chunks(bb)[:, :, x:x + 1].broadcast_to([P, NCH, HG_CHUNK])
        m_mid = dve.do(V.tensor_tensor, chunks(ki), chunks(bb), at(mid), ALU.subtract, after=(m,))
        m_last = dve.do(V.tensor_tensor, chunks(kd), at(last), chunks(bb), ALU.subtract, after=(m,))
        m_k = dve.do(V.tensor_scalar, lf, f, -1.0, 1.0, ALU.mult, ALU.add, after=(m,))
        e1 = act.do(A.activation, qi, ki, ACT.Exp, after=(m_mid,))
        e2 = act.do(A.activation, ki, ki, ACT.Exp, scale=-1.0, after=(e1,))
        e3 = act.do(A.activation, kd, kd, ACT.Exp, after=(m_last,))
        e5 = act.do(A.activation, decs[:, :], chunks(bb)[:, :, last:last + 1].rearrange("p c t -> p (c t)"), ACT.Exp,
                    after=(dec_read[0],))
        e4 = act.do(A.activation, qb, bb, ACT.Exp, after=(e5,))
        m1 = dve.do(V.tensor_tensor, qi, qi, q, ALU.mult, after=(e1, hq_ready))
        m2 = dve.do(V.tensor_tensor, ki, ki, lf, ALU.mult, after=(e2, m_k))
        m3 = dve.do(V.tensor_tensor, kd, kd, lf, ALU.mult, after=(e3,))
        m4 = dve.do(V.tensor_tensor, qb, qb, q, ALU.mult, after=(e4,))
        stage[n] = (m2, m3, m4, e5)

    def intra(n):
        m2, m3, m4, e5 = stage[n]
        claim(6)
        pe.wait(m2)
        for j in range(TT):
            sl = slice(j * P, (j + 1) * P)
            m = T.matmul(bank[6][:, sl], ki[:, sl], qi[:, sl], start=j == 0, stop=True, skip_group_check=True)
        m = pe.done(m)
        mask = maskb if n % 2 else maskf
        e = dve.do(V.tensor_tensor, a_t.rearrange("p (j t) -> p j t", j=TT),
                   bank[6][:, :].rearrange("p (j t) -> p j t", j=TT), mask.unsqueeze(1).broadcast_to([P, TT, P]),
                   ALU.mult, after=(m,))
        free[6] = (e,)
        claim(2)
        pe.wait(m3)
        for j in range(TT):
            m = T.transpose(bank[2][:, j * P:(j + 1) * P], kd[:, j * P:(j + 1) * P], ident)
        m = pe.done(m)
        e2 = act.do(A.activation, kd_t, bank[2][:, :].rearrange("p (j d) -> p j d", j=TT), ACT.Copy, after=(m,))
        free[2] = (e2,)
        stage[n] = (e, e2, m4, e5)

    def state(n):
        hd, back = n // 2, n % 2
        e, e2, m4, e5 = stage[n]
        cols_v = slice(hd * P, (hd + 1) * P)
        bs = (2, 3)
        for half in range(2):
            claim(bs[half])
        pe.wait(e2)
        order = list(range(NCH - 1, 0, -1)) if back else list(range(NCH - 1))
        for half in range(2):
            rws = slice(HG_CHUNK * half, HG_CHUNK * (half + 1))
            first = True
            for c in (c for c in range(NCH) if c % 2 == half and c in order):
                j = c // 2
                m = T.matmul(bank[bs[half]][:, j * P:(j + 1) * P], kd_t[rws, j, :], v_hg[rws, j, cols_v],
                             start=first, stop=True, skip_group_check=True)
                first = False
        m = pe.done(m)
        prev = None
        for c in order:
            to = c - 1 if back else c + 1
            kv = bank[bs[c % 2]][:, (c // 2) * P:(c // 2 + 1) * P]
            if prev is None:
                prev = dve.do(V.tensor_copy, st[:, to, :], kv, after=(m,))
            else:
                prev = dve.do(V.scalar_tensor_tensor, st[:, to, :], st[:, c, :], decs[:, c:c + 1], kv,
                              ALU.mult, ALU.add, after=(prev, e5))
        free[2] = free[3] = (prev,)
        dec_read[0] = prev
        stage[n] = (e, m4, prev)

    def outputs(n):
        hd, back = n // 2, n % 2
        e, m4, s_m = stage[n]
        if not back:
            claim(7)
        pe.wait(e, m4, s_m)
        cols_v = slice(hd * P, (hd + 1) * P)
        for j in range(TT):
            sl = slice(j * P, (j + 1) * P)
            m = T.matmul(bank[7][:, sl], v_hg[:, j, cols_v], a_t[:, sl], start=not back and j == 0, stop=False,
                         skip_group_check=True)
        for c in range(NCH):
            if c == (NCH - 1 if back else 0):
                continue
            sl = slice(c * HG_CHUNK, (c + 1) * HG_CHUNK)
            m = T.matmul(bank[7][:, sl], st[:, c, :], qb[:, sl], start=False, stop=True, skip_group_check=True)
        out_read[:] = [pe.done(m)]
        if back:
            o = zt[:, 4 + hd, :]
            o_ready[hd] = dve.do(V.tensor_copy, o, bank[7][:, :], after=(out_read[0],))
            free[7] = (o_ready[hd],)

    pe.wait(*z_all)
    dec_read = [None]
    for n in range(2 * HEADS):
        prepare(n)
        scores(2 * n)
        intra(n)
        if n:
            transposed(2 * n - 1)
            if n % 2 == 0:
                pv_done = values(n // 2 - 1)
        state(n)
        scores(2 * n + 1)
        transposed(2 * n)
        outputs(n)
    transposed(2 * n + 1)
    values(HEADS - 1)
    for k in range(HEADS):
        hg_done = act.do(A.activation, zt[:, 16 + k, :], zt[:, 16 + k, :], ACT.Silu, after=hg_ready)

    b = take((4, 5))
    read = {}
    for hd in range(HEADS):
        t = tmp[hd % 2]
        m = act.do(A.activation, t[:, :], zt[:, 4 + hd, :], ACT.Square, after=(o_ready[hd], read.get(hd - 2), attn_ready[-1]))
        read[hd] = sum_rows(bank[b][:, TT * hd:TT * (hd + 1)], t[:, :], (m,), True, True, hd == 0)
    r, m = rstd_cols(rcol[:, 0:4 * TT], bank[b][:, 0:4 * TT], P, (read[3],))
    free[b] = (m,)
    mix_ready = list(attn_ready)
    for hd in range(HEADS):
        b = take((4, 5))
        rr = spread(b, rcol[:, TT * hd:TT * (hd + 1)], tmp[2 + hd % 2], (r, *((dt_free[hd - 2],) if hd >= 2 else ())))
        dt_free[hd] = rr
        o = zt[:, 4 + hd, :]
        m = dve.do(V.scalar_tensor_tensor, o, o, col("g_hgo", hd), bank[b][:, :], ALU.mult, ALU.mult, after=(rr, read[hd]))
        free[b] = (m,)
        m = dve.do(V.tensor_tensor, o, o, zt[:, 16 + hd, :], ALU.mult, after=(m, hg_done))
        mix_ready.append(split_tile(o, (m,), h_hi[:, HEADS + hd, :], h_lo[:, HEADS + hd, :]))

    pe.wait(*mix_ready)
    x_marks = []
    with Loop(2) as i:
        for s2 in range(2):
            split_slab()
            tiles = products_fm()
            for t in range(2):
                tiles[t].wait(dve)
                xt = tile_at(xT, i, 4, 2 * s2 + t)
                x_marks.append(read_last(tiles[t], V.tensor_tensor, xt, xt, tiles[t].ps[:, :], ALU.add))
    x_marks = [Mark(m.sem, m.base + r * m.step) for r in range(2) for m in x_marks]

    norm = Norm(x_marks, "g_ffn", (Mark(s_tile, 2 * stream["used"]), dve.now()))
    hid_hi, hid_lo = slot("hid_hi", 0, FT, F32R), slot("hid_lo", FT, FT, F32R)

    def swiglu(i, r0, norm):
        for s2 in range(2):
            split_slab()
            tiles = first_products(norm) if norm and s2 == 0 else products_fm()
            for t in range(2):
                if s2 == 0:
                    dve.wait(ago(dve, 4))
                    m = scaled(tiles[t], tmp[t][:, :])
                    gate_m = act.do(A.activation, tmp[t][:, :], tmp[t][:, :], ACT.Silu, after=(m,))
                    continue
                h_t = tmp[2 + t][:, :]
                tiles[t].wait(dve)
                dve.wait(gate_m)
                m = read_last(tiles[t], V.tensor_tensor, h_t, tmp[t][:, :], tiles[t].ps[:, :], ALU.mult)
                m = dve.do(V.tensor_tensor, h_t, h_t, xrow[:, :], ALU.mult, after=(m,))
                am = act.do(A.activation, tile_at(hid_hi, i, 2, 2 * r0 + t), h_t, ACT.Copy, after=(m,))
                hh = tile_at(hid_hi, i, 2, 2 * r0 + t).bitcast(F32)
                dve.do(V.tensor_tensor, tile_at(hid_lo, i, 2, 2 * r0 + t), h_t, hh, ALU.subtract, after=(am,))

    rounds(FT // 2, swiglu, norm, act=4, dve=4)

    def down(hid_hi, hid_lo, more):
        for b in range(4):
            use_bank(b)
            claim(4 + b)

        def products(first_tile, start, stop, per=2):
            g, hi, lo = slab_parts(per)
            hv, lv = (w[:, :].rearrange("p (k c) -> p k c", k=2) for w in (hi, lo))
            for n in range(KT):
                for k in range(2):
                    last = three(bank[n][:, :], hv[:, k, n * P:(n + 1) * P], lv[:, k, n * P:(n + 1) * P],
                                 first_tile(hid_hi, k), first_tile(hid_lo, k), start and k == 0, stop and k == 1, True)
                if n % 4 == 3:
                    last.then_inc(s_tile, 1)
            return g

        split_slab()
        products(lambda t, k: t[:, k, :], True, False)
        rounds = FT // 4 - 1
        with Loop(rounds, bank_uses=0) as i:
            for s2 in range(2):
                split_slab()
                products(lambda t, k: tile_at(t, i, 4, 2 + 2 * s2 + k), False, False)
        for s2 in range(2):
            if more or s2 == 0:
                split_slab()
            g = products(lambda t, k: t[:, FT - 4 + 2 * s2 + k, :], False, s2 == 1)
        return [Mark(s_tile, 2 * g + 1 + n // 4) for n in range(KT)]

    pe.wait(act.now(), dve.now())
    done = down(hid_hi, hid_lo, True)
    x_ready = []
    for n in range(KT):
        if n < 4:
            V.wait_ge(done[n].sem, done[n].base)
            V.tensor_tensor(xT[:, n, :], xT[:, n, :], bank[n][:, :], ALU.add).then_inc(s_evac[n], 1)
            x_ready.append(Mark(s_evac[n], uses[n]))
        else:
            m = dve.do(V.tensor_tensor, xT[:, n, :], xT[:, n, :], bank[n][:, :], ALU.add, after=(done[n],))
            free[n] = (m,)
            x_ready.append(m)

    p_tm = slot("p_tm", 0, 2, shape=[P, TT, 2 * P])
    p_hi, p_lo = slot("p_hi", 2, 2, F32R), slot("p_lo", 4, 2, F32R)
    proj = slot("ple_proj", 8, KT)
    d_p = nc.alloc_semaphore("p_landed")
    G.wait_ge(s_tile, done[-1].base)
    dma(p_tm[:, :, :], p[0, 0].rearrange("(t q) c -> q t c", q=P), d_p)
    T.wait_ge(d_p, 16)
    p_parts = []
    for k in range(2):
        b = take()
        for t in range(TT):
            m = T.transpose(bank[b][:, t * P:(t + 1) * P], p_tm[:, t, k * P:(k + 1) * P], ident)
        m = pe.done(m)
        am = act.do(A.activation, p_hi[:, k, :], bank[b][:, :], ACT.Copy, after=(m,))
        e = dve.do(V.tensor_tensor, p_lo[:, k, :], bank[b][:, :], p_hi[:, k, :].bitcast(F32), ALU.subtract, after=(am,))
        free[b] = (e,)
        p_parts.append(e)
    split_slab()
    g, hi, lo = slab_parts()
    hv, lv = (w[:, :].rearrange("p (k c) -> p k c", k=2) for w in (hi, lo))
    pe.wait(*p_parts)
    proj_ready = []
    for n in range(KT):
        b = take((4, 5, 6, 7))
        for k in range(2):
            m = three(bank[b][:, :], hv[:, k, n * P:(n + 1) * P], lv[:, k, n * P:(n + 1) * P], p_hi[:, k, :],
                      p_lo[:, k, :], k == 0, k == 1)
        if n % 4 == 3:
            m.then_inc(s_tile, 1)
            m = Mark(s_tile, 2 * g + 1 + n // 4)
        else:
            m = pe.done(m)
        e = act.do(A.activation, proj[:, n, :], bank[b][:, :], ACT.Copy, after=(m,))
        free[b] = (e,)
        proj_ready.append(e)
    norm = Norm(x_ready, "g_ple", (dve.now(),))
    dve.wait(proj_ready[-1])

    def gated_embedding(i, r0, norm):
        for s2 in range(2):
            split_slab()
            tiles = first_products(norm) if norm and s2 == 0 else products_fm()
            for t in range(2):
                n = 2 * s2 + t
                gt = tmp[n][:, :]
                dve.wait(ago(dve, 2))
                m = scaled(tiles[t], gt)
                m = act.do(A.activation, gt, gt, ACT.Sigmoid, after=(m,))
                m = dve.do(V.tensor_tensor, gt, gt, tile_at(proj, i, 4, 4 * r0 + n), ALU.mult, after=(m,))
                xt = tile_at(xT, i, 4, 4 * r0 + n)
                x_marks.append(dve.do(V.tensor_tensor, xt, xt, gt, ALU.add, after=(m,)))

    x_marks = []
    rounds(2, gated_embedding, norm, act=4, dve=8)

    qk, v_ret, gate = slot("ret_qk", 0, 8), slot("ret_v", 8, 8, shape=[P, TT, SGU_W]), slot("ret_gate", 16, 8)
    c2 = slot("const_mix2_sb", 24, 3)
    after_t, before_t, xif_t, xib_t = (c2[:, 0, k * P:(k + 1) * P] for k in range(4))
    cos2, sin2 = c2[:, 1, :], c2[:, 2, :]
    y_hi, y_lo = slot("y_hi", 28, 8, F32R), slot("y_lo", 36, 8, F32R)
    d_c2 = nc.alloc_semaphore("mix2_consts_landed")
    d_logit = nc.alloc_semaphore("decay_logits_landed")
    dma(c2[:, :, :], const_mix2.rearrange("p (k s) -> p k s", k=3), d_c2)
    logit, lg, e8, z8, zz8, q8, dec, zeta, neg8 = (dcol[:, 8 * k:8 * (k + 1)] for k in range(9))
    dma(logit, ret_decay_logit_2.rearrange("d h -> (d h)").partition_broadcast(P), d_logit)
    x_marks = [Mark(m.sem, m.base) for m in x_marks]
    norm = Norm(x_marks, "g_pre_mix_2", (Mark(s_tile, 2 * stream["used"]), dve.now()))

    V.wait_ge(d_c2, 16)

    def rotated(i, r0, norm):
        for s2 in range(2):
            split_slab()
            tiles = first_products(norm) if norm and s2 == 0 else products_fm()
            if norm and s2 == 0:
                dve.do(V.tensor_tensor, cos2, cos2, xrow[:, :], ALU.mult)
                dve.wait(dve.do(V.tensor_tensor, sin2, sin2, xrow[:, :], ALU.mult))
            for t in range(2):
                n = 2 * s2 + t
                sw, dst, ps = tmp[n], tile_at(qk, i, 4, 4 * r0 + n), tiles[t].ps
                tiles[t].wait(act)
                act.do(A.activation, sw[0:64, :], ps[64:128, :], ACT.Copy, after=(ago(dve, 2),))
                am = act.do(A.activation, sw[64:128, :], ps[0:64, :], ACT.Copy)
                dve.wait(am)
                m1 = read_last(tiles[t], V.tensor_tensor, dst, ps[:, :], cos2, ALU.mult)
                m2 = dve.do(V.tensor_tensor, sw[:, :], sw[:, :], sin2, ALU.mult)
                dve.do(V.tensor_tensor, dst, dst, sw[:, :], ALU.add, after=(m1, m2))

    rounds(2, rotated, norm, act=8, dve=8)
    qk_ready = dve.now()

    V.wait_ge(d_logit, 16)
    A.wait_ge(d_logit, 16)
    m = act.do(A.activation, e8, logit, ACT.Abs)
    m = act.do(A.activation, e8, e8, ACT.Exp, scale=-1.0, after=(m,))
    m = dve.do(V.tensor_scalar, z8, e8, 2.0, None, ALU.add, after=(m,))
    m = dve.do(V.reciprocal, z8, z8, after=(m,))
    m = dve.do(V.tensor_tensor, z8, z8, e8, ALU.mult, after=(m,))
    m = dve.do(V.tensor_tensor, zz8, z8, z8, ALU.mult, after=(m,))
    m = dve.do(V.tensor_scalar, q8, zz8, 1 / 17, None, ALU.mult, after=(m,))
    for n in range(15, 1, -2):
        m = dve.do(V.scalar_tensor_tensor, q8, q8, 1 / n, zz8, ALU.add, ALU.mult, after=(m,))
    m = dve.do(V.scalar_tensor_tensor, q8, q8, 1.0, z8, ALU.add, ALU.mult, after=(m,))
    m0 = dve.do(V.tensor_scalar, neg8, logit, 0.0, None, ALU.min)
    lg_ready = dve.do(V.scalar_tensor_tensor, lg, q8, -2.0, neg8, ALU.mult, ALU.add, after=(m, m0))

    dmat, xi_f, xi_b = slot("ret_dmat", 27, 1), slot("ret_xi_f", 25, 1), slot("ret_xi_b", 26, 1)
    K_SCALE = RDK ** -0.5
    for hd in range(HEADS):
        hc = slice(hd * P, (hd + 1) * P)
        m = dve.do(V.tensor_scalar, dmat[:, 0, hc], after_t, lg[:, hd:hd + 1], None, ALU.mult, after=(lg_ready,))
        m = dve.do(V.scalar_tensor_tensor, dmat[:, 0, hc], before_t, lg[:, 4 + hd:5 + hd], dmat[:, 0, hc], ALU.mult,
                   ALU.add, after=(m,))
        act.do(A.activation, xi_f[:, 0, hc], xif_t, ACT.Exp, scale=lg[:, hd:hd + 1], after=(lg_ready, qk_ready))
        me = act.do(A.activation, xi_b[:, 0, hc], xib_t, ACT.Exp, scale=lg[:, 4 + hd:5 + hd])
    mz0 = dve.do(V.tensor_scalar, zeta[:, 0:4], lg[:, 0:4], ccol[:, 6:7], None, ALU.mult)
    mz1 = dve.do(V.tensor_scalar, zeta[:, 4:8], lg[:, 4:8], ccol[:, 7:8], None, ALU.mult)
    act.do(A.activation, dmat[:, 0, :], dmat[:, 0, :], ACT.Exp, after=(m,))
    act.do(A.activation, zeta, zeta, ACT.Exp, after=(mz0, mz1))
    me = act.do(A.activation, dec, lg, ACT.Exp, scale=float(P))
    for t in (dmat, xi_f, xi_b):
        tables = dve.do(V.tensor_scalar, t[:, 0, :], t[:, 0, :], K_SCALE, None, ALU.mult, after=(me,))

    w_sp = slot("w_spatial_raw", 24, 1)[:, 0, :].rearrange("p (g q) -> p g q", g=GRP)
    d_sp = nc.alloc_semaphore("spatial_landed")
    G.wait_ge(tables.sem, tables.base)
    dma(w_sp, w_spatial_2.rearrange("g p q -> p g q"), d_sp)

    with Loop(2) as i:
        for s2 in range(2):
            split_slab()
            tiles = products_tm()
            for t in range(2):
                dst = v_ret[:, 2 * t:2 * t + 2, bass.ds(i * (2 * CW) + s2 * CW, CW)]
                scaled_tm(tiles[t], dst, 2 * t, ACT.Identity)
    v_ready = evac_marks()
    gate_ready = {}

    def gate_slab(j):
        split_slab()
        tiles = products_fm()
        for t in range(2):
            dst = gate[:, 2 * j + t, :]
            gate_ready[j] = act.do(A.activation, dst, dst, ACT.Silu, after=(scaled(tiles[t], dst),))

    RC = TT
    r_f, r_b = (slot(n, at, 2, shape=[P, TT, RDV]) for n, at in (("ret_state_f", 34), ("ret_state_b", 42)))
    ln_stats, ln_mv, ln_rs = sb("ln_stats", [P, 8, 6]), sb("ln_mean_var", [P, 8, 2]), sb("ln_rstd", [P, 8])
    kf, kb = tmp[0][:, :], tmp[1][:, :]
    kv_read, out_done, pair_t, s_t, st_ready, ln_ready, o_read, y_parts = None, {}, {}, {}, {}, {}, {}, []

    def per_chunk(t):
        return t.rearrange("p (j c) -> p j c", j=RC)

    def table(t, hd):
        return t[:, 0, hd * P:(hd + 1) * P].unsqueeze(1).broadcast_to([P, RC, P])

    def ret_prepare(hd):
        q, k = qk[:, hd, :], qk[:, HEADS + hd, :]
        chunk = [slice(j * P, (j + 1) * P) for j in range(RC)]
        claim(0)
        pe.wait(qk_ready)
        for j in range(RC):
            T.matmul(bank[0][:, chunk[j]], k[:, chunk[j]], q[:, chunk[j]], start=j == 0, stop=True,
                     skip_group_check=True)
        claim(1)
        for j in range(RC):
            m = T.transpose(bank[1][:, chunk[j]], k[:, chunk[j]], ident)
        m = pe.done(m)
        m1 = act.do(A.activation, kf, bank[1][:, :], ACT.Identity, scale=zeta[:, hd:hd + 1], after=(m, kv_read))
        m2 = act.do(A.activation, kb, bank[1][:, :], ACT.Identity, scale=zeta[:, 4 + hd:5 + hd])
        free[1] = (m2,)
        sm = dve.do(V.tensor_tensor, per_chunk(k), per_chunk(bank[0][:, :]), table(dmat, hd), ALU.mult,
                    after=(m, tables))
        free[0] = (sm,)
        xf = tmp[2 + hd % 2][:, :]
        m = dve.do(V.tensor_tensor, per_chunk(xf), per_chunk(q), table(xi_f, hd), ALU.mult, after=(out_done.get(hd - 2),))
        xm = dve.do(V.tensor_tensor, per_chunk(q), per_chunk(q), table(xi_b, hd), ALU.mult, after=(m,))
        s_t[hd] = (sm, xm)
        for b in (2, 3, 4):
            claim(b)
        pe.wait(m1, m2, *v_ready)
        vc = slice(hd * RDV, (hd + 1) * RDV)
        for n, (src, j) in enumerate(((kf, 0), (kf, 1), (kf, 2), (kb, 3), (kb, 2), (kb, 1))):
            m = T.matmul(bank[2 + n // 2][:, (n % 2) * RDV:(n % 2 + 1) * RDV], src[:, chunk[j]], v_ret[:, j, vc],
                         start=n % 2 == 0, stop=True, skip_group_check=True)
        pair_t[hd] = pe.done(m)
        return pair_t[hd]

    def ret_states(hd):
        for d, r in ((0, r_f), (1, r_b)):
            for j in range(RC - 1):
                n = 3 * d + j
                kv = bank[2 + n // 2][:, (n % 2) * RDV:(n % 2 + 1) * RDV]
                if j == 0:
                    m = dve.do(V.tensor_copy, r[:, 0, :], kv, after=(pair_t[hd], out_done.get(hd - 1)))
                else:
                    m = dve.do(V.scalar_tensor_tensor, r[:, j, :], r[:, j - 1, :], dec[:, 4 * d + hd:4 * d + hd + 1],
                               kv, ALU.mult, ALU.add, after=(m,))
        st_ready[hd] = m
        free[2] = free[3] = free[4] = (m,)

    def ret_outputs(hd):
        claim(5)
        claim(6)
        pe.wait(*s_t[hd], st_ready[hd])
        vc = slice(hd * RDV, (hd + 1) * RDV)
        for j in range(RC):
            c = slice(j * P, (j + 1) * P)
            terms = [(qk[:, HEADS + hd, c], v_ret[:, j, vc])]
            if j > 0:
                terms.append((tmp[2 + hd % 2][:, c], r_f[:, j - 1, :]))
            if j < RC - 1:
                terms.append((qk[:, hd, c], r_b[:, RC - 2 - j, :]))
            o = bank[5 + j // 2][:, (j % 2) * RDV:(j % 2 + 1) * RDV]
            for n, (a, b) in enumerate(terms):
                m = T.matmul(o, a, b, start=n == 0, stop=n == len(terms) - 1)
        out_done[hd] = pe.done(m)

    def ret_layernorm(hd):
        base = 4 * (hd % 2)
        for j in range(RC):
            o = bank[5 + j // 2][:, (j % 2) * RDV:(j % 2 + 1) * RDV]
            m = dve.do(V.bn_stats, ln_stats[:, base + j, :], o, after=(out_done[hd],))
            mm = dve.do(V.bn_aggr, ln_mv[:, base + j, :], ln_stats[:, base + j, :], after=(m,))
        rs = ln_rs[:, base:base + 4]
        m = act.do(A.activation, rs, ln_mv[:, base:base + 4, 1:2].rearrange("p j a -> p (j a)"), ACT.Sqrt, bias=eps_col,
                   scale=1.0, after=(mm,))
        m = dve.do(V.reciprocal, rs, rs, after=(m,))
        for j in range(RC):
            o = bank[5 + j // 2][:, (j % 2) * RDV:(j % 2 + 1) * RDV]
            dst = tmp[4 + 2 * (hd % 2) + j // 2][:, (j % 2) * RDV:(j % 2 + 1) * RDV]
            mm = dve.do(V.tensor_scalar, dst, o, ln_mv[:, base + j, 0:1], rs[:, j:j + 1], ALU.subtract, ALU.mult,
                        after=(m, o_read.get(hd - 2)))
        free[5] = free[6] = (mm,)
        ln_ready[hd] = mm

    def ret_gated(hd):
        pe.wait(ln_ready[hd])
        for e in range(2):
            claim(7)
            for j in range(RC):
                src = tmp[4 + 2 * (hd % 2) + j // 2][:, (j % 2) * RDV + e * P:(j % 2) * RDV + (e + 1) * P]
                m = T.transpose(bank[7][:, j * P:(j + 1) * P], src, ident)
            m = o_read[hd] = pe.done(m)
            n = 2 * hd + e
            m = dve.do(V.tensor_tensor, gate[:, n, :], gate[:, n, :], bank[7][:, :], ALU.mult, after=(m, gate_ready[hd]))
            free[7] = (m,)
            y_parts.append(split_tile(gate[:, n, :], (m,), y_hi[:, n, :], y_lo[:, n, :]))

    for step in range(HEADS + 2):
        if step < HEADS:
            kv_read = ret_prepare(step)
        if 1 <= step <= HEADS:
            ret_outputs(step - 1)
        if step < HEADS:
            ret_states(step)
            gate_slab(step)
        if 1 <= step <= HEADS:
            ret_layernorm(step - 1)
        if step >= 2:
            ret_gated(step - 2)

    bs_b = slot("b_spatial_rows", 26, 1)
    d_bs = nc.alloc_semaphore("b_spatial_landed")
    G.wait_ge(dve.sem, dve.count)
    dma(bs_b[:, 0, :], b_spatial_2.rearrange("g p -> (g p)").partition_broadcast(P), d_bs)
    with Loop(2) as i:
        for s2 in range(2):
            split_slab()
            tiles = products_tm()
            for t in range(2):
                dst = v_ret[:, 2 * t:2 * t + 2, bass.ds(i * (2 * CW) + s2 * CW, CW)]
                scaled_tm(tiles[t], dst, 2 * t, ACT.Gelu_apprx_tanh)
    sv_ready = evac_marks()
    for t in range(TT):
        for j in range(2):
            m = dve.do(V.bn_stats, ln_stats[:, 2 * t + j, :], v_ret[:, t, j * S:(j + 1) * S], after=sv_ready)
        m = dve.do(V.bn_aggr, ln_mv[:, t, :], ln_stats[:, 2 * t:2 * t + 2, :], after=(m,))
    m = act.do(A.activation, ln_rs[:, 0:TT], ln_mv[:, 0:TT, 1:2].rearrange("p j a -> p (j a)"), ACT.Sqrt, bias=eps_col,
               scale=1.0, after=(m,))
    m = dve.do(V.reciprocal, ln_rs[:, 0:TT], ln_rs[:, 0:TT], after=(m,))
    for t in range(TT):
        xhat_ready = dve.do(V.tensor_scalar, v_ret[:, t, :], v_ret[:, t, :], ln_mv[:, t, 0:1], ln_rs[:, t:t + 1],
                            ALU.subtract, ALU.mult, after=(m,))

    merged = slot("merged", 0, 8)

    def gated_branch(add):
        ops = 2 if add else 1
        act.wait(dve.now())
        with Loop(4, act=2, dve=2 * ops) as i:
            split_slab()
            tiles = products_fm(y_hi, y_lo)
            for t in range(2):
                tiles[t].wait(act)
                act.wait(ago(dve, ops * (t + 1)))
                read_last(tiles[t], A.activation, tmp[2 + t][:, :], tiles[t].ps[:, :], ACT.Copy)
            copied = [Mark(s_evac[x.b], uses[x.b], i, 1) for x in tiles]
            split_slab()
            tiles = products_fm()
            for t in range(2):
                dve.wait(ago(dve, ops))
                m = scaled(tiles[t], tmp[4 + t][:, :])
                am = act.do(A.activation, tmp[4 + t][:, :], tmp[4 + t][:, :], ACT.Sigmoid, after=(m,))
                dst = tile_at(merged, i, 2, t)
                if add:
                    m = dve.do(V.tensor_tensor, tmp[4 + t][:, :], tmp[4 + t][:, :], tmp[2 + t][:, :], ALU.mult,
                               after=(copied[t], am))
                    dve.do(V.tensor_tensor, dst, dst, tmp[4 + t][:, :], ALU.add, after=(m,))
                else:
                    dve.do(V.tensor_tensor, dst, tmp[4 + t][:, :], tmp[2 + t][:, :], ALU.mult, after=(copied[t], am))

    pe.wait(*y_parts)
    gated_branch(False)

    w_t, w_rows, mixed = slot("w_spatial_t", 25, 1)[:, 0, :], slot("w_spatial_rowsums", 27, 1)[:, 0, :], slot("mixed", 16, 8)
    T.wait_ge(d_sp, 16)
    V.wait_ge(d_bs, 16)
    b = take()
    for g in range(GRP):
        m = T.transpose(bank[b][:, g * P:(g + 1) * P], w_sp[:, g, :], ident)
    wt_ready = dve.do(V.tensor_copy, w_t, bank[b][:, :], after=(pe.done(m),))
    free[b] = (wt_ready,)
    b = take()
    m = pe.do(T.matmul, bank[b][:, :], ones, w_t, start=True, stop=True, after=(wt_ready,))
    rows_ready = dve.do(V.tensor_copy, w_rows, bank[b][:, :], after=(m,))
    free[b] = (rows_ready,)
    pe.wait(xhat_ready)
    mix_read = {}
    for c in range(KT):
        b = take()
        grp = slice(P * (c // 2), P * (c // 2 + 1))
        for j in range(RC):
            m = T.matmul(bank[b][:, j * P:(j + 1) * P], v_ret[:, j, c * P:(c + 1) * P], w_t[:, grp],
                         start=j == 0, stop=True, skip_group_check=True)
        m = pe.done(m)
        off = tmp[c % 2][:, 0:P]
        m1 = dve.do(V.scalar_tensor_tensor, off, w_rows[:, grp], col("sgu_ln_b_2", c), bs_b[:, 0, grp], ALU.mult, ALU.add,
                    after=(rows_ready, mix_read.get(c - 2)))
        mix_read[c] = dve.do(V.scalar_tensor_tensor, per_chunk(mixed[:, c, :]), per_chunk(bank[b][:, :]),
                             col("sgu_ln_g_2", c), off.unsqueeze(1).broadcast_to([P, RC, P]), ALU.mult, ALU.add,
                             after=(m, m1))
        free[b] = (mix_read[c],)

    act.wait(dve.now())
    with Loop(2, act=8, dve=8) as i:
        for s2 in range(2):
            split_slab()
            tiles = products_fm()
            for t in range(2):
                n = 2 * s2 + t
                w = tmp[n][:, :]
                dve.wait(ago(dve, 2))
                am = act.do(A.activation, w, w, ACT.Gelu_apprx_tanh, after=(scaled(tiles[t], w),))
                m = dve.do(V.tensor_tensor, w, w, tile_at(mixed, i, 4, n), ALU.mult, after=(am,))
                am = act.do(A.activation, tile_at(y_hi, i, 4, n), w, ACT.Copy, after=(m,))
                dve.do(V.tensor_tensor, tile_at(y_lo, i, 4, n), w, tile_at(y_hi, i, 4, n).bitcast(F32), ALU.subtract,
                       after=(am,))
    pe.wait(dve.now())
    gated_branch(True)

    ready = dve.now()
    for k in range(KT):
        m = split_tile(merged[:, k, :], (ready,), h_hi[:, k, :], h_lo[:, k, :])
    pe.wait(m)
    o2 = slot("mixed_out", 8, 8)
    o_marks = []
    with Loop(2) as i:
        for s2 in range(2):
            split_slab()
            tiles = products_fm()
            for t in range(2):
                dst = tile_at(o2, i, 4, 2 * s2 + t)
                tiles[t].wait((act, dve)[t])
                if t == 0:
                    m = read_last(tiles[t], A.activation, dst, tiles[t].ps[:, :], ACT.Copy)
                else:
                    m = read_last(tiles[t], V.tensor_copy, dst, tiles[t].ps[:, :])
                o_marks.append(m)
    o_marks = [Mark(m.sem, m.base + r * m.step) for r in range(2) for m in o_marks]

    def add_normed(src, ready, gname, busy=()):
        b = take()
        read = {}
        act.wait(*busy)
        for k in range(KT):
            t = tmp[k]
            m = act.do(A.activation, t[:, :], src[:, k, :], ACT.Square, after=(ready[k],))
            read[k] = sum_rows(bank[b][:, 0:TT], t[:, :], (m,), k == 0, k == KT - 1, k == 0)
        r, m = rstd_cols(rcol[:, 0:TT], bank[b][:, 0:TT], D, (read[KT - 1],))
        free[b] = (m,)
        b = take()
        r = spread(b, rcol[:, 0:TT], tmp[2], (r,))
        made, added = [], {}
        for k in range(KT):
            t = tmp[3 + k % 2]
            m = dve.do(V.scalar_tensor_tensor, t[:, :], src[:, k, :], col(gname, k), bank[b][:, :], ALU.mult, ALU.mult,
                       after=(r, added.get(k - 2)))
            added[k] = dve.do(V.tensor_tensor, xT[:, k, :], xT[:, k, :], t[:, :], ALU.add, after=(m,))
            made.append(added[k])
        free[b] = (m,)
        return made

    x_ready = add_normed(o2, o_marks, "g_post_mix_2", (dve.now(),))

    norm = Norm(x_ready, "g_pre_ffn_2", (Mark(s_tile, 2 * stream["used"]), ))
    act.wait(dve.now())
    hid_hi, hid_lo = slot("hid2_hi", 0, FT, F32R), slot("hid2_lo", FT, FT, F32R)

    def col_at(name, i, off):
        return cols[:, bass.ds(i * 2 + ROWS[name] + off, 1)]

    def conv_mlp(i, r0, norm):
        for s2 in range(2):
            split_slab()
            tiles = first_products(norm) if norm and s2 == 0 else products_fm()
            acc = [tmp[2 * s2 + t][:, :] for t in range(2)]
            hid = [tmp[4 + t][:, :] for t in range(2)]
            f = [FT * s2 + t + 2 * r0 for t in range(2)]
            m = [scaled(tiles[t], hid[t]) for t in range(2)]
            am = [act.do(A.activation, acc[t], hid[t], ACT.Identity, scale=col_at("conv_w1", i, f[t]),
                         bias=col_at("conv_b_2", i, f[t]), after=(m[t], ago(dve, 8 if s2 else 10)))
                  for t in range(2)]
            m = [dve.do(V.scalar_tensor_tensor, acc[t][:, 1:S], hid[t][:, 0:S - 1], col_at("conv_w0", i, f[t]),
                        acc[t][:, 1:S], ALU.mult, ALU.add, after=(am[t],)) for t in range(2)]
            m = [dve.do(V.scalar_tensor_tensor, acc[t][:, 0:S - 1], hid[t][:, 1:S], col_at("conv_w2", i, f[t]),
                        acc[t][:, 0:S - 1], ALU.mult, ALU.add, after=(m[t],)) for t in range(2)]
            if s2 == 0:
                g_m = [act.do(A.activation, acc[t], acc[t], ACT.Gelu_apprx_tanh, after=(m[t],)) for t in range(2)]
                continue
            m = [dve.do(V.tensor_tensor, acc[t], tmp[t][:, :], acc[t], ALU.mult, after=(m[t], g_m[t])) for t in range(2)]
            his = [tile_at(hid_hi, i, 2, 2 * r0 + t) for t in range(2)]
            am = [act.do(A.activation, his[t], acc[t], ACT.Copy, after=(m[t],)) for t in range(2)]
            for t in range(2):
                dve.do(V.tensor_tensor, tile_at(hid_lo, i, 2, 2 * r0 + t), acc[t], his[t].bitcast(F32), ALU.subtract,
                       after=(am[t],))

    rounds(FT // 2, conv_mlp, norm, act=8, dve=12)

    pe.wait(act.now(), dve.now())
    done = down(hid_hi, hid_lo, False)
    o3 = slot("mlp_out", 0, KT)
    o3_ready = []
    for n in range(KT):
        if n < 4:
            act.wait(done[n], done[-1])
            A.activation(o3[:, n, :], bank[n][:, :], ACT.Copy).then_inc(s_evac[n], 1)
            o3_ready.append(Mark(s_evac[n], uses[n]))
        else:
            m = dve.do(V.tensor_copy, o3[:, n, :], bank[n][:, :], after=(done[-1],))
            free[n] = (m,)
            o3_ready.append(m)
    x_ready = add_normed(o3, o3_ready, "g_post_ffn_2", (dve.now(),))

    out_tm = slot("out_tm", 8, 8)
    stored = nc.alloc_semaphore("out_stored")
    for half in range(2):
        banks = [4 * half + t for t in range(TT)]
        for b in banks:
            claim(b)
        for k in range(4):
            pe.wait(x_ready[4 * half + k])
            for t in range(TT):
                m = T.transpose(bank[banks[t]][:, k * P:(k + 1) * P], xT[:, 4 * half + k, t * P:(t + 1) * P], ident)
        m = pe.done(m)
        for t in range(TT):
            n = 4 * half + t
            if t % 2:
                e = act.do(A.activation, out_tm[:, n, :], bank[banks[t]][:, :], ACT.Copy, after=(m,))
            else:
                e = dve.do(V.tensor_copy, out_tm[:, n, :], bank[banks[t]][:, :], after=(m,))
            SP.wait_ge(e.sem, e.base)
            SP.dma_start(out[0, t * P:(t + 1) * P, half * 4 * P:(half + 1) * 4 * P], out_tm[:, n, :]).then_inc(stored, 16)
    SP.wait_ge(stored, 16 * 2 * TT)


_INS = ["x", "p", "positions", "g_mix", "w_in", "g_qa", "g_kva", "w_qb", "w_kvb", "g_qn", "g_kn", "lb_param",
        "g_hgo", "w_o", "g_ffn", "w_gate", "w_up", "w_down", "g_ple", "w_ple_gate", "w_ple_proj", "g_pre_mix_2",
        "w_in_2", "ret_decay_logit_2", "sgu_ln_g_2", "sgu_ln_b_2", "w_spatial_2", "b_spatial_2", "w_ret_o_2",
        "w_sgu_o_2", "w_out_2", "g_post_mix_2", "g_pre_ffn_2", "w_up_2", "conv_w_2", "conv_b_2", "w_down_2",
        "g_post_ffn_2"]


def kernel(**inputs):
    import concourse.bacc as bacc
    from concourse.bass_utils import run_bass_kernel_spmd

    nc = bacc.Bacc("TRN2", target_bir_lowering=False, num_devices=1)
    arrays = {n: np.ascontiguousarray(inputs[n]) for n in _INS}
    arrays.update(const_tables())
    args = {n: nc.dram_tensor(f"in_{n}", a.shape, mybir.dt.from_np(a.dtype), kind="ExternalInput").ap()
            for n, a in arrays.items()}
    out = nc.dram_tensor("out", (1, S, D), F32, kind="ExternalOutput").ap()
    program(nc, **args, out=out)
    r = run_bass_kernel_spmd(nc, [{f"in_{n}": a for n, a in arrays.items()}], core_ids=[0])
    return r.results[0]["out"]
```

```python
import numpy as np

import concourse.bass as bass
from concourse import mybir

F32, F32R, I32 = mybir.dt.float32, mybir.dt.float32r, mybir.dt.int32
ALU, ACT, AX = mybir.AluOpType, mybir.ActivationFunctionType, mybir.AxisListType

COMPUTE = (mybir.EngineType.PE, mybir.EngineType.Activation, mybir.EngineType.DVE)
SP_ONLY = (mybir.EngineType.SP,)

P = 128
S = 512
D = 1024
KT = D // P
TT = S // P
EPS = 1e-6
HEADS = 4
NOPE, ROPE, VH = 128, 64, 128
QK = NOPE + ROPE
LORA = 256
HG_CHUNK = 64
NCH = S // HG_CHUNK
F1 = 2816
FT = F1 // P
SLAB = 2048
CW = SLAB // KT
RDK, RDV = 128, 256
SGU_W, GRP = 1024, 4
F2T = 2 * F1 // P

ROWS = {}
_at = 0
for _n, _k in (("g_mix", 8), ("g_qa", 2), ("g_kva", 2), ("g_qn", 1), ("g_kn", 1), ("g_hgo", 4), ("lb_param", 16),
               ("g_ffn", 8), ("g_ple", 8), ("g_pre_mix_2", 8), ("g_post_mix_2", 8), ("g_pre_ffn_2", 8),
               ("g_post_ffn_2", 8), ("conv_b_2", F2T)):
    ROWS[_n] = _at
    _at += _k
assert _at <= P
ROWS["conv_w0"], ROWS["conv_w1"], ROWS["g_qn_rope"], ROWS["g_kn_rope"] = P, P + F2T, P + 2 * F2T, P + 2 * F2T + 1
ROWS["conv_w2"], ROWS["sgu_ln_g_2"], ROWS["sgu_ln_b_2"] = 2 * P, 2 * P + F2T, 2 * P + F2T + 8


def const_tables():
    i = np.arange(P)
    ident = np.eye(P)
    ones = np.ones((P, P))
    inv = (10000.0 ** (-np.arange(0, ROPE, 2) / ROPE))
    cols = np.zeros((P, 12))
    cols[:, 0] = EPS
    cols[:, 1] = np.pi / 2
    cols[:, 2] = inv[i % 32]
    cols[:, 3] = np.where(i % 64 < 32, -1.0, 1.0)
    cols[:, 4] = 1.0
    cols[:, 5] = RDK ** -0.5
    cols[:, 6] = 127 - i
    cols[:, 7] = i
    cols[:, 8] = i < 64
    cols[:, 9] = i >= 64
    small = np.concatenate([ident, ones, cols], 1)
    perm = np.zeros((P, P))
    perm[i ^ 32, i] = 1.0
    s, t = i[:, None], i[None, :]
    same = s // HG_CHUNK == t // HG_CHUNK
    maskf = same & (s <= t)
    maskb = same & (s >= t)
    reset = np.ones((P, S))
    reset[:, ::HG_CHUNK] = 0.0
    mix1 = np.concatenate([perm, maskf, maskb, reset], 1)
    m, n = i[:, None], i[None, :]
    after = np.maximum(n - m, 0)
    before = np.maximum(m - n, 0)
    xif = np.broadcast_to(n + 1, (P, P))
    xib = np.broadcast_to(P - n, (P, P))
    half = RDK // 2
    freq = (1.0 / (10000.0 ** (np.arange(half) / half))).astype(np.float32)
    ang = (np.arange(S, dtype=np.float32)[None, :] * freq[i % half][:, None]).astype(np.float32).astype(np.float64)
    cos, sin = np.cos(ang), np.sin(ang) * np.where(i < half, -1.0, 1.0)[:, None]
    mix2 = np.concatenate([after, before, xif, xib, cos, sin], 1)
    return {k: np.ascontiguousarray(v, dtype=np.float32)
            for k, v in (("const_small", small), ("const_mix1", mix1), ("const_mix2", mix2))}


class Mark:

    def __init__(self, sem, base, i=None, step=0):
        self.sem, self.base, self.i, self.step = sem, base, i, step

    def value(self):
        return self.base if self.i is None else self.i * self.step + self.base

    def before(self):
        return Mark(self.sem, self.base - self.step, self.i, self.step)

    def last(self, rounds):
        return Mark(self.sem, self.base + (rounds - 1) * self.step)


class Queue:

    def __init__(self, nc, engine, name):
        self.nc, self.e, self.sem, self.count, self.i, self.step = nc, engine, nc.alloc_semaphore(name), 0, None, 0
        self.seen = {}

    def wait(self, *marks):
        for m in marks:
            if m is None:
                continue
            key = (m.sem.name, m.i is None)
            if self.seen.get(key, -1) >= m.base:
                continue
            self.seen[key] = m.base
            self.e.wait_ge(m.sem, m.value())

    def done(self, ins):
        ins.then_inc(self.sem, 1)
        self.count += 1
        return Mark(self.sem, self.count, self.i, self.step)

    def do(self, fn, *args, after=(), **kw):
        self.wait(*after)
        return self.done(fn(*args, **kw))

    def now(self):
        return Mark(self.sem, self.count, self.i, self.step)


def program(nc, x, p, positions, g_mix, w_in, g_qa, g_kva, w_qb, w_kvb, g_qn, g_kn, lb_param, g_hgo, w_o,
            g_ffn, w_gate, w_up, w_down, g_ple, w_ple_gate, w_ple_proj, g_pre_mix_2, w_in_2,
            ret_decay_logit_2, sgu_ln_g_2, sgu_ln_b_2, w_spatial_2, b_spatial_2, w_ret_o_2, w_sgu_o_2,
            w_out_2, g_post_mix_2, g_pre_ffn_2, w_up_2, conv_w_2, conv_b_2, w_down_2, g_post_ffn_2,
            const_small, const_mix1, const_mix2, out):
    pe, act, dve = Queue(nc, nc.tensor, "pe_done"), Queue(nc, nc.scalar, "act_done"), Queue(nc, nc.vector, "dve_done")
    T, A, V, G, SP = nc.tensor, nc.scalar, nc.vector, nc.gpsimd, nc.sync
    queues = (pe, act, dve)
    w_in, w_qb, w_kvb, w_o, w_gate, w_up, w_down, w_ple_gate, w_ple_proj = (
        w[0] for w in (w_in, w_qb, w_kvb, w_o, w_gate, w_up, w_down, w_ple_gate, w_ple_proj))

    limit = []
    top = [(nc.sbuf_base + 63) // 64 * 64]

    def sb(name, shape, dt=F32, at=None):
        size = int(np.prod(shape[1:])) * 4
        if at is None:
            at = top[0]
            top[0] += (size + 31) // 32 * 32
            assert not limit or top[0] <= limit[0]
        return nc.alloc_sbuf_tensor_at(name, shape, dtype=dt, offset=at)

    xT = sb("residual", [P, KT, S])
    raw = [sb(f"slab_raw{j}", [P, SLAB]) for j in range(2)]
    w_hi = [sb(f"slab_hi{j}", [P, SLAB], F32R) for j in range(2)]
    w_lo = [sb(f"slab_lo{j}", [P, SLAB], F32R) for j in range(2)]
    h_base = top[0]
    h_hi = sb("h_hi", [P, KT, S], F32R)
    h_lo = sb("h_lo", [P, KT, S], F32R)
    cs = sb("const_small_sb", [P, 2 * P + 12])
    ident, ones, ccol = cs[:, 0:P], cs[:, P:2 * P], cs[:, 2 * P:]
    eps_col, halfpi_col, freq_col, sign_col = (ccol[:, k:k + 1] for k in range(4))
    cols = sb("param_cols", [P, 3 * P])
    dcol = sb("decay_cols", [P, 8 * 10])
    rcol = sb("rstd_cols", [P, 32])
    xcol = sb("x_rstd_cols", [P, TT])
    xrow = sb("x_rstd_rows", [P, S])
    NT = 8
    tmp = [sb(f"tmp{j}", [P, S]) for j in range(NT)]
    tmp_end = top[0]
    arena = top[0] + 2048
    limit.append(arena)
    BLK = S * 4
    assert arena + 44 * BLK <= nc.sbuf_usable_end, (arena, nc.sbuf_usable_end)

    def slot(name, first, n, dt=F32, shape=None):
        assert first + n <= 44
        return sb(name, shape or [P, n, S], dt, at=arena + first * BLK)

    def col(name, k=0):
        c = ROWS[name] + k
        return cols[:, c:c + 1]

    bank = [nc.alloc_psum_tensor(f"bank{b}", [P, S], F32) for b in range(8)]
    free = [()] * 8
    turn = [0]

    def take(banks=(4, 5, 6, 7)):
        b = banks[turn[0] % len(banks)]
        turn[0] += 1
        claim(b)
        return b

    def claim(b):
        pe.wait(*free[b])
        if b < 4 and uses[b]:
            pe.wait(Mark(s_evac[b], uses[b]))

    landed = [nc.alloc_semaphore(f"slab_landed{j}") for j in range(2)]
    s_hi = nc.alloc_semaphore("slab_hi_done")
    s_lo = nc.alloc_semaphore("slab_lo_done")
    s_tile = nc.alloc_semaphore("slab_products")
    s_evac = [nc.alloc_semaphore(f"bank_read{b}") for b in range(4)]
    landings, landing = [0, 0], {}
    stream = {"loaded": 0, "split": 0, "used": 0}
    uses = [0] * 4
    loop = {"i": None, "n": 1}

    def at_round(value, per_round):
        return value if loop["i"] is None else loop["i"] * per_round + value

    def load_slab(columns, *srcs, i=None, per_round=2):
        g = stream["loaded"]
        stream["loaded"] += 1
        rounds = 0 if i is None else i
        if g >= 2:
            SP.wait_ge(s_lo, rounds * per_round + g - 1)
        k = srcs[0].shape[1]
        dst = raw[g % 2][:, 0:k * columns].rearrange("p (k c) -> p k c", k=k)
        at = 0
        for src in srcs:
            n = int(np.prod(src.shape[2:]))
            SP.dma_start(dst[:, :, at:at + n] if len(srcs) > 1 else dst, src).then_inc(landed[g % 2], 16)
            landings[g % 2] += 16
            at += n
        landing[g] = landings[g % 2]

    def load_loop(rounds, *sources):
        first = stream["loaded"]
        with nc.Fori(0, rounds, engines=SP_ONLY) as i:
            for src in sources:
                load_slab(SLAB // src(i).shape[1], src(i), i=i, per_round=len(sources))
        assert len(sources) == 2
        for g in range(first, first + 2 * rounds):
            landing[g] = landing[first + (g - first) % 2] + 16 * ((g - first) // 2)
        for j in range(2):
            landings[j] += 16 * (rounds - 1)
        stream["loaded"] = first + 2 * rounds

    def split_slab(slabs_per_round=2):
        g = stream["split"]
        stream["split"] += 1
        A.wait_ge(landed[g % 2], at_round(landing[g], 8 * slabs_per_round))
        if g >= 2:
            A.wait_ge(s_tile, at_round(2 * (g - 1), 2 * slabs_per_round))
        A.activation(w_hi[g % 2][:, :], raw[g % 2][:, :], ACT.Copy).then_inc(s_hi, 1)
        V.wait_ge(s_hi, at_round(g + 1, slabs_per_round))
        V.tensor_tensor(w_lo[g % 2][:, :], raw[g % 2][:, :], w_hi[g % 2][:, :].bitcast(F32),
                        ALU.subtract).then_inc(s_lo, 1)

    def slab_parts(slabs_per_round=2):
        g = stream["used"]
        stream["used"] += 1
        T.wait_ge(s_lo, at_round(g + 1, slabs_per_round))
        return g, w_hi[g % 2], w_lo[g % 2]

    def three(psum, a_hi, a_lo, b_hi, b_lo, start, stop, skip=False):
        T.matmul(psum, a_hi, b_hi, start=start, stop=False, skip_group_check=skip)
        T.matmul(psum, a_hi, b_lo, start=False, stop=False, skip_group_check=skip)
        return T.matmul(psum, a_lo, b_hi, start=False, stop=stop, skip_group_check=skip)

    def use_bank(b):
        if loop["i"] is None:
            pe.wait(*free[b])
        if uses[b]:
            T.wait_ge(s_evac[b], at_round(uses[b], 1))
        uses[b] += 1

    class Product:

        def __init__(self, b, ready):
            self.b, self.ready, self.ps = b, ready, bank[b]

        def wait(self, *qs):
            for q in qs:
                q.e.wait_ge(s_tile, self.ready)

    def products_fm(src_hi=None, src_lo=None, per=2, ready=None):
        g, hi, lo = slab_parts(per)
        src_hi, src_lo = src_hi or h_hi, src_lo or h_lo
        hv, lv = (w[:, :].rearrange("p (k c) -> p k c", k=KT) for w in (hi, lo))
        banks = [2 * (g % 2) + t for t in range(2)]
        for b in banks:
            use_bank(b)

        def product(k, t):
            ins = three(bank[banks[t]][:, :], hv[:, k, t * P:(t + 1) * P], lv[:, k, t * P:(t + 1) * P],
                        src_hi[:, k, :], src_lo[:, k, :], k == 0, k == KT - 1)
            if k == KT - 1:
                ins.then_inc(s_tile, 1)

        if ready is None:
            for t in range(2):
                for k in range(KT):
                    product(k, t)
        else:
            for k in range(KT):
                pe.wait(ready[k])
                for t in range(2):
                    product(k, t)
        return [Product(banks[t], at_round(2 * g + t + 1, 2 * per)) for t in range(2)]

    def products_tm(per=2):
        g, hi, lo = slab_parts(per)
        hv, lv = (w[:, :].rearrange("p (k c) -> p k c", k=KT) for w in (hi, lo))
        tiles = []
        for t in range(2):
            b = 2 * (g % 2) + t
            use_bank(b)
            for u in range(2):
                tok = slice((2 * t + u) * P, (2 * t + u + 1) * P)
                for k in range(KT):
                    last = three(bank[b][:, u * CW:(u + 1) * CW], h_hi[:, k, tok], h_lo[:, k, tok],
                                 hv[:, k, :], lv[:, k, :], k == 0, k == KT - 1)
            last.then_inc(s_tile, 1)
            tiles.append(Product(b, at_round(2 * g + t + 1, 2 * per)))
        return tiles

    def read_last(prod, fn, *args, **kw):
        fn(*args, **kw).then_inc(s_evac[prod.b], 1)
        return Mark(s_evac[prod.b], uses[prod.b], loop["i"], 0 if loop["i"] is None else 1)

    class Loop:

        def __init__(self, n, slabs=2, bank_uses=1, **counts):
            self.n, self.slabs, self.bank_uses, self.counts = n, slabs, bank_uses, counts

        def __enter__(self):
            for b in range(4):
                pe.wait(*free[b])
            self.f = nc.Fori(0, self.n, engines=COMPUTE)
            i = self.f.__enter__()
            loop["i"] = i
            self.start = dict(stream)
            self.uses = list(uses)
            self.base = [q.count for q in queues]
            for q, k in zip(queues, ("pe", "act", "dve")):
                q.i, q.step = i, self.counts.get(k, 0)
                q.outer, q.seen = q.seen, {}
            return i

        def __exit__(self, *e):
            if e[0] is None:
                for k in ("split", "used"):
                    n = stream[k] - self.start[k]
                    assert n == self.slabs, (k, n)
                    stream[k] = self.start[k] + n * self.n
                for b in range(4):
                    assert uses[b] - self.uses[b] == self.bank_uses, (b, uses[b] - self.uses[b])
                    uses[b] = self.uses[b] + self.n * self.bank_uses
                said = {}
                for q, k, b0 in zip(queues, ("pe", "act", "dve"), self.base):
                    said[k] = q.count - b0
                wrong = {k: v for k, v in said.items() if v != self.counts.get(k, 0)}
                assert not wrong, said
                for q, b0 in zip(queues, self.base):
                    q.count = b0 + (q.count - b0) * self.n
                    q.i, q.step, q.seen = None, 0, q.outer
                loop["i"] = None
            return self.f.__exit__(*e)

    def dma(dst, src, sem, e=G):
        return e.dma_start(dst, src).then_inc(sem, 16)

    def weight_cols(w, c0, n=CW):
        return w[:, c0:c0 + n].rearrange("(k p) c -> p k c", p=P)

    def weight_cols_at(w, i, step, c0):
        return w[:, bass.ds(i * step + c0, CW)].rearrange("(k p) c -> p k c", p=P)

    def sum_rows(dst, sq, ready, first, last, clear, which=None):
        pe.wait(*ready)
        for t in range(TT):
            ins = T.matmul(dst[:, t:t + 1], sq[:, t * P:(t + 1) * P], which or ones[:, 0:1], start=clear and t == 0,
                           stop=last, skip_group_check=True)
        return pe.done(ins)

    def rstd_cols(dst, sums, n, ready):
        m = act.do(A.activation, dst, sums, ACT.Sqrt, bias=eps_col, scale=1.0 / n, after=ready)
        return dve.do(V.reciprocal, dst, dst, after=(m,)), m

    def spread(b, rcols, dtile, ready, busy=()):
        dtile = dtile[:, :]
        d = dtile.rearrange("p (t c) -> p t c", t=TT)
        m = dve.do(V.tensor_tensor, d, ident.unsqueeze(1).broadcast_to([P, TT, P]),
                   rcols.unsqueeze(2).broadcast_to([P, TT, P]), ALU.mult, after=(*ready, *busy))
        return pe.do(T.matmul, bank[b][:, :], ones, dtile, start=True, stop=True, after=(m,))

    def sum_tiles(marks, first=0):
        m = marks[0]
        for k in range(1, len(marks)):
            m = dve.do(V.tensor_tensor, tmp[first][:, :], tmp[first][:, :], tmp[first + k][:, :], ALU.add,
                       after=(m, marks[k]))
        return m

    class Norm:

        def __init__(self, gname, ready=None, busy=()):
            self.gname, self.parts, self.squares = gname, [], []
            self.busy = busy
            if ready is not None:
                for k in range(KT):
                    self.tile(k, ready[k])
                self.finish()

        def tile(self, k, ready):
            m = act.do(A.activation, h_hi[:, k, :], xT[:, k, :], ACT.Identity, scale=col(self.gname, k),
                       after=(*(self.busy if k == 0 else ()), ready))
            self.parts.append(dve.do(V.scalar_tensor_tensor, h_lo[:, k, :], xT[:, k, :], col(self.gname, k),
                                     h_hi[:, k, :].bitcast(F32), ALU.mult, ALU.subtract, after=(m,)))

        def finish(self):
            marks = [act.do(A.activation, tmp[k][:, :], xT[:, k, :], ACT.Square) for k in range(KT)]
            self.sum = sum_tiles(marks)

        def rows(self):
            b = take()
            m = sum_rows(bank[b][:, 0:TT], tmp[0][:, :], (self.sum,), True, True, True)
            r, m = rstd_cols(xcol[:, :], bank[b][:, 0:TT], D, (m,))
            free[b] = (m,)
            b = take()
            m = spread(b, xcol[:, :], tmp[1], (r,))
            m = dve.do(V.tensor_copy, xrow[:, :], bank[b][:, :], after=(m,))
            free[b] = (m,)
            dve.wait(m)
            act.wait(m)

    def first_products(norm):
        tiles = products_fm(ready=norm.parts)
        norm.rows()
        return tiles

    def scaled(prod, dst, q=None):
        prod.wait(dve)
        return read_last(prod, V.tensor_tensor, dst, prod.ps[:, :], xrow[:, :], ALU.mult)

    def scaled_tm(prod, dst, tok, fn):
        prod.wait(act)
        src = prod.ps[:, :].rearrange("p (u c) -> p u c", u=2)
        A.activation(dst[:, 0, :], src[:, 0, :], fn, scale=xcol[:, tok:tok + 1])
        return read_last(prod, A.activation, dst[:, 1, :], src[:, 1, :], fn, scale=xcol[:, tok + 1:tok + 2])

    def rounds(n, body, norm=None, **counts):
        body(0, 0, norm)
        with Loop(n - 1, **counts) as i:
            body(i, 1, None)

    def ago(q, k):
        return None if q.i is None else Mark(q.sem, q.count + k - q.step, q.i, q.step)

    def tile_at(t, i, step, off):
        return t[:, bass.ds(i * step + off, 1), :].rearrange("p a s -> p (a s)")

    def evac_marks():
        return [Mark(s_evac[b], uses[b]) for b in range(4)]

    def split_tile(t_ap, ready, hi_ap, lo_ap, busy=()):
        am = act.do(A.activation, hi_ap, t_ap, ACT.Copy, after=(*ready, *busy))
        return dve.do(V.tensor_tensor, lo_ap, t_ap, hi_ap.bitcast(F32), ALU.subtract, after=(am,))

    d_const, d_rows, d_rows_a, d_x = (
        nc.alloc_semaphore(n) for n in ("consts_landed", "rows_landed", "rows_landed_from_act", "x_landed"))
    c1 = slot("const_mix1_sb", 43, 1, shape=[P, 3 * P + P])
    perm, maskf, maskb = c1[:, 0:P], c1[:, P:2 * P], c1[:, 2 * P:3 * P]
    x_tm = slot("x_tm", 0, 8, shape=[P, TT, D])
    rows = slot("param_rows", 8, 1, shape=[P, 3, P])
    rows_zero = dve.do(V.memset, rows[:, :, :], 0.0)
    dma(cs[:, :], const_small, d_const, SP)
    for t in range(TT):
        dma(x_tm[:, t, :], x[0, t * P:(t + 1) * P, :], d_x, SP)
    load_slab(CW, weight_cols(w_in, 0))
    G.wait_ge(dve.sem, rows_zero.base)
    A.wait_ge(dve.sem, rows_zero.base)
    row_loads = [0, 0]

    def load_rows(dst, src):
        k = int(row_loads[0] > row_loads[1])
        dma(dst, src, (d_rows, d_rows_a)[k], (G, A)[k])
        row_loads[k] += 1

    for name, ap in (("g_mix", g_mix), ("g_qa", g_qa), ("g_kva", g_kva), ("g_qn", g_qn[:, 0:NOPE]),
                     ("g_kn", g_kn[:, 0:NOPE]), ("g_ffn", g_ffn), ("g_ple", g_ple)):
        src = ap.rearrange("a (k c) -> (a k) c", c=P)
        r = ROWS[name]
        load_rows(rows[r:r + src.shape[0], 0, :], src)
    for name, src in (("g_hgo", g_hgo.rearrange("a h d -> (a h) d")),
                      ("lb_param", lb_param.rearrange("a d (h c) -> (a d h) c", c=P)),
                      *((n, ap.rearrange("(k c) -> k c", c=P)) for n, ap in (
                          ("g_pre_mix_2", g_pre_mix_2), ("g_post_mix_2", g_post_mix_2), ("g_pre_ffn_2", g_pre_ffn_2),
                          ("g_post_ffn_2", g_post_ffn_2), ("conv_b_2", conv_b_2)))):
        r = ROWS[name]
        load_rows(rows[r:r + src.shape[0], 0, :], src)
    for k in range(3):
        src = conv_w_2[k, :].rearrange("(k c) -> k c", c=P)
        r, blk = ROWS[f"conv_w{k}"] % P, ROWS[f"conv_w{k}"] // P
        load_rows(rows[r:r + F2T, blk, :], src)
    for name, ap in (("sgu_ln_g_2", sgu_ln_g_2), ("sgu_ln_b_2", sgu_ln_b_2)):
        r = ROWS[name] - 2 * P
        load_rows(rows[r:r + 8, 2, :], ap.rearrange("(k c) -> k c", c=P))
    for name, ap in (("g_qn_rope", g_qn), ("g_kn_rope", g_kn)):
        r = ROWS[name] - P
        for half in range(2):
            load_rows(rows[r:r + 1, 1, half * ROPE:(half + 1) * ROPE], ap[:, NOPE:QK])
    def cols_of(w, c0=0, step=2 * CW):
        return lambda i: weight_cols_at(w, i, step, c0)

    def rows_of(w, s0, per_round):
        return lambda i: w[bass.ds(i * (per_round * 2 * P) + s0 * 2 * P, 2 * P), :].rearrange("(k p) c -> p k c", p=P)

    load_slab(CW, weight_cols(w_in, LORA))
    load_slab(2 * ROPE, *[weight_cols(w_in, 2 * LORA, ROPE)] * 2)
    z0 = 2 * LORA + ROPE
    load_loop(3, cols_of(w_in, z0), cols_of(w_in, z0 + CW))
    load_slab(CW, weight_cols(w_in, z0 + 6 * CW))
    qb_cols = w_qb.rearrange("(k p) (h c) -> p k h c", p=P, c=QK)
    load_slab(HEADS * QK, *[qb_cols[:, :, hd, 0:NOPE] for hd in range(HEADS)],
              *[qb_cols[:, :, hd, NOPE:QK] for hd in range(HEADS)])
    load_slab(CW, weight_cols(w_in, z0 + 7 * CW))
    load_slab(HEADS * 2 * P, w_kvb.rearrange("(k p) c -> p k c", p=P))
    for n in range(2):
        load_slab(CW, weight_cols(w_in, z0 + (8 + n) * CW))
    load_loop(2, cols_of(w_o), cols_of(w_o, CW))
    load_loop(FT // 2, cols_of(w_gate, 0, CW), cols_of(w_up, 0, CW))
    load_slab(D, w_down[0:2 * P, :].rearrange("(k p) c -> p k c", p=P))
    load_loop(FT // 4, rows_of(w_down, 1, 2), rows_of(w_down, 2, 2))
    load_slab(D, w_ple_proj.rearrange("(k p) c -> p k c", p=P))
    load_loop(2, cols_of(w_ple_gate), cols_of(w_ple_gate, CW))
    load_loop(6, cols_of(w_in_2), cols_of(w_in_2, CW))
    load_loop(2, cols_of(w_in_2, 4 * D), cols_of(w_in_2, 4 * D + CW))
    load_loop(4, cols_of(w_ret_o_2, 0, CW), cols_of(w_in_2, 5 * D, CW))
    load_loop(2, cols_of(w_in_2, 3 * D), cols_of(w_in_2, 3 * D + CW))
    load_loop(4, cols_of(w_sgu_o_2, 0, CW), cols_of(w_in_2, 6 * D, CW))
    load_loop(2, cols_of(w_out_2), cols_of(w_out_2, CW))
    load_loop(FT // 2, cols_of(w_up_2, 0, CW), cols_of(w_up_2, F1, CW))
    load_slab(D, w_down_2[0:2 * P, :].rearrange("(k p) c -> p k c", p=P))
    load_loop(FT // 4, rows_of(w_down_2, 1, 2), rows_of(w_down_2, 2, 2))
    T.wait_ge(d_const, 16)
    A.wait_ge(d_const, 16)
    V.wait_ge(d_const, 16)
    T.wait_ge(d_x, 16 * TT)

    x_ready = []
    for k in range(KT):
        b = take((4, 5, 6, 7))
        for t in range(TT):
            m = T.transpose(bank[b][:, t * P:(t + 1) * P], x_tm[:, t, k * P:(k + 1) * P], ident)
        m = pe.done(m)
        if k % 2:
            e = dve.do(V.tensor_copy, xT[:, k, :], bank[b][:, :], after=(m,))
        else:
            e = act.do(A.activation, xT[:, k, :], bank[b][:, :], ACT.Copy, after=(m,))
        free[b] = (e,)
        x_ready.append(e)
    T.wait_ge(d_rows, 16 * row_loads[0])
    T.wait_ge(d_rows_a, 16 * row_loads[1])
    b = take()
    for blk in range(3):
        m = T.transpose(bank[b][:, blk * P:(blk + 1) * P], rows[:, blk, :], ident)
    cols_ready = dve.do(V.tensor_copy, cols[:, :], bank[b][:, 0:3 * P], after=(pe.done(m),))
    free[b] = (cols_ready,)
    split_slab()

    norm = Norm("g_mix", x_ready, (cols_ready,))
    d_c1 = nc.alloc_semaphore("mix1_consts_landed")
    G.wait_ge(pe.sem, pe.count)
    dma(c1[:, 0:3 * P], const_mix1[:, 0:3 * P], d_c1)

    zt = slot("z", 0, 20)
    v_hg = zt[:, 12:16, :]
    c_raw = slot("c_raw", 20, 4)
    cq_hi, cq_lo, ckv_hi, ckv_lo = (slot(n, 32 + 2 * k, 2, F32R)
                                    for k, n in enumerate(("cq_hi", "cq_lo", "ckv_hi", "ckv_lo")))
    c_hi = [cq_hi[:, 0, :], cq_hi[:, 1, :], ckv_hi[:, 0, :], ckv_hi[:, 1, :]]
    c_lo = [cq_lo[:, 0, :], cq_lo[:, 1, :], ckv_lo[:, 0, :], ckv_lo[:, 1, :]]
    kr_raw = slot("kr_raw", 24, 1)
    c_ready = []
    for j in range(2):
        split_slab()
        tiles = products_fm() if j else first_products(norm)
        for t in range(2):
            c_ready.append(scaled(tiles[t], c_raw[:, 2 * j + t, :]))
    split_slab()
    g, hi, lo = slab_parts()
    hv, lv = (w[:, 0:KT * 2 * ROPE].rearrange("p (k c) -> p k c", k=KT) for w in (hi, lo))
    b = 2 * (g % 2)
    use_bank(b)
    use_bank(b + 1)
    for k in range(KT):
        last = three(bank[b][:, :], hv[:, k, :], lv[:, k, :], h_hi[:, k, :], h_lo[:, k, :], k == 0, k == KT - 1)
    last.then_inc(s_tile, 2)
    V.wait_ge(s_tile, 2 * g + 2)
    V.tensor_tensor(kr_raw[:, 0, :], bank[b][:, :], xrow[:, :], ALU.mult).then_inc(s_evac[b], 1)
    V.sem_inc(s_evac[b + 1], 1)

    b = take()
    m = [act.do(A.activation, tmp[k][:, :], c_raw[:, k, :], ACT.Square, after=(c_ready[k], dve.now())) for k in range(4)]
    for j in range(2):
        read = sum_rows(bank[b][:, TT * j:TT * (j + 1)], tmp[2 * j][:, :], (sum_tiles(m[2 * j:2 * j + 2], 2 * j),),
                        True, True, j == 0)
    r, m = rstd_cols(rcol[:, 0:2 * TT], bank[b][:, 0:2 * TT], LORA, (read,))
    free[b] = (m,)
    scaled_c = []
    c_banks = [take() for j in range(2)]
    c_rows = [spread(c_banks[j], rcol[:, TT * j:TT * (j + 1)], tmp[2 * j + 1], (r,)) for j in range(2)]
    for j, gname in enumerate(("g_qa", "g_kva")):
        b, rr = c_banks[j], c_rows[j]
        for k in range(2):
            kk = 2 * j + k
            hm = dve.do(V.scalar_tensor_tensor, tmp[4 + kk][:, :], c_raw[:, kk, :], col(gname, k), bank[b][:, :],
                        ALU.mult, ALU.mult, after=(rr,))
            scaled_c.append(hm)
        free[b] = (hm,)
    c_parts = [split_tile(tmp[4 + kk][:, :], (scaled_c[kk],), c_hi[kk], c_lo[kk]) for kk in range(4)]

    lbc = sb("lower_bounds", [P, 4, 8])
    L0, L1 = (cols[:, ROWS["lb_param"] + 8 * k:ROWS["lb_param"] + 8 * (k + 1)] for k in range(2))
    lower, one_minus, e0, e1 = (lbc[:, k, :] for k in range(4))
    m = dve.do(V.tensor_tensor, lower, L0, L1, ALU.max, after=(cols_ready,))
    a0 = dve.do(V.tensor_tensor, e0, L0, lower, ALU.subtract, after=(m,))
    a1 = dve.do(V.tensor_tensor, e1, L1, lower, ALU.subtract, after=(m,))
    m0 = act.do(A.activation, e0, e0, ACT.Exp, after=(a0,))
    m1 = act.do(A.activation, e1, e1, ACT.Exp, after=(a1,))
    m = dve.do(V.tensor_tensor, e1, e0, e1, ALU.add, after=(m0, m1))
    m = dve.do(V.reciprocal, e1, e1, after=(m,))
    m = dve.do(V.tensor_tensor, lower, e0, e1, ALU.mult, after=(m,))
    low_ready = dve.do(V.tensor_scalar, one_minus, lower, -1.0, 1.0, ALU.mult, ALU.add, after=(m,))
    with Loop(3) as i:
        for s2 in range(2):
            split_slab()
            tiles = products_fm()
            for t in range(2):
                scaled(tiles[t], tile_at(zt, i, 4, 2 * s2 + t))
    z_ready = evac_marks()
    tiles = products_tm()
    q_nope, q_rope = slot("q_nope", 25, 4), slot("q_rope", 29, 2)
    k_nope, k_rope = slot("k_nope", 20, 4), slot("k_rope", 40, 2)
    v_mla = slot("v_mla", 32, 4)
    cos1, sin1 = slot("rope_cos", 42, 1)[:, 0, :], slot("rope_sin", 31, 1)[:, 0, :]

    pos_i = sb("pos_i", [P, S], I32, at=arena + 31 * BLK)
    d_pos = nc.alloc_semaphore("positions_landed")
    dma(pos_i[:, :], positions[0].partition_broadcast(P), d_pos)
    V.wait_ge(d_pos, 16)
    C1, C2 = 6.28125, float(np.float32(2 * np.pi - 6.28125) // 2.0 ** -23 * 2.0 ** -23)
    C3 = float(2 * np.pi - C1 - C2)
    MAGIC = 1.5 * 2.0 ** 23
    PI = 3.1415925
    m = dve.do(V.tensor_copy, tmp[0][:, :], pos_i[:, :], after=(c_parts[-1],))
    m = dve.do(V.tensor_scalar, tmp[0][:, :], tmp[0][:, :], freq_col, None, ALU.mult, after=(m,))
    m = dve.do(V.tensor_scalar, tmp[1][:, :], tmp[0][:, :], float(1 / (2 * np.pi)), MAGIC, ALU.mult, ALU.add, after=(m,))
    m = dve.do(V.tensor_scalar, tmp[1][:, :], tmp[1][:, :], MAGIC, None, ALU.subtract, after=(m,))
    for c in (C1, C2, C3):
        m = dve.do(V.scalar_tensor_tensor, tmp[0][:, :], tmp[1][:, :], -c, tmp[0][:, :], ALU.mult, ALU.add, after=(m,))
    m = dve.do(V.tensor_scalar, tmp[0][:, :], tmp[0][:, :], -PI, PI, ALU.max, ALU.min, after=(m,))
    m1 = act.do(A.activation, tmp[1][:, :], tmp[0][:, :], ACT.Abs, after=(m,))
    m1 = act.do(A.activation, cos1, tmp[1][:, :], ACT.Sin, bias=halfpi_col, scale=-1.0, after=(m1,))
    m2 = act.do(A.activation, tmp[1][:, :], tmp[0][:, :], ACT.Sin, after=(m1,))
    tables = dve.do(V.tensor_scalar, sin1, tmp[1][:, :], sign_col, None, ALU.mult, after=(m1, m2))
    V.wait_ge(d_c1, 16)
    T.wait_ge(d_c1, 16)

    def rotate(t, ready, gcol, tb, g_done=False):
        if gcol is not None:
            ready = (dve.do(V.tensor_scalar, t, t, gcol, None, ALU.mult, after=ready),)
        b = take((4, 5, 6))
        m = pe.do(T.matmul, bank[b][:, :], perm, t, start=True, stop=True, after=ready)
        sw = dve.do(V.tensor_tensor, tmp[tb][:, :], bank[b][:, :], sin1, ALU.mult, after=(m, tables))
        free[b] = (sw,)
        m = dve.do(V.tensor_tensor, t, t, cos1, ALU.mult, after=(m, sw))
        return dve.do(V.tensor_tensor, t, t, tmp[tb][:, :], ALU.add, after=(m, sw))

    def hi_out(tiles, s2):
        for t in range(2):
            scaled_tm(tiles[t], v_hg[:, 2 * t:2 * t + 2, s2 * CW:(s2 + 1) * CW], 2 * t, ACT.Identity)

    for k in range(HEADS):
        hq_ready = act.do(A.activation, zt[:, k, :], zt[:, k, :], ACT.Silu, after=z_ready)
    split_slab()
    hi_out(tiles, 0)

    claim(7)
    sums = bank[7]
    sq_read, to_sum = {}, []

    def squares(src, ready, jobs):
        n = len(to_sum)
        m = act.do(A.activation, tmp[n % 4][:, :], src, ACT.Square, after=(*ready, sq_read.get(n - 4)))
        to_sum.append((n, m, jobs))
        return m

    def sum_squares(upto):
        for n, m, jobs in to_sum[len(sq_read):upto]:
            for hd, rws, first, last in jobs:
                sq_read[n] = sum_rows(sums[:, TT * hd:TT * (hd + 1)], tmp[n % 4][:, :], (m,), first, last,
                                      n == 0 and hd == jobs[0][0], rws)

    lower_half, upper_half, all_rows = ccol[:, 8:9], ccol[:, 9:10], None
    kr_sq = squares(kr_raw[:, 0, :], z_ready + [m2], [(HEADS + hd, lower_half, True, False) for hd in range(HEADS)])
    KR = rotate(kr_raw[:, 0, :], (kr_sq, cols_ready, *z_ready), col("g_kn_rope"), 4)
    split_slab()

    g, hi, lo = slab_parts()
    hv, lv = (w[:, 0:2 * HEADS * QK].rearrange("p (k c) -> p k c", k=2) for w in (hi, lo))
    pe.wait(c_parts[1])
    q_ready = []
    for t in range(6):
        b = take((4, 5, 6))
        for k in range(2):
            m = three(bank[b][:, :], hv[:, k, t * P:(t + 1) * P], lv[:, k, t * P:(t + 1) * P],
                      c_hi[k], c_lo[k], k == 0, k == 1)
        if t in (2, 5):
            m.then_inc(s_tile, 1)
            m = Mark(s_tile, 2 * g + 1 + (t == 5))
        else:
            m = pe.done(m)
        dst = q_nope[:, t, :] if t < HEADS else q_rope[:, t - HEADS, :]
        e = dve.do(V.tensor_copy, dst, bank[b][:, :], after=(m,))
        jobs = ([(t, all_rows, True, False)] if t < HEADS else
                [(2 * (t - HEADS), lower_half, False, True), (2 * (t - HEADS) + 1, upper_half, False, True)])
        squares(dst, (e,), jobs)
        sum_squares(t)
        free[b] = (e,)
        q_ready.append(e)

    tiles = products_tm()
    f_ready = []
    for k in range(8):
        f = zt[:, 4 + k, :]
        m = act.do(A.activation, f, f, ACT.Sigmoid)
        f_ready.append(dve.do(V.tensor_scalar, f, f, one_minus[:, k:k + 1], lower[:, k:k + 1], ALU.mult, ALU.add,
                              after=(m, low_ready)))
    split_slab()
    hi_out(tiles, 1)

    split_slab()
    g, hi, lo = slab_parts()
    hv, lv = (w[:, :].rearrange("p (k h c) -> p k h c", k=2, h=HEADS) for w in (hi, lo))
    pe.wait(c_parts[3])
    k_ready, v_ready = [], []
    for t in range(HEADS):
        b = take((4, 5, 6))
        for k in range(2):
            m = three(bank[b][:, :], hv[:, k, t, 0:P], lv[:, k, t, 0:P], c_hi[2 + k], c_lo[2 + k],
                      k == 0, k == 1)
        m = pe.done(m)
        e = dve.do(V.tensor_copy, k_nope[:, t, :], bank[b][:, :], after=(m,))
        squares(k_nope[:, t, :], (e,), [(HEADS + t, all_rows, False, True)])
        sum_squares(len(to_sum) - 1)
        free[b] = (e,)
        k_ready.append(e)
    for t in range(TT):
        b = take((4, 5, 6))
        tok = slice(t * P, (t + 1) * P)
        for k in range(2):
            m = three(bank[b][:, :].rearrange("p (h c) -> p h c", h=HEADS), ckv_hi[:, k, tok], ckv_lo[:, k, tok],
                      hv[:, k, :, P:2 * P], lv[:, k, :, P:2 * P], k == 0, k == 1)
        if t in (1, 3):
            m.then_inc(s_tile, 1)
            m = Mark(s_tile, 2 * g + 1 + (t == 3))
        else:
            m = pe.done(m)
        if t == 0:
            sum_squares(len(to_sum))
            r_all, rm = rstd_cols(rcol[:, :], sums[:, 0:32], QK, (sq_read[len(to_sum) - 1],))
            free[7] = (rm,)
        e = act.do(A.activation, v_mla[:, t, :], bank[b][:, :], ACT.Copy, after=(m, Mark(s_tile, 2 * g)))
        free[b] = (e,)
        v_ready.append(e)

    dt_free, head_ready, row_bank = {}, {}, {}
    order = [n for hd in range(HEADS) for n in (hd, HEADS + hd)]

    def head_rows(at):
        n = order[at]
        b = row_bank[n] = 4 + at % 4
        claim(b)
        dt = tmp[at % 4]
        dt_free[n] = spread(b, rcol[:, TT * n:TT * (n + 1)], dt, (r_all, *((dt_free[order[at - 4]],) if at >= 4 else ())))

    def head_scaled(n):
        hd, is_k = n % HEADS, n >= HEADS
        half = slice(ROPE * (hd % 2), ROPE * (hd % 2 + 1))
        b, rr = row_bank[n], dt_free[n]
        t = (k_nope if is_k else q_nope)[:, hd, :]
        m1 = dve.do(V.scalar_tensor_tensor, t, t, col("g_kn" if is_k else "g_qn"), bank[b][:, :], ALU.mult, ALU.mult,
                    after=(rr, (k_ready if is_k else q_ready)[hd]))
        if is_k:
            m2 = dve.do(V.tensor_tensor, k_rope[half, hd // 2, :], kr_raw[half, 0, :], bank[b][half, :], ALU.mult,
                        after=(rr, KR))
        else:
            t = q_rope[half, hd // 2, :]
            m2 = dve.do(V.scalar_tensor_tensor, t, t, col("g_qn_rope")[half, :], bank[b][half, :], ALU.mult, ALU.mult,
                        after=(rr, q_ready[HEADS + hd // 2]))
        free[b] = (m1, m2)
        head_ready[n] = (m1, m2)

    def pair_rotated(pair):
        m = rotate(q_rope[:, pair, :], (head_ready[2 * pair][1], head_ready[2 * pair + 1][1]), None, 4 + pair)
        for hd in (2 * pair, 2 * pair + 1):
            head_ready[hd] = (head_ready[hd][0], m)

    tiles = products_fm()
    for at in range(4):
        head_rows(at)
    split_slab()
    hg_ready = [scaled(tiles[t], zt[:, 16 + t, :]) for t in range(2)]
    tiles = products_fm()
    h_read = Mark(s_tile, 2 * stream["used"])
    for at in range(4):
        head_scaled(order[at])
    pair_rotated(0)
    for at in range(4, 8):
        head_rows(at)
    split_slab()
    hg_ready += [scaled(tiles[t], zt[:, 18 + t, :]) for t in range(2)]
    z_all = evac_marks()
    for at in range(4, 8):
        head_scaled(order[at])
    pair_rotated(1)
    log_f = [sb(f"log_f{k}", [P, S], at=h_base + (4 + k + 4 * (k // 4)) * BLK)[:, :] for k in range(8)]
    lf_ready = [act.do(A.activation, log_f[k], zt[:, 4 + k, :], ACT.Ln, after=(f_ready[k], h_read)) for k in range(8)]
    for k in range(HEADS):
        hg_done = act.do(A.activation, zt[:, 16 + k, :], zt[:, 16 + k, :], ACT.Silu, after=hg_ready)
    reset = slot("reset", 24, 1)[:, 0, :]
    d_reset = nc.alloc_semaphore("reset_landed")
    G.wait_ge(dve.sem, dve.count)
    dma(reset, const_mix1[:, 3 * P:3 * P + S], d_reset)

    p_t = slot("weights_t", 36, 4)
    scale = QK ** -0.5
    mcol = sb("softmax_cols", [P, 2, 4])
    pv_done, exp_read, copied = None, {}, {}
    units = [(hd, j) for hd in range(HEADS) for j in range(TT)]
    score, attn_ready = {}, []

    def scores(u):
        hd, j = units[u]
        b = 4 + u % 2
        claim(b)
        qt = slice(j * P, (j + 1) * P)
        half = slice(ROPE * (hd % 2), ROPE * (hd % 2 + 1))
        pe.wait(*head_ready[hd], *head_ready[HEADS + hd])
        T.matmul(bank[b][:, :], q_nope[:, hd, qt], k_nope[:, hd, :], start=True, stop=False)
        m = pe.done(T.matmul(bank[b][:, :], q_rope[half, hd // 2, qt], k_rope[half, hd // 2, :], start=False, stop=True))
        c = mcol[:, u % 2, :]
        m = dve.do(V.reduce_max, c[:, 0:1], bank[b][:, :], AX.X, after=(m,))
        m = dve.do(V.tensor_scalar, c[:, 1:2], c[:, 0:1], -scale, None, ALU.mult, after=(m,))
        w = tmp[u % 2]
        m = act.do(A.activation, w[:, :], bank[b][:, :], ACT.Exp, bias=c[:, 1:2], scale=scale, accum_out=c[:, 2:3],
                   after=(m, exp_read.get(u - 2)))
        free[b] = (m,)
        score[u] = m

    def weights(u):
        c, w = mcol[:, u % 2, :], tmp[u % 2]
        m = dve.do(V.reciprocal, c[:, 3:4], c[:, 2:3], after=(score[u],))
        score[u] = dve.do(V.tensor_scalar, w[:, :], w[:, :], c[:, 3:4], None, ALU.mult, after=(m,))

    def transposed(u):
        hd, j = units[u]
        b = 0
        claim(b)
        pe.wait(score[u])
        for kb in range(TT):
            m = T.transpose(bank[b][:, kb * P:(kb + 1) * P], tmp[u % 2][:, kb * P:(kb + 1) * P], ident)
        m = exp_read[u] = pe.done(m)
        copied[u] = act.do(A.activation, p_t[:, :, j * P:(j + 1) * P],
                           bank[b][:, :].rearrange("p (k q) -> p k q", k=TT), ACT.Copy,
                           after=(m, pv_done, *((v_ready[-1],) if u == 0 else ())))
        free[b] = (copied[u],)

    def values(hd):
        b = 1
        claim(b)
        pe.wait(copied[TT * hd + TT - 1])
        for kb in range(TT):
            m = T.matmul(bank[b][:, :], v_mla[:, kb, hd * VH:(hd + 1) * VH], p_t[:, kb, :], start=kb == 0,
                         stop=kb == TT - 1)
        m = pe.done(m)
        am = act.do(A.activation, h_hi[:, hd, :], bank[b][:, :], ACT.Copy, after=(m,))
        e = dve.do(V.tensor_tensor, h_lo[:, hd, :], bank[b][:, :], h_hi[:, hd, :].bitcast(F32), ALU.subtract, after=(am,))
        free[b] = (e,)
        attn_ready.append(e)
        return m

    qi, ki, kd = (tmp[k][:, :] for k in range(2, 5))
    a_t = slot("gla_scores", 31, 1)[:, 0, :]
    kd_t = slot("gla_keys_t", 42, 1)[:, 0, :].rearrange("p (j d) -> p j d", j=TT)
    st = sb("gla_states", [P, NCH, P], at=tmp_end - 2 * BLK)
    decs = sb("gla_decay", [P, 2, NCH])
    scores_read = [head_ready[n][1] for n in range(8)] + [dt_free[n] for n in range(8)]
    out_read, kv_read, dec_read, o_ready = None, None, {}, {}
    V.wait_ge(d_reset, 16)
    stage = {}

    def chunks(t):
        return t.rearrange("p (c t) -> p c t", t=HG_CHUNK)

    def prepare(n):
        hd, back = n // 2, n % 2
        k = 4 * back + hd
        f, bb = zt[:, 4 + k, :], log_f[k]
        mid, last = (HG_CHUNK // 2, 0) if back else (HG_CHUNK // 2 - 1, HG_CHUNK - 1)
        if back:
            m = dve.do(V.tensor_tensor_scan, bb[:, ::-1], reset, bb[:, ::-1], 0.0, ALU.mult, ALU.add,
                       after=(lf_ready[k],))
        else:
            m = dve.do(V.tensor_tensor_scan, bb, reset, bb, 0.0, ALU.mult, ALU.add, after=(lf_ready[k],))
        at = lambda x: chunks(bb)[:, :, x:x + 1].broadcast_to([P, NCH, HG_CHUNK])
        m_mid = dve.do(V.tensor_tensor, chunks(ki), chunks(bb), at(mid), ALU.subtract, after=(m, *scores_read))
        m_last = dve.do(V.tensor_tensor, chunks(kd), at(last), chunks(bb), ALU.subtract, after=(m,))
        m_k = act.do(A.activation, f, f, ACT.Identity, scale=-1.0, bias=ccol[:, 4:5])
        e1 = act.do(A.activation, qi, ki, ACT.Exp, after=(m_mid, *scores_read))
        e2 = act.do(A.activation, ki, ki, ACT.Exp, scale=-1.0, after=(e1,))
        e3 = act.do(A.activation, kd, kd, ACT.Exp, after=(m_last,))
        e5 = act.do(A.activation, decs[:, n % 2, :], chunks(bb)[:, :, last:last + 1].rearrange("p c t -> p (c t)"),
                    ACT.Exp, after=(dec_read.get(n - 2),))
        e4 = act.do(A.activation, bb, bb, ACT.Exp, after=(e5,))
        stage[n] = (e1, e2, e3, e4, e5, m_k)

    def decayed(n):
        hd, back = n // 2, n % 2
        q, k, qb = zt[:, hd, :], zt[:, 4 + 4 * back + hd, :], log_f[4 * back + hd]
        e1, e2, e3, e4, e5, m_k = stage[n]
        m1 = dve.do(V.tensor_tensor, qi, qi, q, ALU.mult, after=(e1, hq_ready))
        m3 = dve.do(V.tensor_tensor, kd, kd, k, ALU.mult, after=(e3, m_k))
        m2 = dve.do(V.tensor_tensor, k, ki, k, ALU.mult, after=(e2, m3))
        m4 = dve.do(V.tensor_tensor, qb, qb, q, ALU.mult, after=(e4,))
        stage[n] = (m2, m3, m4, e5)

    def intra(n):
        m2, m3, m4, e5 = stage[n]
        k = zt[:, 4 + 4 * (n % 2) + n // 2, :]
        claim(6)
        pe.wait(m2)
        for j in range(TT):
            sl = slice(j * P, (j + 1) * P)
            m = T.matmul(bank[6][:, sl], k[:, sl], qi[:, sl], start=j == 0, stop=True, skip_group_check=True)
        m = pe.done(m)
        mask = maskb if n % 2 else maskf
        e = dve.do(V.tensor_tensor, a_t.rearrange("p (j t) -> p j t", j=TT),
                   bank[6][:, :].rearrange("p (j t) -> p j t", j=TT), mask.unsqueeze(1).broadcast_to([P, TT, P]),
                   ALU.mult, after=(m, out_read))
        free[6] = (e,)
        claim(2)
        pe.wait(m3)
        for j in range(TT):
            m = T.transpose(bank[2][:, j * P:(j + 1) * P], kd[:, j * P:(j + 1) * P], ident)
        m = pe.done(m)
        scores_read[:] = [m]
        e2 = act.do(A.activation, kd_t, bank[2][:, :].rearrange("p (j d) -> p j d", j=TT), ACT.Copy,
                    after=(m, kv_read))
        free[2] = (e2,)
        stage[n] = (e, e2, m4, e5)

    def state(n):
        hd, back = n // 2, n % 2
        e, e2, m4, e5 = stage[n]
        cols_v = slice(hd * P, (hd + 1) * P)
        bs = (2, 3)
        for half in range(2):
            claim(bs[half])
        pe.wait(e2)
        order = list(range(NCH - 1, 0, -1)) if back else list(range(NCH - 1))
        for half in range(2):
            rws = slice(HG_CHUNK * half, HG_CHUNK * (half + 1))
            first = True
            for c in (c for c in range(NCH) if c % 2 == half and c in order):
                j = c // 2
                m = T.matmul(bank[bs[half]][:, j * P:(j + 1) * P], kd_t[rws, j, :], v_hg[rws, j, cols_v],
                             start=first, stop=True, skip_group_check=True)
                first = False
        m = kv_done = pe.done(m)
        prev = None
        for c in order:
            to = c - 1 if back else c + 1
            kv = bank[bs[c % 2]][:, (c // 2) * P:(c // 2 + 1) * P]
            if prev is None:
                prev = dve.do(V.tensor_copy, st[:, to, :], kv, after=(m, out_read))
            else:
                prev = dve.do(V.scalar_tensor_tensor, st[:, to, :], st[:, c, :], decs[:, n % 2, c:c + 1], kv,
                              ALU.mult, ALU.add, after=(prev, e5))
        free[2] = free[3] = (prev,)
        dec_read[n] = prev
        stage[n] = (e, m4, prev)
        return kv_done

    def outputs(n):
        hd, back = n // 2, n % 2
        e, m4, s_m = stage[n]
        if not back:
            claim(7)
        pe.wait(e, m4, s_m)
        qb = log_f[4 * back + hd]
        cols_v = slice(hd * P, (hd + 1) * P)
        for j in range(TT):
            sl = slice(j * P, (j + 1) * P)
            m = T.matmul(bank[7][:, sl], v_hg[:, j, cols_v], a_t[:, sl], start=not back and j == 0, stop=False,
                         skip_group_check=True)
        for c in range(NCH):
            if c == (NCH - 1 if back else 0):
                continue
            sl = slice(c * HG_CHUNK, (c + 1) * HG_CHUNK)
            m = T.matmul(bank[7][:, sl], st[:, c, :], qb[:, sl], start=False, stop=True, skip_group_check=True)
        read = pe.done(m)
        if back:
            o = zt[:, 4 + hd, :]
            o_ready[hd] = dve.do(V.tensor_copy, o, bank[7][:, :], after=(read,))
            free[7] = (o_ready[hd],)
        return read

    norm_stage, mix_ready = {}, {}

    def head_squares(hd):
        norm_stage[hd] = act.do(A.activation, zt[:, 8 + hd, :], zt[:, 4 + hd, :], ACT.Square, after=(o_ready[hd],))

    def head_sums(hd):
        claim(3)
        m = sum_rows(bank[3][:, 0:TT], zt[:, 8 + hd, :], (norm_stage[hd],), True, True, True)
        r, m = rstd_cols(rcol[:, TT * hd:TT * (hd + 1)], bank[3][:, 0:TT], P, (m,))
        free[3] = (m,)
        norm_stage[hd] = r

    def head_output(hd):
        claim(3)
        r = spread(3, rcol[:, TT * hd:TT * (hd + 1)], zt[:, 8 + hd, :], (norm_stage[hd],))
        o = zt[:, 4 + hd, :]
        m = dve.do(V.scalar_tensor_tensor, o, o, col("g_hgo", hd), bank[3][:, :], ALU.mult, ALU.mult, after=(r,))
        free[3] = (m,)
        m = dve.do(V.tensor_tensor, o, o, zt[:, 16 + hd, :], ALU.mult, after=(m, hg_done))
        mix_ready[HEADS + hd] = split_tile(o, (m,), h_hi[:, HEADS + hd, :], h_lo[:, HEADS + hd, :], lf_read)

    pe.wait(*z_all)
    lf_read = []
    scores(0)
    prepare(0)
    decayed(0)
    for n in range(2 * HEADS):
        prev_head = n // 2 - 1 if n >= 2 and n % 2 == 0 else None
        intra(n)
        if n < 2 * HEADS - 1:
            prepare(n + 1)
        weights(2 * n)
        if prev_head is not None:
            head_squares(prev_head)
        if n:
            transposed(2 * n - 1)
        kv_read = state(n)
        scores(2 * n + 1)
        if n < 2 * HEADS - 1:
            decayed(n + 1)
        weights(2 * n + 1)
        if prev_head is not None:
            head_sums(prev_head)
        if n and n % 2 == 0:
            pv_done = values(n // 2 - 1)
        transposed(2 * n)
        if n < 2 * HEADS - 1:
            scores(2 * n + 2)
        out_read = outputs(n)
        if prev_head is not None:
            head_output(prev_head)
    head_squares(HEADS - 1)
    head_sums(HEADS - 1)
    transposed(2 * n + 1)
    values(HEADS - 1)
    head_output(HEADS - 1)
    mix_ready = attn_ready + [mix_ready[HEADS + hd] for hd in range(HEADS)]

    x_marks = []
    with Loop(2) as i:
        for s2 in range(2):
            split_slab()
            tiles = products_fm(ready=mix_ready if s2 == 0 else None)
            for t in range(2):
                tiles[t].wait(dve)
                xt = tile_at(xT, i, 4, 2 * s2 + t)
                x_marks.append(read_last(tiles[t], V.tensor_tensor, xt, xt, tiles[t].ps[:, :], ALU.add))
    x_marks = [Mark(m.sem, m.base + r * m.step) for r in range(2) for m in x_marks]

    norm = Norm("g_ffn", x_marks, (Mark(s_tile, 2 * stream["used"]), dve.now()))
    hid_hi, hid_lo = slot("hid_hi", 0, FT, F32R), slot("hid_lo", FT, FT, F32R)

    def swiglu(i, r0, norm):
        for s2 in range(2):
            split_slab()
            tiles = first_products(norm) if norm and s2 == 0 else products_fm()
            for t in range(2):
                if s2 == 0:
                    dve.wait(ago(dve, 4))
                    m = scaled(tiles[t], tmp[t][:, :])
                    gate_m = act.do(A.activation, tmp[t][:, :], tmp[t][:, :], ACT.Silu, after=(m,))
                    continue
                h_t = tmp[2 + t][:, :]
                tiles[t].wait(dve)
                dve.wait(gate_m)
                m = read_last(tiles[t], V.tensor_tensor, h_t, tmp[t][:, :], tiles[t].ps[:, :], ALU.mult)
                m = dve.do(V.tensor_tensor, h_t, h_t, xrow[:, :], ALU.mult, after=(m,))
                am = act.do(A.activation, tile_at(hid_hi, i, 2, 2 * r0 + t), h_t, ACT.Copy, after=(m,))
                hh = tile_at(hid_hi, i, 2, 2 * r0 + t).bitcast(F32)
                dve.do(V.tensor_tensor, tile_at(hid_lo, i, 2, 2 * r0 + t), h_t, hh, ALU.subtract, after=(am,))

    rounds(FT // 2, swiglu, norm, act=4, dve=4)

    def down(hid_hi, hid_lo, more, last_round):
        whole = dve.now()
        pe.wait(Mark(dve.sem, dve.count - last_round))
        for b in range(4):
            use_bank(b)
            claim(4 + b)

        def products(first_tile, start, stop, per=2):
            g, hi, lo = slab_parts(per)
            hv, lv = (w[:, :].rearrange("p (k c) -> p k c", k=2) for w in (hi, lo))
            for n in range(KT):
                for k in range(2):
                    last = three(bank[n][:, :], hv[:, k, n * P:(n + 1) * P], lv[:, k, n * P:(n + 1) * P],
                                 first_tile(hid_hi, k), first_tile(hid_lo, k), start and k == 0, stop and k == 1, True)
                if n % 4 == 3:
                    last.then_inc(s_tile, 1)
            return g

        split_slab()
        products(lambda t, k: t[:, k, :], True, False)
        rounds = FT // 4 - 1
        with Loop(rounds, bank_uses=0) as i:
            for s2 in range(2):
                split_slab()
                products(lambda t, k: tile_at(t, i, 4, 2 + 2 * s2 + k), False, False)
        for s2 in range(2):
            if more or s2 == 0:
                split_slab()
            if s2 == 1:
                pe.wait(whole)
            g = products(lambda t, k: t[:, FT - 4 + 2 * s2 + k, :], False, s2 == 1)
        return [Mark(s_tile, 2 * g + 1 + n // 4) for n in range(KT)]

    p_tm = sb("p_tm", [P, TT, 2 * P], at=tmp_end - 2 * BLK)
    d_p = nc.alloc_semaphore("p_landed")
    G.wait_ge(dve.sem, dve.count)
    dma(p_tm[:, :, :], p[0, 0].rearrange("(t q) c -> q t c", q=P), d_p)
    done = down(hid_hi, hid_lo, True, 4)
    x_ready = []
    for n in range(KT):
        if n < 4:
            V.wait_ge(done[n].sem, done[n].base)
            V.tensor_tensor(xT[:, n, :], xT[:, n, :], bank[n][:, :], ALU.add).then_inc(s_evac[n], 1)
            x_ready.append(Mark(s_evac[n], uses[n]))
        else:
            m = dve.do(V.tensor_tensor, xT[:, n, :], xT[:, n, :], bank[n][:, :], ALU.add, after=(done[n],))
            free[n] = (m,)
            x_ready.append(m)

    p_hi, p_lo = slot("p_hi", 2, 2, F32R), slot("p_lo", 4, 2, F32R)
    proj = slot("ple_proj", 8, KT)
    T.wait_ge(d_p, 16)
    p_parts = []
    for k in range(2):
        b = take()
        for t in range(TT):
            m = T.transpose(bank[b][:, t * P:(t + 1) * P], p_tm[:, t, k * P:(k + 1) * P], ident)
        m = pe.done(m)
        am = act.do(A.activation, p_hi[:, k, :], bank[b][:, :], ACT.Copy, after=(m,))
        e = dve.do(V.tensor_tensor, p_lo[:, k, :], bank[b][:, :], p_hi[:, k, :].bitcast(F32), ALU.subtract, after=(am,))
        free[b] = (e,)
        p_parts.append(e)
    split_slab()
    g, hi, lo = slab_parts()
    hv, lv = (w[:, :].rearrange("p (k c) -> p k c", k=2) for w in (hi, lo))
    pe.wait(*p_parts)
    proj_ready = []
    for n in range(KT):
        b = take((4, 5, 6, 7))
        for k in range(2):
            m = three(bank[b][:, :], hv[:, k, n * P:(n + 1) * P], lv[:, k, n * P:(n + 1) * P], p_hi[:, k, :],
                      p_lo[:, k, :], k == 0, k == 1)
        if n % 4 == 3:
            m.then_inc(s_tile, 1)
            m = Mark(s_tile, 2 * g + 1 + n // 4)
        else:
            m = pe.done(m)
        e = act.do(A.activation, proj[:, n, :], bank[b][:, :], ACT.Copy, after=(m,))
        free[b] = (e,)
        proj_ready.append(e)
    norm = Norm("g_ple", x_ready, (dve.now(),))
    dve.wait(proj_ready[-1])

    def gated_embedding(i, r0, norm):
        for s2 in range(2):
            split_slab()
            tiles = first_products(norm) if norm and s2 == 0 else products_fm()
            for t in range(2):
                n = 2 * s2 + t
                gt = tmp[n][:, :]
                dve.wait(ago(dve, 2))
                m = scaled(tiles[t], gt)
                m = act.do(A.activation, gt, gt, ACT.Sigmoid, after=(m,))
                m = dve.do(V.tensor_tensor, gt, gt, tile_at(proj, i, 4, 4 * r0 + n), ALU.mult, after=(m,))
                xt = tile_at(xT, i, 4, 4 * r0 + n)
                x_marks.append(dve.do(V.tensor_tensor, xt, xt, gt, ALU.add, after=(m,)))

    x_marks = []
    rounds(2, gated_embedding, norm, act=4, dve=8)

    qk, v_ret, gate = slot("ret_qk", 0, 8), slot("ret_v", 8, 8, shape=[P, TT, SGU_W]), slot("ret_gate", 16, 8)
    c2 = slot("const_mix2_sb", 24, 3)
    after_t, before_t, xif_t, xib_t = (c2[:, 0, k * P:(k + 1) * P] for k in range(4))
    cos2, sin2 = c2[:, 1, :], c2[:, 2, :]
    y_hi, y_lo = slot("y_hi", 28, 8, F32R), slot("y_lo", 36, 8, F32R)
    d_c2 = nc.alloc_semaphore("mix2_consts_landed")
    d_logit = nc.alloc_semaphore("decay_logits_landed")
    G.wait_ge(s_tile, done[-1].base)
    dma(c2[:, :, :], const_mix2.rearrange("p (k s) -> p k s", k=3), d_c2)
    logit, lg, e8, z8, zz8, q8, dec, zeta, neg8 = (dcol[:, 8 * k:8 * (k + 1)] for k in range(9))
    dma(logit, ret_decay_logit_2.rearrange("d h -> (d h)").partition_broadcast(P), d_logit)
    x_marks = [Mark(m.sem, m.base) for m in x_marks]
    norm = Norm("g_pre_mix_2", x_marks, (Mark(s_tile, 2 * stream["used"]), dve.now()))

    V.wait_ge(d_c2, 16)

    def rotated(i, r0, norm):
        for s2 in range(2):
            split_slab()
            tiles = first_products(norm) if norm and s2 == 0 else products_fm()
            if norm and s2 == 0:
                dve.do(V.tensor_tensor, cos2, cos2, xrow[:, :], ALU.mult)
                dve.wait(dve.do(V.tensor_tensor, sin2, sin2, xrow[:, :], ALU.mult))
            for t in range(2):
                n = 2 * s2 + t
                sw, dst, ps = tmp[n], tile_at(qk, i, 4, 4 * r0 + n), tiles[t].ps
                tiles[t].wait(act)
                act.do(A.activation, sw[0:64, :], ps[64:128, :], ACT.Copy, after=(ago(dve, 2),))
                am = act.do(A.activation, sw[64:128, :], ps[0:64, :], ACT.Copy)
                dve.wait(am)
                m1 = read_last(tiles[t], V.tensor_tensor, dst, ps[:, :], cos2, ALU.mult)
                m2 = dve.do(V.tensor_tensor, sw[:, :], sw[:, :], sin2, ALU.mult)
                dve.do(V.tensor_tensor, dst, dst, sw[:, :], ALU.add, after=(m1, m2))

    rounds(2, rotated, norm, act=8, dve=8)
    qk_ready = dve.now()

    V.wait_ge(d_logit, 16)
    A.wait_ge(d_logit, 16)
    m = act.do(A.activation, e8, logit, ACT.Abs)
    m = act.do(A.activation, e8, e8, ACT.Exp, scale=-1.0, after=(m,))
    m = dve.do(V.tensor_scalar, z8, e8, 2.0, None, ALU.add, after=(m,))
    m = dve.do(V.reciprocal, z8, z8, after=(m,))
    m = dve.do(V.tensor_tensor, z8, z8, e8, ALU.mult, after=(m,))
    m = dve.do(V.tensor_tensor, zz8, z8, z8, ALU.mult, after=(m,))
    m = dve.do(V.tensor_scalar, q8, zz8, 1 / 17, None, ALU.mult, after=(m,))
    for n in range(15, 1, -2):
        m = dve.do(V.scalar_tensor_tensor, q8, q8, 1 / n, zz8, ALU.add, ALU.mult, after=(m,))
    m = dve.do(V.scalar_tensor_tensor, q8, q8, 1.0, z8, ALU.add, ALU.mult, after=(m,))
    m0 = dve.do(V.tensor_scalar, neg8, logit, 0.0, None, ALU.min)
    lg_ready = dve.do(V.scalar_tensor_tensor, lg, q8, -2.0, neg8, ALU.mult, ALU.add, after=(m, m0))

    dmat, xi_f, xi_b = slot("ret_dmat", 27, 1), slot("ret_xi_f", 25, 1), slot("ret_xi_b", 26, 1)
    K_SCALE = RDK ** -0.5
    for hd in range(HEADS):
        hc = slice(hd * P, (hd + 1) * P)
        m = dve.do(V.tensor_scalar, dmat[:, 0, hc], after_t, lg[:, hd:hd + 1], None, ALU.mult, after=(lg_ready,))
        m = dve.do(V.scalar_tensor_tensor, dmat[:, 0, hc], before_t, lg[:, 4 + hd:5 + hd], dmat[:, 0, hc], ALU.mult,
                   ALU.add, after=(m,))
        act.do(A.activation, xi_f[:, 0, hc], xif_t, ACT.Exp, scale=lg[:, hd:hd + 1], after=(lg_ready, qk_ready))
        me = act.do(A.activation, xi_b[:, 0, hc], xib_t, ACT.Exp, scale=lg[:, 4 + hd:5 + hd])
    mz0 = dve.do(V.tensor_scalar, zeta[:, 0:4], lg[:, 0:4], ccol[:, 6:7], None, ALU.mult)
    mz1 = dve.do(V.tensor_scalar, zeta[:, 4:8], lg[:, 4:8], ccol[:, 7:8], None, ALU.mult)
    act.do(A.activation, dmat[:, 0, :], dmat[:, 0, :], ACT.Exp, after=(m,))
    act.do(A.activation, zeta, zeta, ACT.Exp, after=(mz0, mz1))
    me = act.do(A.activation, dec, lg, ACT.Exp, scale=float(P))
    for t in (dmat, xi_f, xi_b):
        tables = dve.do(V.tensor_scalar, t[:, 0, :], t[:, 0, :], K_SCALE, None, ALU.mult, after=(me,))

    w_sp = slot("w_spatial_raw", 24, 1)[:, 0, :].rearrange("p (g q) -> p g q", g=GRP)
    d_sp = nc.alloc_semaphore("spatial_landed")
    G.wait_ge(tables.sem, tables.base)
    dma(w_sp, w_spatial_2.rearrange("g p q -> p g q"), d_sp)

    with Loop(2) as i:
        for s2 in range(2):
            split_slab()
            tiles = products_tm()
            for t in range(2):
                dst = v_ret[:, 2 * t:2 * t + 2, bass.ds(i * (2 * CW) + s2 * CW, CW)]
                scaled_tm(tiles[t], dst, 2 * t, ACT.Identity)
    v_ready = evac_marks()
    gate_ready = {}

    def gate_slab(j):
        split_slab()
        tiles = products_fm()
        for t in range(2):
            dst = gate[:, 2 * j + t, :]
            gate_ready[j] = act.do(A.activation, dst, dst, ACT.Silu, after=(scaled(tiles[t], dst),))

    RC = TT
    r_f, r_b = (slot(n, at, 2, shape=[P, TT, RDV]) for n, at in (("ret_state_f", 34), ("ret_state_b", 42)))
    ln_stats, ln_mv, ln_rs = sb("ln_stats", [P, 8, 6]), sb("ln_mean_var", [P, 8, 2]), sb("ln_rstd", [P, 8])
    kf, kb = tmp[0][:, :], tmp[1][:, :]
    keys_t, kv_read, out_done, pair_t, s_t, st_ready, ln_ready, o_read, y_parts = {}, None, {}, {}, {}, {}, {}, {}, []

    def per_chunk(t):
        return t.rearrange("p (j c) -> p j c", j=RC)

    def table(t, hd):
        return t[:, 0, hd * P:(hd + 1) * P].unsqueeze(1).broadcast_to([P, RC, P])

    def ret_prepare(hd):
        q, k = qk[:, hd, :], qk[:, HEADS + hd, :]
        chunk = [slice(j * P, (j + 1) * P) for j in range(RC)]
        claim(0)
        pe.wait(qk_ready)
        for j in range(RC):
            T.matmul(bank[0][:, chunk[j]], k[:, chunk[j]], q[:, chunk[j]], start=j == 0, stop=True,
                     skip_group_check=True)
        claim(1)
        for j in range(RC):
            m = T.transpose(bank[1][:, chunk[j]], k[:, chunk[j]], ident)
        m = pe.done(m)
        m1 = act.do(A.activation, kf, bank[1][:, :], ACT.Identity, scale=zeta[:, hd:hd + 1], after=(m, kv_read))
        m2 = act.do(A.activation, kb, bank[1][:, :], ACT.Identity, scale=zeta[:, 4 + hd:5 + hd])
        free[1] = (m2,)
        sm = dve.do(V.tensor_tensor, per_chunk(k), per_chunk(bank[0][:, :]), table(dmat, hd), ALU.mult,
                    after=(m, tables))
        free[0] = (sm,)
        xf = tmp[2 + hd % 2][:, :]
        m = dve.do(V.tensor_tensor, per_chunk(xf), per_chunk(q), table(xi_f, hd), ALU.mult, after=(out_done.get(hd - 2),))
        xm = dve.do(V.tensor_tensor, per_chunk(q), per_chunk(q), table(xi_b, hd), ALU.mult, after=(m,))
        s_t[hd] = (sm, xm)
        keys_t[hd] = (m1, m2)

    def ret_pairs(hd):
        chunk = [slice(j * P, (j + 1) * P) for j in range(RC)]
        for b in (2, 3, 4):
            claim(b)
        pe.wait(*keys_t[hd], *v_ready)
        vc = slice(hd * RDV, (hd + 1) * RDV)
        for n, (src, j) in enumerate(((kf, 0), (kf, 1), (kf, 2), (kb, 3), (kb, 2), (kb, 1))):
            m = T.matmul(bank[2 + n // 2][:, (n % 2) * RDV:(n % 2 + 1) * RDV], src[:, chunk[j]], v_ret[:, j, vc],
                         start=n % 2 == 0, stop=True, skip_group_check=True)
        pair_t[hd] = pe.done(m)
        return pair_t[hd]

    def ret_states(hd):
        for d, r in ((0, r_f), (1, r_b)):
            for j in range(RC - 1):
                n = 3 * d + j
                kv = bank[2 + n // 2][:, (n % 2) * RDV:(n % 2 + 1) * RDV]
                if j == 0:
                    m = dve.do(V.tensor_copy, r[:, 0, :], kv, after=(pair_t[hd], out_done.get(hd - 1)))
                else:
                    m = dve.do(V.scalar_tensor_tensor, r[:, j, :], r[:, j - 1, :], dec[:, 4 * d + hd:4 * d + hd + 1],
                               kv, ALU.mult, ALU.add, after=(m,))
        st_ready[hd] = m
        free[2] = free[3] = free[4] = (m,)

    def ret_outputs(hd):
        claim(5)
        claim(6)
        pe.wait(*s_t[hd], st_ready[hd])
        vc = slice(hd * RDV, (hd + 1) * RDV)
        for j in range(RC):
            c = slice(j * P, (j + 1) * P)
            terms = [(qk[:, HEADS + hd, c], v_ret[:, j, vc])]
            if j > 0:
                terms.append((tmp[2 + hd % 2][:, c], r_f[:, j - 1, :]))
            if j < RC - 1:
                terms.append((qk[:, hd, c], r_b[:, RC - 2 - j, :]))
            o = bank[5 + j // 2][:, (j % 2) * RDV:(j % 2 + 1) * RDV]
            for n, (a, b) in enumerate(terms):
                m = T.matmul(o, a, b, start=n == 0, stop=n == len(terms) - 1)
        out_done[hd] = pe.done(m)

    def ret_layernorm(hd):
        base = 4 * (hd % 2)
        for j in range(RC):
            o = bank[5 + j // 2][:, (j % 2) * RDV:(j % 2 + 1) * RDV]
            m = dve.do(V.bn_stats, ln_stats[:, base + j, :], o, after=(out_done[hd],))
            mm = dve.do(V.bn_aggr, ln_mv[:, base + j, :], ln_stats[:, base + j, :], after=(m,))
        rs = ln_rs[:, base:base + 4]
        m = act.do(A.activation, rs, ln_mv[:, base:base + 4, 1:2].rearrange("p j a -> p (j a)"), ACT.Sqrt, bias=eps_col,
                   scale=1.0, after=(mm,))
        m = dve.do(V.reciprocal, rs, rs, after=(m,))
        for j in range(RC):
            o = bank[5 + j // 2][:, (j % 2) * RDV:(j % 2 + 1) * RDV]
            dst = tmp[4 + 2 * (hd % 2) + j // 2][:, (j % 2) * RDV:(j % 2 + 1) * RDV]
            mm = dve.do(V.tensor_scalar, dst, o, ln_mv[:, base + j, 0:1], rs[:, j:j + 1], ALU.subtract, ALU.mult,
                        after=(m, o_read.get(hd - 2)))
        free[5] = free[6] = (mm,)
        ln_ready[hd] = mm

    def ret_gated(hd):
        pe.wait(ln_ready[hd])
        for e in range(2):
            claim(7)
            for j in range(RC):
                src = tmp[4 + 2 * (hd % 2) + j // 2][:, (j % 2) * RDV + e * P:(j % 2) * RDV + (e + 1) * P]
                m = T.transpose(bank[7][:, j * P:(j + 1) * P], src, ident)
            m = o_read[hd] = pe.done(m)
            n = 2 * hd + e
            m = dve.do(V.tensor_tensor, gate[:, n, :], gate[:, n, :], bank[7][:, :], ALU.mult, after=(m, gate_ready[hd]))
            free[7] = (m,)
            y_parts.append(split_tile(gate[:, n, :], (m,), y_hi[:, n, :], y_lo[:, n, :]))

    SLABS = (1, 2, 3, 5)
    for step in range(HEADS + 2):
        if step < HEADS:
            ret_prepare(step)
        if 1 <= step <= HEADS:
            ret_outputs(step - 1)
        if step < HEADS:
            kv_read = ret_pairs(step)
            ret_states(step)
        if 1 <= step <= HEADS:
            ret_layernorm(step - 1)
        if step in SLABS:
            gate_slab(SLABS.index(step))
        if step >= 2:
            ret_gated(step - 2)

    bs_b = slot("b_spatial_rows", 26, 1)
    d_bs = nc.alloc_semaphore("b_spatial_landed")
    G.wait_ge(dve.sem, dve.count)
    dma(bs_b[:, 0, :], b_spatial_2.rearrange("g p -> (g p)").partition_broadcast(P), d_bs)
    sv_stats = sb("sv_stats", [P, TT, 4, 6])
    with Loop(2, dve=8) as i:
        for s2 in range(2):
            split_slab()
            tiles = products_tm()
            for t in range(2):
                dst = v_ret[:, 2 * t:2 * t + 2, bass.ds(i * (2 * CW) + s2 * CW, CW)]
                m = scaled_tm(tiles[t], dst, 2 * t, ACT.Gelu_apprx_tanh)
                for u in range(2):
                    st6 = sv_stats[:, 2 * t + u, bass.ds(i * 2 + s2, 1), :].rearrange("p a s -> p (a s)")
                    m = dve.do(V.bn_stats, st6, dst[:, u, :], after=(m,))
    for t in range(TT):
        m = dve.do(V.bn_aggr, ln_mv[:, t, :], sv_stats[:, t, :, :], after=(dve.now(),))
    m = act.do(A.activation, ln_rs[:, 0:TT], ln_mv[:, 0:TT, 1:2].rearrange("p j a -> p (j a)"), ACT.Sqrt, bias=eps_col,
               scale=1.0, after=(m,))
    m = dve.do(V.reciprocal, ln_rs[:, 0:TT], ln_rs[:, 0:TT], after=(m,))
    for t in range(TT):
        xhat_ready = dve.do(V.tensor_scalar, v_ret[:, t, :], v_ret[:, t, :], ln_mv[:, t, 0:1], ln_rs[:, t:t + 1],
                            ALU.subtract, ALU.mult, after=(m,))

    merged = slot("merged", 0, 8)

    def gated_branch(add, y_ready):
        ops = 2 if add else 1
        act.wait(dve.now())
        with Loop(4, act=2, dve=2 * ops) as i:
            split_slab()
            tiles = products_fm(y_hi, y_lo, ready=y_ready)
            for t in range(2):
                tiles[t].wait(act)
                act.wait(ago(dve, ops * (t + 1)))
                read_last(tiles[t], A.activation, tmp[2 + t][:, :], tiles[t].ps[:, :], ACT.Copy)
            copied = [Mark(s_evac[x.b], uses[x.b], i, 1) for x in tiles]
            split_slab()
            tiles = products_fm()
            for t in range(2):
                dve.wait(ago(dve, ops))
                m = scaled(tiles[t], tmp[4 + t][:, :])
                am = act.do(A.activation, tmp[4 + t][:, :], tmp[4 + t][:, :], ACT.Sigmoid, after=(m,))
                dst = tile_at(merged, i, 2, t)
                if add:
                    m = dve.do(V.tensor_tensor, tmp[4 + t][:, :], tmp[4 + t][:, :], tmp[2 + t][:, :], ALU.mult,
                               after=(copied[t], am))
                    dve.do(V.tensor_tensor, dst, dst, tmp[4 + t][:, :], ALU.add, after=(m,))
                else:
                    dve.do(V.tensor_tensor, dst, tmp[4 + t][:, :], tmp[2 + t][:, :], ALU.mult, after=(copied[t], am))

    gated_branch(False, y_parts)

    w_t, w_rows, mixed = slot("w_spatial_t", 25, 1)[:, 0, :], slot("w_spatial_rowsums", 27, 1)[:, 0, :], slot("mixed", 16, 8)
    T.wait_ge(d_sp, 16)
    V.wait_ge(d_bs, 16)
    b = take()
    for g in range(GRP):
        m = T.transpose(bank[b][:, g * P:(g + 1) * P], w_sp[:, g, :], ident)
    wt_ready = dve.do(V.tensor_copy, w_t, bank[b][:, :], after=(pe.done(m),))
    free[b] = (wt_ready,)
    b = take()
    m = pe.do(T.matmul, bank[b][:, :], ones, w_t, start=True, stop=True, after=(wt_ready,))
    rows_ready = dve.do(V.tensor_copy, w_rows, bank[b][:, :], after=(m,))
    free[b] = (rows_ready,)
    pe.wait(xhat_ready)
    mix_read = {}
    for c in range(KT):
        b = take()
        grp = slice(P * (c // 2), P * (c // 2 + 1))
        for j in range(RC):
            m = T.matmul(bank[b][:, j * P:(j + 1) * P], v_ret[:, j, c * P:(c + 1) * P], w_t[:, grp],
                         start=j == 0, stop=True, skip_group_check=True)
        m = pe.done(m)
        off = tmp[c % 2][:, 0:P]
        m1 = dve.do(V.scalar_tensor_tensor, off, w_rows[:, grp], col("sgu_ln_b_2", c), bs_b[:, 0, grp], ALU.mult, ALU.add,
                    after=(rows_ready, mix_read.get(c - 2)))
        mix_read[c] = dve.do(V.scalar_tensor_tensor, per_chunk(mixed[:, c, :]), per_chunk(bank[b][:, :]),
                             col("sgu_ln_g_2", c), off.unsqueeze(1).broadcast_to([P, RC, P]), ALU.mult, ALU.add,
                             after=(m, m1))
        free[b] = (mix_read[c],)

    act.wait(dve.now())
    y_parts = []
    with Loop(2, act=8, dve=8) as i:
        for s2 in range(2):
            split_slab()
            tiles = products_fm()
            for t in range(2):
                n = 2 * s2 + t
                w = tmp[n][:, :]
                dve.wait(ago(dve, 2))
                am = act.do(A.activation, w, w, ACT.Gelu_apprx_tanh, after=(scaled(tiles[t], w),))
                m = dve.do(V.tensor_tensor, w, w, tile_at(mixed, i, 4, n), ALU.mult, after=(am,))
                am = act.do(A.activation, tile_at(y_hi, i, 4, n), w, ACT.Copy, after=(m,))
                y_parts.append(dve.do(V.tensor_tensor, tile_at(y_lo, i, 4, n), w, tile_at(y_hi, i, 4, n).bitcast(F32),
                                      ALU.subtract, after=(am,)))
    y_parts = [Mark(m.sem, m.base + r * m.step) for r in range(2) for m in y_parts]
    gated_branch(True, y_parts)

    ready = dve.now()
    merged_parts = [split_tile(merged[:, k, :], (ready,), h_hi[:, k, :], h_lo[:, k, :]) for k in range(KT)]
    o2 = slot("mixed_out", 8, 8)
    o_marks = []
    with Loop(2) as i:
        for s2 in range(2):
            split_slab()
            tiles = products_fm(ready=merged_parts if s2 == 0 else None)
            for t in range(2):
                dst = tile_at(o2, i, 4, 2 * s2 + t)
                tiles[t].wait((act, dve)[t])
                if t == 0:
                    m = read_last(tiles[t], A.activation, dst, tiles[t].ps[:, :], ACT.Copy)
                else:
                    m = read_last(tiles[t], V.tensor_copy, dst, tiles[t].ps[:, :])
                o_marks.append(m)
    o_marks = [Mark(m.sem, m.base + r * m.step) for r in range(2) for m in o_marks]

    def add_normed(src, ready, gname, busy, norm=None, banks=(4, 5, 6, 7)):
        act.wait(*busy)
        marks = [act.do(A.activation, tmp[k][:, :], src[k], ACT.Square, after=(ready[k],)) for k in range(KT)]
        b = take(banks)
        m = sum_rows(bank[b][:, 0:TT], tmp[0][:, :], (sum_tiles(marks),), True, True, True)
        r, m = rstd_cols(rcol[:, 0:TT], bank[b][:, 0:TT], D, (m,))
        free[b] = (m,)
        b = take(banks)
        r = spread(b, rcol[:, 0:TT], tmp[1], (r,))
        rows = bank[b]
        if norm is None:
            r = dve.do(V.tensor_copy, xrow[:, :], rows[:, :], after=(r,))
            rows = xrow
        made = []

        def scale_add(k):
            t = tmp[2 + k % 3]
            m = dve.do(V.scalar_tensor_tensor, t[:, :], src[k], col(gname, k), rows[:, :], ALU.mult, ALU.mult,
                       after=(r, made[k - 3] if k > 2 else None))
            free[b] = (m,)
            made.append(dve.do(V.tensor_tensor, xT[:, k, :], xT[:, k, :], t[:, :], ALU.add, after=(m,)))

        for k in range(KT + 1):
            if k < KT:
                scale_add(k)
            if norm and k:
                norm.tile(k - 1, made[k - 1])
        return made

    norm = Norm("g_pre_ffn_2", busy=(Mark(s_tile, 2 * stream["used"]),))
    x_ready = add_normed([o2[:, k, :] for k in range(KT)], o_marks, "g_post_mix_2", (dve.now(),), norm)

    act.wait(x_ready[-1])
    norm.finish()
    hid_hi, hid_lo = slot("hid2_hi", 0, FT, F32R), slot("hid2_lo", FT, FT, F32R)

    def col_at(name, i, off):
        return cols[:, bass.ds(i * 2 + ROWS[name] + off, 1)]

    def conv_mlp(i, r0, norm):
        for s2 in range(2):
            split_slab()
            tiles = first_products(norm) if norm and s2 == 0 else products_fm()
            acc = [tmp[2 * s2 + t][:, :] for t in range(2)]
            hid = [tmp[4 + t][:, :] for t in range(2)]
            f = [FT * s2 + t + 2 * r0 for t in range(2)]
            m = [scaled(tiles[t], hid[t]) for t in range(2)]
            am = [act.do(A.activation, acc[t], hid[t], ACT.Identity, scale=col_at("conv_w1", i, f[t]),
                         bias=col_at("conv_b_2", i, f[t]), after=(m[t], ago(dve, 8 if s2 else 10)))
                  for t in range(2)]
            m = [dve.do(V.scalar_tensor_tensor, acc[t][:, 1:S], hid[t][:, 0:S - 1], col_at("conv_w0", i, f[t]),
                        acc[t][:, 1:S], ALU.mult, ALU.add, after=(am[t],)) for t in range(2)]
            m = [dve.do(V.scalar_tensor_tensor, acc[t][:, 0:S - 1], hid[t][:, 1:S], col_at("conv_w2", i, f[t]),
                        acc[t][:, 0:S - 1], ALU.mult, ALU.add, after=(m[t],)) for t in range(2)]
            if s2 == 0:
                g_m = [act.do(A.activation, acc[t], acc[t], ACT.Gelu_apprx_tanh, after=(m[t],)) for t in range(2)]
                continue
            m = [dve.do(V.tensor_tensor, acc[t], tmp[t][:, :], acc[t], ALU.mult, after=(m[t], g_m[t])) for t in range(2)]
            his = [tile_at(hid_hi, i, 2, 2 * r0 + t) for t in range(2)]
            am = [act.do(A.activation, his[t], acc[t], ACT.Copy, after=(m[t],)) for t in range(2)]
            for t in range(2):
                dve.do(V.tensor_tensor, tile_at(hid_lo, i, 2, 2 * r0 + t), acc[t], his[t].bitcast(F32), ALU.subtract,
                       after=(am[t],))

    rounds(FT // 2, conv_mlp, norm, act=8, dve=12)

    done = down(hid_hi, hid_lo, False, 12)
    o3 = slot("mlp_out", 0, 2)
    o3_ready = {}
    for n in (6, 7):
        o3_ready[n] = dve.do(V.tensor_copy, o3[:, n - 6, :], bank[n][:, :], after=(done[n],))
        free[n] = (o3_ready[n],)
    x_ready = add_normed([bank[n][:, :] for n in range(6)] + [o3[:, n, :] for n in range(2)],
                         [done[n] if n < 6 else o3_ready[n] for n in range(KT)], "g_post_ffn_2", (), None, (6, 7))
    for b in range(4):
        free[b] = (x_ready[b],)
        uses[b] = 0
    for b in (4, 5):
        free[b] = (x_ready[b],)

    out_tm = slot("out_tm", 8, 8)
    stored = nc.alloc_semaphore("out_stored")
    for half in range(2):
        banks = [4 * half + t for t in range(TT)]
        for b in banks:
            claim(b)
        for k in range(4):
            pe.wait(x_ready[4 * half + k])
            for t in range(TT):
                m = T.transpose(bank[banks[t]][:, k * P:(k + 1) * P], xT[:, 4 * half + k, t * P:(t + 1) * P], ident)
        m = pe.done(m)
        for t in range(TT):
            n = 4 * half + t
            if t % 2:
                e = act.do(A.activation, out_tm[:, n, :], bank[banks[t]][:, :], ACT.Copy, after=(m,))
            else:
                e = dve.do(V.tensor_copy, out_tm[:, n, :], bank[banks[t]][:, :], after=(m,))
            SP.wait_ge(e.sem, e.base)
            SP.dma_start(out[0, t * P:(t + 1) * P, half * 4 * P:(half + 1) * 4 * P], out_tm[:, n, :]).then_inc(stored, 16)
    SP.wait_ge(stored, 16 * 2 * TT)


_INS = ["x", "p", "positions", "g_mix", "w_in", "g_qa", "g_kva", "w_qb", "w_kvb", "g_qn", "g_kn", "lb_param",
        "g_hgo", "w_o", "g_ffn", "w_gate", "w_up", "w_down", "g_ple", "w_ple_gate", "w_ple_proj", "g_pre_mix_2",
        "w_in_2", "ret_decay_logit_2", "sgu_ln_g_2", "sgu_ln_b_2", "w_spatial_2", "b_spatial_2", "w_ret_o_2",
        "w_sgu_o_2", "w_out_2", "g_post_mix_2", "g_pre_ffn_2", "w_up_2", "conv_w_2", "conv_b_2", "w_down_2",
        "g_post_ffn_2"]


def kernel(**inputs):
    import concourse.bacc as bacc
    from concourse.bass_utils import run_bass_kernel_spmd

    nc = bacc.Bacc("TRN2", target_bir_lowering=False, num_devices=1)
    arrays = {n: np.ascontiguousarray(inputs[n]) for n in _INS}
    arrays.update(const_tables())
    args = {n: nc.dram_tensor(f"in_{n}", a.shape, mybir.dt.from_np(a.dtype), kind="ExternalInput").ap()
            for n, a in arrays.items()}
    out = nc.dram_tensor("out", (1, S, D), F32, kind="ExternalOutput").ap()
    program(nc, **args, out=out)
    r = run_bass_kernel_spmd(nc, [{f"in_{n}": a for n, a in arrays.items()}], core_ids=[0])
    return r.results[0]["out"]
```
